# Optimizing a Trainium2 kernel written in Bass

```python
import jax, jax.numpy as jnp
from jax import lax
import numpy as np

D_MODEL = 1024
BATCH = 1
SEQ = 512
DEPTH = 1
DEC_BATCH = 8
DEC_SEQ = 16
PAST_LEN = 256

CHUNK = 64
N_MEM = 256
N_XHEADS = 4
XHEAD_DIM = D_MODEL // N_XHEADS
D_CONV = 512
CONV_WIDTH = 31
CONV_BUF = CONV_WIDTH - 1
D_RWKV = 1024
RWKV_HEAD = 64
RWKV_HEADS = D_RWKV // RWKV_HEAD
D_DECAY_LORA = 64
D_AAA_LORA = 64
D_GATE_LORA = 128
N_BRANCH = 2
D_FF = -(-8 * D_MODEL // (3 * 256)) * 256
EPS_RMS = 1e-6
EPS_LN = 1e-5
EPS_GN = RWKV_HEAD * 1e-5
D_SHIFT = 3 * D_RWKV + D_DECAY_LORA + D_AAA_LORA + D_GATE_LORA
OFF_RWKV = 2 * D_CONV
OFF_GATE = OFF_RWKV + D_SHIFT
D_IN = OFF_GATE + N_BRANCH * D_MODEL

kernel_name = "gated_conformer_rwkv7_stream_step"

def _rms(x, g):
    xf = x.astype(jnp.float32)
    y = xf * lax.rsqrt(jnp.mean(xf * xf, -1, keepdims=True) + EPS_RMS) * g.astype(jnp.float32)
    return y.astype(x.dtype)

def _layernorm(x, g, b):
    xf = x.astype(jnp.float32)
    mu = jnp.mean(xf, -1, keepdims=True)
    var = jnp.mean(jnp.square(xf - mu), -1, keepdims=True)
    return ((xf - mu) * lax.rsqrt(var + EPS_LN) * g.astype(jnp.float32) + b.astype(jnp.float32)).astype(x.dtype)

def _wkv7(r, w, k, v, kk, a, s0):
    def step(S, inp):
        r_t, w_t, k_t, v_t, kk_t, a_t = inp
        sa = jnp.einsum('bhvk,bhk->bhv', S, -kk_t)
        S = (S * w_t[:, :, None, :] + sa[..., None] * (kk_t * a_t)[:, :, None, :]
             + v_t[..., None] * k_t[:, :, None, :])
        return S, jnp.einsum('bhvk,bhk->bhv', S, r_t)
    xs = tuple(jnp.moveaxis(t, 1, 0) for t in (r, w, k, v, kk, a))
    s_fin, ys = lax.scan(step, s0, xs)
    return jnp.moveaxis(ys, 0, 1), s_fin

def _mixer(xn, conv_buf, shift_buf, wkv_state, p):
    f32 = jnp.float32
    B, T, _ = xn.shape
    proj = xn @ p["w_in"]
    conv_in = proj[..., :OFF_RWKV]
    pr = proj[..., OFF_RWKV:OFF_GATE]
    gates = jax.nn.sigmoid(proj[..., OFF_GATE:])

    u = conv_in[..., :D_CONV] * jax.nn.sigmoid(conv_in[..., D_CONV:])
    u_pad = jnp.concatenate([conv_buf.astype(u.dtype), u], 1)
    c = lax.conv_general_dilated(u_pad, p["w_dw"][:, None, :], (1,), 'VALID',
                                 dimension_numbers=('NWC', 'WIO', 'NWC'),
                                 feature_group_count=D_CONV) + p["b_dw"]
    c = _layernorm(c, p["ln_conv_g"], p["ln_conv_b"])
    conv_out = jax.nn.silu(c) @ p["w_o_conv"]
    new_conv = u_pad[:, -CONV_BUF:]

    pr_prev = jnp.concatenate([shift_buf.astype(pr.dtype), pr[:, :-1]], 1)
    pm = pr + (pr_prev - pr) * p["mu_shift"]
    new_shift = pr[:, -1:]
    o1 = D_RWKV; o2 = 2 * D_RWKV; o3 = 3 * D_RWKV
    o4 = o3 + D_DECAY_LORA; o5 = o4 + D_AAA_LORA
    r, k, v, wd, ad, gd = jnp.split(pm, [o1, o2, o3, o4, o5], -1)
    w_log = -jax.nn.softplus(-(p["w0"] + jnp.tanh(wd) @ p["w_up"]).astype(f32)) - 0.5
    decay = jnp.exp(-jnp.exp(w_log))
    a = jax.nn.sigmoid((p["a0"] + ad @ p["a_up"]).astype(f32))
    g = jax.nn.sigmoid(gd) @ p["g_up"]
    hs = (B, T, RWKV_HEADS, RWKV_HEAD)
    kf = k.astype(f32)
    kk = (kf * p["k_k"].astype(f32)).reshape(hs)
    kk = kk / jnp.maximum(jnp.sqrt(jnp.sum(kk * kk, -1, keepdims=True)), 1e-12)
    kf = kf * (1.0 + (a - 1.0) * p["k_a"].astype(f32))
    rh = r.astype(f32).reshape(hs)
    kh = kf.reshape(hs)
    vh = v.astype(f32).reshape(hs)
    y, new_wkv = _wkv7(rh, decay.reshape(hs), kh, vh, kk, a.reshape(hs), wkv_state.astype(f32))
    mu = jnp.mean(y, -1, keepdims=True)
    var = jnp.mean(jnp.square(y - mu), -1, keepdims=True)
    y = ((y - mu) * lax.rsqrt(var + EPS_GN)).reshape(B, T, D_RWKV)
    y = y * p["ln_x_g"].astype(f32) + p["ln_x_b"].astype(f32)
    bonus = jnp.sum(rh * kh * p["r_k"].astype(f32), -1, keepdims=True) * vh
    y = y + bonus.reshape(B, T, D_RWKV)
    rwkv_out = (y.astype(xn.dtype) * g) @ p["w_o_rwkv"]

    merged = gates[..., :D_MODEL] * conv_out + gates[..., D_MODEL:] * rwkv_out
    return merged @ p["w_out"], new_conv, new_shift, new_wkv.astype(xn.dtype)

def _mem_kv(mem, g_mem, w_k_mem, w_v_mem):
    B = mem.shape[0]
    mn = _rms(mem, g_mem)
    mk = (mn @ w_k_mem).reshape(B, N_MEM, N_XHEADS, XHEAD_DIM)
    mv = (mn @ w_v_mem).reshape(B, N_MEM, N_XHEADS, XHEAD_DIM)
    return mk, mv

def _cross_attn(xn, mem_k, mem_v, w_q_x, w_o_x):
    B, T, _ = xn.shape
    q = (xn @ w_q_x).reshape(B, T, N_XHEADS, XHEAD_DIM)
    s = jnp.einsum('bthd,bmhd->bhtm', q, mem_k.astype(q.dtype)).astype(jnp.float32) * (XHEAD_DIM ** -0.5)
    pw = jax.nn.softmax(s, -1).astype(xn.dtype)
    o = jnp.einsum('bhtm,bmhd->bthd', pw, mem_v.astype(xn.dtype)).reshape(B, T, D_MODEL)
    return o @ w_o_x

def _swiglu(xn, w_gate, w_up, w_down):
    return (jax.nn.silu(xn @ w_gate) * (xn @ w_up)) @ w_down

def _layer(x, mem_k, mem_v, conv_buf, shift_buf, wkv_state, p):
    mix, new_conv, new_shift, new_wkv = _mixer(_rms(x, p["g_norm_mix"]), conv_buf, shift_buf, wkv_state, p)
    h = x + mix
    h = h + _cross_attn(_rms(h, p["g_norm_x"]), mem_k, mem_v, p["w_q_x"], p["w_o_x"])
    h = h + _swiglu(_rms(h, p["g_norm_ffn"]), p["w_ffn_gate"], p["w_ffn_up"], p["w_ffn_down"])
    return h, new_conv, new_shift, new_wkv

def setup_inputs(seed: int = 0) -> dict:
    key = jax.random.key(seed)
    ks = iter(jax.random.split(key, 64))
    f32 = jnp.float32
    L = DEPTH
    D = D_MODEL

    def nrm(shape, scale):
        return jax.random.normal(next(ks), shape, f32) * scale

    def gain(shape):
        return 1.0 + nrm(shape, 0.02)

    def unif(shape, lo, hi):
        return jax.random.uniform(next(ks), shape, f32, lo, hi)

    return {
        "x_prompt": nrm((BATCH, SEQ, D), 1.0),
        "x_sample": nrm((DEC_BATCH, DEC_SEQ, D), 1.0),
        "cache_mem_k": nrm((L, DEC_BATCH, N_MEM, N_XHEADS, XHEAD_DIM), 1.0),
        "cache_mem_v": nrm((L, DEC_BATCH, N_MEM, N_XHEADS, XHEAD_DIM), 1.0),
        "state_conv": nrm((L, DEC_BATCH, CONV_BUF, D_CONV), 0.5),
        "state_shift": nrm((L, DEC_BATCH, 1, D_SHIFT), 1.0),
        "state_wkv": nrm((L, DEC_BATCH, RWKV_HEADS, RWKV_HEAD, RWKV_HEAD), 1.0),
        "mem_prompt": nrm((BATCH, N_MEM, D), 1.0),
        "g_norm_mix": gain((L, D)),
        "w_in": nrm((L, D, D_IN), D ** -0.5),
        "mu_shift": unif((L, D_SHIFT), 0.0, 1.0),
        "w_dw": nrm((L, CONV_WIDTH, D_CONV), CONV_WIDTH ** -0.5),
        "b_dw": nrm((L, D_CONV), 0.02),
        "ln_conv_g": gain((L, D_CONV)),
        "ln_conv_b": nrm((L, D_CONV), 0.02),
        "w_o_conv": nrm((L, D_CONV, D), D_CONV ** -0.5),
        "w0": unif((L, D_RWKV), -3.0, 1.0),
        "w_up": nrm((L, D_DECAY_LORA, D_RWKV), 0.5 * D_DECAY_LORA ** -0.5),
        "a0": nrm((L, D_RWKV), 0.1),
        "a_up": nrm((L, D_AAA_LORA, D_RWKV), 0.5 * D_AAA_LORA ** -0.5),
        "g_up": nrm((L, D_GATE_LORA, D_RWKV), D_GATE_LORA ** -0.5),
        "k_k": 0.85 + nrm((L, D_RWKV), 0.02),
        "k_a": gain((L, D_RWKV)),
        "r_k": nrm((L, RWKV_HEADS, RWKV_HEAD), 0.1),
        "ln_x_g": gain((L, D_RWKV)),
        "ln_x_b": nrm((L, D_RWKV), 0.02),
        "w_o_rwkv": nrm((L, D_RWKV, D), D_RWKV ** -0.5),
        "w_out": nrm((L, D, D), D ** -0.5),
        "g_norm_x": gain((L, D)),
        "g_mem": gain((L, D)),
        "w_q_x": nrm((L, D, D), D ** -0.5),
        "w_k_mem": nrm((L, D, D), D ** -0.5),
        "w_v_mem": nrm((L, D, D), D ** -0.5),
        "w_o_x": nrm((L, D, D), D ** -0.5),
        "g_norm_ffn": gain((L, D)),
        "w_ffn_gate": nrm((L, D, D_FF), D ** -0.5),
        "w_ffn_up": nrm((L, D, D_FF), D ** -0.5),
        "w_ffn_down": nrm((L, D_FF, D), D_FF ** -0.5),
        "g_norm_final": gain((D,)),
    }

def reference(x_prompt, x_sample, cache_mem_k, cache_mem_v, state_conv, state_shift, state_wkv, mem_prompt,
              g_norm_mix, w_in, mu_shift, w_dw, b_dw, ln_conv_g, ln_conv_b, w_o_conv,
              w0, w_up, a0, a_up, g_up, k_k, k_a, r_k, ln_x_g, ln_x_b, w_o_rwkv, w_out,
              g_norm_x, g_mem, w_q_x, w_k_mem, w_v_mem, w_o_x,
              g_norm_ffn, w_ffn_gate, w_ffn_up, w_ffn_down, g_norm_final):
    Bp = x_prompt.shape[0]
    dt = x_prompt.dtype
    hp, hs = x_prompt, x_sample
    mk_l, mv_l, cp_l, sp_l, wp_l, cs_l, ss_l, ws_l = [], [], [], [], [], [], [], []
    for i in range(DEPTH):
        p = {
            "g_norm_mix": g_norm_mix[i], "w_in": w_in[i], "mu_shift": mu_shift[i],
            "w_dw": w_dw[i], "b_dw": b_dw[i], "ln_conv_g": ln_conv_g[i], "ln_conv_b": ln_conv_b[i],
            "w_o_conv": w_o_conv[i], "w0": w0[i], "w_up": w_up[i], "a0": a0[i], "a_up": a_up[i],
            "g_up": g_up[i], "k_k": k_k[i], "k_a": k_a[i], "r_k": r_k[i], "ln_x_g": ln_x_g[i],
            "ln_x_b": ln_x_b[i], "w_o_rwkv": w_o_rwkv[i], "w_out": w_out[i],
            "g_norm_x": g_norm_x[i], "w_q_x": w_q_x[i], "w_o_x": w_o_x[i],
            "g_norm_ffn": g_norm_ffn[i], "w_ffn_gate": w_ffn_gate[i], "w_ffn_up": w_ffn_up[i],
            "w_ffn_down": w_ffn_down[i],
        }
        mk, mv = _mem_kv(mem_prompt, g_mem[i], w_k_mem[i], w_v_mem[i])
        conv0 = jnp.zeros((Bp, CONV_BUF, D_CONV), dt)
        shift0 = jnp.zeros((Bp, 1, D_SHIFT), dt)
        wkv0 = jnp.zeros((Bp, RWKV_HEADS, RWKV_HEAD, RWKV_HEAD), jnp.float32)
        hp, cp, sp, wp = _layer(hp, mk, mv, conv0, shift0, wkv0, p)
        hs, cs, ss, ws = _layer(hs, cache_mem_k[i], cache_mem_v[i], state_conv[i], state_shift[i],
                                state_wkv[i], p)
        mk_l.append(mk); mv_l.append(mv); cp_l.append(cp); sp_l.append(sp); wp_l.append(wp)
        cs_l.append(cs); ss_l.append(ss); ws_l.append(ws)
    y_prompt = _rms(hp, g_norm_final)
    y_sample = _rms(hs, g_norm_final)
    mem_k_prompt = jnp.stack(mk_l)
    mem_v_prompt = jnp.stack(mv_l)
    conv_prompt = jnp.stack(cp_l)
    shift_prompt = jnp.stack(sp_l)
    wkv_prompt = jnp.stack(wp_l)
    conv_sample = jnp.stack(cs_l)
    shift_sample = jnp.stack(ss_l)
    wkv_sample = jnp.stack(ws_l)
    return (y_prompt, y_sample, mem_k_prompt, mem_v_prompt, conv_prompt, shift_prompt, wkv_prompt,
            conv_sample, shift_sample, wkv_sample)


_drawn_inputs = setup_inputs


def setup_inputs(seed=0):
    import zlib

    import numpy as np

    out = dict(_drawn_inputs(seed))
    spreads = {}
    factors = {'b_dw': 4.192,
     'ln_conv_g': 7.327,
     'ln_conv_b': 8.0,
     'k_k': 8.0,
     'ln_x_g': 8.0,
     'ln_x_b': 8.0,
     'g_norm_x': 8.0,
     'g_mem': 2.925,
     'g_norm_ffn': 4.162,
     'g_norm_final': 2.869}
    for name, (base, spread) in spreads.items():
        noise = np.random.default_rng([zlib.crc32(name.encode()), seed]).standard_normal(out[name].shape)
        drawn = base * np.exp(spread * noise) if base else spread * noise
        out[name] = __import__('jax').numpy.asarray(drawn.astype(out[name].dtype))
    for name, factor in factors.items():
        out[name] = (out[name] * factor).astype(out[name].dtype)
    return out
```

```python
from contextlib import ExitStack, nullcontext

import concourse.bass as bass
import numpy as np
from concourse import mybir

F32 = mybir.dt.float32
F32R = mybir.dt.float32r
ALU = mybir.AluOpType
ACT = mybir.ActivationFunctionType
AX = mybir.AxisListType

P = 128
D = 1024
DT = D // P
SEQ = 512
NS = 8
TS = 16
NT = SEQ + NS * TS
HALF = NT // 2
DC = 512
CT = DC // P
TAPS = 31
BUF = TAPS - 1
NMEM = 256
XH = 4
HEADS = 16
DFF = 2816
SHT = 26
RT = 24
C = 64
NCH = SEQ // C
LEVELS = 6
DECAY = float(np.exp(-0.5))
EPS_RMS, EPS_LN, EPS_GN = 1e-6, 1e-5, 64e-5
UW = (BUF + SEQ) + NS * (BUF + TS)
PW = (1 + SEQ) + NS * (1 + TS)

VECS = [("g_norm_mix", 8), ("mu_shift", 26), ("b_dw", 4), ("ln_conv_g", 4), ("ln_conv_b", 4), ("w0", 8), ("a0", 8),
        ("k_k", 8), ("k_a", 8), ("r_k", 8), ("ln_x_g", 8), ("ln_x_b", 8), ("g_norm_x", 8), ("g_mem", 8),
        ("g_norm_ffn", 8), ("g_norm_final", 8), ("w_dw", CT * TAPS)]
VCOL, _n = {}, 0
for _name, _w in VECS:
    VCOL[_name] = _n
    _n += _w
NVEC = _n

CONSTS = [("ident", 128), ("mean_d", 128), ("mean_c", 128), ("head_sum", 128),
          ("stream", 4), ("eps", 3)]
CCOL, _n = {}, 0
for _name, _w in CONSTS:
    CCOL[_name] = _n
    _n += _w
NCONST = _n
STREAM_LEVELS = 4
NWMASK = 2 * 128 + (LEVELS + 1) * 128

THIRDS = (8, 8, 6)
SLOTS, _n = {}, 0
for _name, _w in [("glu", 8), ("rkv", 24), ("lora", 2), ("gate", 16), ("conv", 8), ("orwkv", 8), ("out", 8),
                  ("mk", 8), ("mv", 8), ("q", 8), ("ox", 8), ("f0", 16), ("d0", 8), ("f1", 16), ("d1", 8),
                  ("f2", 12), ("d2", 8)]:
    SLOTS[_name] = (_n, _w)
    _n += _w
NSLOT = _n


def program(nc, io):
    ctx = ExitStack()
    with ctx:
        base = -(-nc.sbuf_base // 32) * 32

        def at(name, offset, shape, dt=F32):
            return nc.alloc_sbuf_tensor_at(name, shape, dt, offset=base + offset)

        def sem(name):
            return ctx.enter_context(nc.semaphore(name))

        KB = 1024
        raw = [at(f"raw{s}", s * 4 * KB, [P, D]) for s in range(2)]
        whi = [at(f"whi{s}", (2 + s) * 4 * KB, [P, 8, P], F32R) for s in range(2)]
        wlo = [at(f"wlo{s}", (4 + s) * 4 * KB, [P, 8, P], F32R) for s in range(2)]
        o = 24 * KB
        cst = at("cst", o, [P, NCONST]); o += -(-4 * NCONST // 32) * 32
        wmask = at("wmask", o, [P, NWMASK]); o += 4 * NWMASK
        vec = at("vec", o, [P, NVEC]); o += -(-4 * NVEC // 32) * 32
        par = at("par", o, [P, 40]); o += 160
        o = -(-o // 64) * 64
        T20 = 4 * DT * NT
        A_O, K_O, V_O, B_O, M_O = o, o + 2 * T20, o + 3 * T20, o + 4 * T20, o + 5 * T20
        W_O = M_O + 3 * 2560 + 512
        ar = at("ar", A_O, [P, DT, 2, NT])
        kt = at("kt", K_O, [P, DT, NT])
        vt = at("vt", V_O, [P, DT, NT])
        bt = at("bt", B_O, [P, DT, NT])
        lora = at("lora", M_O, [P, NT])
        sgd = at("sgd", M_O + 2560, [P, NT])
        bon = at("bon", M_O + 5120, [16, NT])
        wcum = at("wcum", M_O + 7680, [P, DT, 16])
        xnh = at("xnh", B_O, [P, DT, NT], F32R)
        xnl = at("xnl", W_O, [P, DT, NT], F32R)
        up = at("up", W_O + T20, [P, CT, UW])
        acc = at("acc", W_O + T20 + 4 * CT * UW, [P, CT, NT])
        o = W_O + T20 + 4 * CT * UW + 4 * CT * NT
        pr = [at(f"pr{s}", o + s * 2624, [P, PW]) for s in range(2)]
        tmp = [at(f"tmp{s}", o + (2 + s) * 2624, [P, PW]) for s in range(2)]
        o += 4 * 2624
        shin = at("shin", o, [P, SHT, NS]); o += 4 * SHT * NS
        shout = at("shout", o, [P, SHT, 1 + NS]); o += 4 * SHT * (1 + NS)
        assert o <= 212800, o
        xin = at("xin", W_O + T20, [P, DT, NT])
        sq = [at(f"sq{s}", V_O + s * 2560, [P, NT]) for s in range(2)]
        std = at("std", V_O + 5120, [P, NT])
        rstd = at("rstd", V_O + 7680, [P, NT])
        xnf = [at(f"xnf{s}", V_O + 10240 + s * 2560, [P, NT]) for s in range(2)]
        ch = at("ch", W_O, [P, CT, NT], F32R)
        cl = at("cl", W_O + T20 // 2, [P, CT, NT], F32R)
        lw = at("lw", W_O + T20, [P, D])
        erow = at("erow", W_O + T20 + 4096, [16, D])
        smask = at("smask", W_O + T20 + 8192, [P, NT])
        slot_o = [W_O + q * 2560 for q in range(8)] + [W_O + T20 + 4 * CT * UW + q * 2560 for q in range(13)]

        def pair(name):
            return [at(f"{name}{s}", slot_o.pop(0), [P, NT]) for s in range(2)]

        p_l, p_L, p_m, p_e1, p_ta, p_kf, p_kk, p_b2, p_rk = [
            pair(n) for n in ("p_l", "p_L", "p_m", "p_e1", "p_ta", "p_kf", "p_kk", "p_b2", "p_rk")]
        rn = at("rn", slot_o.pop(0), [16, NT])
        o = W_O

        def blk(name):
            nonlocal o
            o += 4096
            return at(name, o - 4096, [P, 8, P])

        def stk(name, w=64):
            nonlocal o
            o += 8 * w * 4
            return at(name, o - 8 * w * 4, [P, 8, w])

        bd, kd, ad, vd = blk("bd"), blk("kd"), blk("ad"), blk("vd")
        atd, akd, xtd, td = blk("atd"), blk("akd"), blk("xtd"), blk("td")
        btd, ktd, vtd, sd = blk("btd"), blk("ktd"), blk("vtd"), blk("sd")
        ud, xd, rhsd = blk("ud"), blk("xd"), blk("rhsd")
        scb, sck = stk("scb", 128), stk("sck", 128)
        assert o <= 212800, o
        ssd = bt[:, :, 0:SEQ].rearrange("p t (b c) -> p t b c", b=4)
        um = kt[:, :, 0:256].rearrange("p t (b c) -> p t b c", b=4)
        vm = kt[:, :, 256:512].rearrange("p t (b c) -> p t b c", b=4)
        ns = ar[:, :, 0, 0:256].rearrange("p t (b c) -> p t b c", b=4)
        gup = at("gup", W_O + 4096, [P, D])
        erow2 = at("erow2", W_O, [16, D])
        mean16 = at("mean16", W_O + 8192, [16, NT])
        rstd16 = at("rstd16", W_O + 8192 + 2560, [16, NT])
        psq = [at(f"psq{s}", W_O + 8192 + (2 + s) * 2560, [P, NT]) for s in range(2)]
        bv = at("bv", M_O, [P, NT])
        po = [at(f"po{s}", W_O + T20 + 2 * T20 + s * 2560, [P, NT]) for s in range(2)]
        yoh = at("yoh", K_O, [P, DT, NT], F32R)
        yol = at("yol", B_O, [P, DT, NT], F32R)
        m1t = at("m1t", W_O + T20, [P, DT, NT])
        t2t = at("t2t", W_O + 2 * T20, [P, DT, NT])
        mgh = at("mgh", A_O, [P, DT, NT], F32R)
        mgl = at("mgl", A_O + T20, [P, DT, NT], F32R)

        ht = at("ht", V_O, [P, DT, NT])
        q_o = W_O
        n2_bufs = ([at(f"sqb{s}", q_o + s * 2560, [P, NT]) for s in range(2)], at("stdb", q_o + 5120, [P, NT]),
                   at("rstdb", q_o + 7680, [P, NT]), [at(f"xnb{s}", q_o + 10240 + s * 2560, [P, NT]) for s in range(2)])
        hnh = at("hnh", B_O, [P, DT, NT], F32R)
        hnl = at("hnl", W_O + T20, [P, DT, NT], F32R)
        T8 = 4 * DT * NMEM
        memt = at("memt", W_O + 2 * T20, [P, DT, NMEM])
        memh = at("memh", W_O + 2 * T20 + T8, [P, DT, NMEM], F32R)
        meml = at("meml", W_O + 2 * T20 + 2 * T8, [P, DT, NMEM], F32R)
        mkt = at("mkt", A_O, [P, DT, NMEM])
        mvt = at("mvt", A_O + T8, [P, DT, NMEM])
        mv = at("mv", A_O + 2 * T8, [P, 2, D])
        qt = at("qt", A_O + 3 * T8, [P, DT, NT])
        pt = at("pt", A_O + 3 * T8 + T20, [P, 2, XH, SEQ])
        kc = at("kc", B_O, [P, DT, 2 * NMEM])
        vc = at("vc", W_O + T20, [P, 4, D])
        pex = [at(f"pex{s}", B_O + 2 * T8 + s * 4096, [P, 1024]) for s in range(2)]
        xmask = at("xmask", B_O + 2 * T8 + 8192, [P, 2 * NMEM])
        o = B_O + 2 * T8 + 10240
        mx = at("mx", o, [P, 2, XH])
        nmx = at("nmx", o + 32, [P, 2, XH])
        sm = at("sm", o + 64, [P, 2, XH])
        rs = at("rs", o + 96, [P, 2, XH])
        assert o + 128 <= W_O
        oth = at("oth", W_O + 2 * T20, [P, DT, NT], F32R)
        otl = at("otl", W_O, [P, DT, NT], F32R)
        n3_bufs = ([at(f"sqc{s}", B_O + s * 2560, [P, NT]) for s in range(2)], at("stdc", B_O + 5120, [P, NT]),
                   at("rstdc", B_O + 7680, [P, NT]), [at(f"xnc{s}", B_O + 10240 + s * 2560, [P, NT]) for s in range(2)])
        fnh = at("fnh", A_O, [P, DT, NT], F32R)
        fnl = at("fnl", A_O + T20, [P, DT, NT], F32R)
        hdh = at("hdh", W_O, [P, DT, NT], F32R)
        hdl = at("hdl", W_O + T20, [P, DT, NT], F32R)
        fth = at("fth", W_O + 2 * T20, [P, NT])
        fsg = at("fsg", W_O + 2 * T20 + 2560, [P, NT])
        fhd = at("fhd", W_O + 2 * T20 + 5120, [P, NT])

        ps = [ctx.enter_context(nc.psum_tensor(f"ps{i}", [P, 1024], F32)) for i in range(4)]
        CUT = 512 - HALF

        def span(t, n=NT):
            return t[:, CUT:CUT + NT] if n == NT else t[:, 0:n]

        def cut(t, h, n=NT):
            return t[:, CUT + h * HALF:CUT + (h + 1) * HALF] if n == NT else t[:, 0:n]

        def bank(g, b):
            return ps[2 * g + b // 2][:, 512 * (b % 2):512 * (b % 2) + 512]

        def const(name):
            c = CCOL[name]
            return cst[:, c:c + dict(CONSTS)[name]]

        def v1(name, k):
            if isinstance(k, int):
                return vec[:, VCOL[name] + k:VCOL[name] + k + 1]
            return vec[:, bass.ds(k + VCOL[name], 1)]

        def eps(i):
            return cst[:, CCOL["eps"] + i:CCOL["eps"] + i + 1]

        def row(a):
            return a.rearrange("p a n -> p (a n)")

        def tile_of(a, k, part=None):
            ks = slice(k, k + 1) if isinstance(k, int) else bass.ds(k, 1)
            return row(a[:, ks, :] if part is None else a[:, ks, part, :])

        def streams(a, start, width, off, n):
            return a[:, start:start + NS * width].rearrange("p (b c) -> p b c", b=NS)[:, :, off:off + n]

        def by_stream(a):
            return a.rearrange("p (b c) -> p b c", b=NS)

        names = """consts_in x_in w_hi w_lo mm_done params sq_ready sq_summed ms_ready std_ready rstd_ready xn_ready
            xh_ready xl_ready glu_gate u_ready history_in pad_ready pr_ready pr_free diff_ready
            lora_tanh conv_step conv_done cmean_ready centred square_ready square_summed var_ready dev_ready inv_ready
            cn_ready ct_ready cs_ready ch_ready cl_ready stored lw_in
            rn_ready z_ready tz_ready rnb_ready e_ready prep_dve prep_pool bonus_ready bonus_in
            pool_waits zeroed staged ad_staged sck_in sc_ready tb_ready vd_ready scm ad_e ad_o ak_o bkt_in v_in t_ready t_new x_ready
            x_new x_part xt_new xt_part rhs_ready rhs_in u_psum u_in s_ready s_sum s_new y_ready y_in sig_ready
            ss_in pst_ready pd_e pd_o ys_in um_ready ns_out up_zero pr_zero shift_half bonus_used ns_sum ysum_ready mean_in mb_ready g3_ready             post_dve po_ready yh_ready yl_ready mt_in merge_dve mg_ready mgh_ready mgl_ready res_in mem_in h_added mk_in mvt_in q_in mvx_ready mv_in             sp_ready mx_ready ex_ready pn_ready ptp_ready pt_in o_ready oh_ready ol_ready kc_in vc_in xm_in             kc_used vc_used ft_ready fh_ready fhh_ready             fhl_ready y_done all_stored gup_in""".split()
        S = {n: sem(n) for n in names}
        raw_in = [sem(f"raw_in{s}") for s in range(2)]
        psum_free = [sem(f"psum_free{s}") for s in range(2)]
        g2_out = [sem(f"g2_out{s}") for s in range(2)]
        m1_out = [sem(f"m1_out{s}") for s in range(2)]

        block = ctx.enter_context(nc.Block())

        def load_slots(sp, lo, hi):
            with sp.Fori(0, (hi - lo) // 2) as i:
                for s in range(2):
                    if lo > 0:
                        sp.wait_ge(S["w_lo"], 2 * i + (lo + s - 1))
                    sp.dma_start(raw[s][:], io["slots"][bass.ds(2 * i + (lo + s), 1), :, :].rearrange("a p n -> (a p) n"))\
                        .then_inc(raw_in[s], 16)

        def hi_part(act, i, m, first=False):
            s = m % 2
            act.wait_ge(raw_in[s], 16 * i + 16 * (m // 2) + 16)
            if not first:
                act.wait_ge(S["mm_done"], 2 * i + (m + 1))
            nc.scalar.activation(whi[s][:].rearrange("p a b -> p (a b)"), raw[s][:], ACT.Copy).then_inc(S["w_hi"], 1)

        def await_(pool, s, value):
            pool.wait_ge(s, value)
            pool.sem_inc(S["pool_waits"], 1)

        def lo_part(pool, i, m):
            s = m % 2
            pool.wait_ge(S["w_hi"], 2 * i + (m + 1))
            nc.gpsimd.tensor_tensor(wlo[s][:].rearrange("p a b -> p (a b)"), raw[s][:],
                                    whi[s][:].rearrange("p a b -> p (a b)").bitcast(F32), ALU.subtract).then_inc(S["w_lo"], 1)

        def dense(pe, stage, hi, lo, k_tiles=DT, n=NT):
            n0, cnt = SLOTS[stage]
            nh = 2 if n == NT else 1
            w = n // nh
            with pe.Fori(0, cnt // 2) as i:
                for s in range(2):
                    pe.wait_ge(S["w_lo"], 2 * i + (n0 + s + 1))
                    pe.wait_ge(psum_free[s], i + (n0 // 2 + 1))
                    for k in range(k_tiles):
                        for q, (a, b) in enumerate(((whi[s], lo), (whi[s], hi), (wlo[s], hi))):
                            for h in range(nh):
                                last = nc.tensor.matmul(cut(ps[s], h, n), a[:, k, :], b[:, k, h * w:(h + 1) * w],
                                                        start=(k == 0 and q == 0), stop=(k == k_tiles - 1 and q == 2))
                    last.then_inc(S["mm_done"], 1)

        def norm_act(act, q, src, xh, bufs, n=NT):
            sqb, stdb, _, xnb = bufs
            for k in range(DT):
                if 8 * q + k >= 2:
                    act.wait_ge(S["sq_summed"], 8 * q + k - 1)
                nc.scalar.activation(sqb[k % 2][:, 0:n], src(k), ACT.Square).then_inc(S["sq_ready"], 1)
            act.wait_ge(S["ms_ready"], q + 1)
            nc.scalar.activation(stdb[:, 0:n], span(ps[2], n), ACT.Sqrt, bias=eps(0)).then_inc(S["std_ready"], 1)
            if xh is None:
                return
            for k in range(DT):
                act.wait_ge(S["xn_ready"], 8 * q + k + 1)
                nc.scalar.activation(xh[:, k, 0:n], xnb[k % 2][:, 0:n], ACT.Copy).then_inc(S["xh_ready"], 1)

        def norm_pe(pe, q, bufs, n=NT):
            nh = 2 if n == NT else 1
            w = n // nh
            for k in range(DT):
                pe.wait_ge(S["sq_ready"], 8 * q + k + 1)
                for h in range(nh):
                    last = nc.tensor.matmul(cut(ps[2], h, n), const("mean_d"), bufs[0][k % 2][:, h * w:(h + 1) * w],
                                            start=(k == 0), stop=(k == DT - 1))
                last.then_inc(S["sq_summed"] if k < DT - 1 else S["ms_ready"], 1)
            pe.wait_ge(S["ms_ready"], q + 1)
            pe.sem_inc(S["sq_summed"], 1)

        def norm_dve(dve, q, src, gname, bufs, n=NT):
            _, stdb, rb, xnb = bufs
            dve.wait_ge(S["std_ready"], q + 1)
            nc.vector.reciprocal(rb[:, 0:n], stdb[:, 0:n]).then_inc(S["rstd_ready"], 1)
            dve.wait_ge(S["rstd_ready"], q + 1)
            for k in range(DT):
                if k >= 2:
                    dve.wait_ge(S["xl_ready"], 8 * q + k - 1)
                nc.vector.scalar_tensor_tensor(out=xnb[k % 2][:, 0:n], in0=src(k), scalar=v1(gname, k), in1=rb[:, 0:n],
                                               op0=ALU.mult, op1=ALU.mult).then_inc(S["xn_ready"], 1)

        def norm_pool(pool, q, xh, xl, bufs, n=NT):
            for k in range(DT):
                pool.wait_ge(S["xh_ready"], 8 * q + k + 1)
                nc.gpsimd.tensor_tensor(xl[:, k, 0:n], bufs[3][k % 2][:, 0:n], xh[:, k, 0:n].bitcast(F32),
                                        ALU.subtract).then_inc(S["xl_ready"], 1)


        gs = [slice(0, 4), slice(4, 8)]
        EVEN, ODD = slice(0, 64), slice(64, 128)
        RHS_LEVEL = 2

        def places(prompt, i):
            n = LEVELS if prompt else STREAM_LEVELS
            u0 = 2 * i + (0 if prompt else 2 * NCH)
            lv = lambda L, g: 2 * n * i + (0 if prompt else 2 * LEVELS * NCH) + 2 * L + g + 1
            lt = lambda L, g: 2 * (n - 1) * i + (0 if prompt else 2 * (LEVELS - 1) * NCH) + 2 * (L - 1) + g + 1
            return u0, bass.ds(C * i + (0 if prompt else SEQ), C), n, lv, lt, (lambda L, g: lt(L + 1, g))

        def four(a):
            return a.rearrange("p (t c) -> p t c", t=4)

        def rec_rhs_pe(w, prompt, i):
            mm = nc.tensor.matmul
            u0 = places(prompt, i)[0]
            if not prompt:
                w("ss_in", 16 * i + 16)
                for g in range(2):
                    w("v_in", u0 + g + 1)
                    for p in range(4):
                        t = 4 * g + p
                        v = bank(g, 3)[:, P * p:P * p + P].rearrange("p (a b c) -> p a b c", a=2, b=4)
                        for b in range(4):
                            last = mm(v[:, :, b, :], ssd[:, t, b, :], ar[:, t, :, bass.ds(C * i + (SEQ + TS * b), TS)],
                                      start=True, stop=True)
                    last.then_inc(S["pst_ready"], 1)
            for g in range(2):
                w("v_in", u0 + g + 1)
                w("ak_o", u0 + g + 1)
                if prompt:
                    w("s_new", u0 + g + 1)
                    w("ad_staged", u0 + g + 1)
                else:
                    w("pd_e", 2 * i + g + 1)
                    w("pd_o", 2 * i + g + 1)
                    w("ys_in", 2 * i + g + 1)
                for p in range(4):
                    t = 4 * g + p
                    out = bank(g, 3)[:, P * p:P * p + P]
                    mm(out, ad[:, t, :], sd[:, t, :] if prompt else const("ident"), start=True, stop=False)
                    last = mm(out, akd[:, t, :], vtd[:, t, :], start=False, stop=True)
                last.then_inc(S["rhs_ready"], 1)

        def rec_pe(pe, prompt, i):
            u0, col, n, lv, lt, lx = places(prompt, i)

            def w(name, v):
                pe.wait_ge(S[name], v)

            mm = nc.tensor.matmul
            for g in range(2):
                w("staged", u0 + g + 1)
                w("y_in", u0 + g + 1)
                for d, b in ((bd, 0), (kd, 1)):
                    for p in range(4):
                        last = mm(bank(g, b)[:, P * p:P * p + P].rearrange("p (a c) -> p a c", a=2), d[:, 4 * g + p, :],
                                  ar[:, 4 * g + p, :, col], start=True, stop=True)
                    last.then_inc(S["sc_ready"], 1)
            for g in range(2):
                w("s_new", u0 + g + 1)
                for d, b in ((bd, 2), (kd, 3)):
                    for p in range(4):
                        last = nc.tensor.transpose(bank(g, b)[:, P * p:P * p + P], d[:, 4 * g + p, :], const("ident"))
                last.then_inc(S["tb_ready"], 1)
            for L in range(n):
                for g in range(2):
                    if L == 0:
                        w("ad_e", u0 + g + 1)
                        w("ad_o", u0 + g + 1)
                    else:
                        w("x_new", lx(L - 1, g))
                    for p in range(4):
                        last = mm(bank(g, 0)[:, P * p:P * p + P], atd[:, 4 * g + p, :],
                                  const("ident") if L == 0 else xd[:, 4 * g + p, :], start=True, stop=True)
                    last.then_inc(S["t_ready"], 1)
                if L == 0:
                    for g in range(2):
                        w("bkt_in", u0 + g + 1)
                        for p in range(4):
                            last = nc.tensor.transpose(bank(g, 2)[:, P * p:P * p + P], vd[:, 4 * g + p, :], const("ident"))
                        last.then_inc(S["vd_ready"], 1)
                    continue
                if L == RHS_LEVEL:
                    rec_rhs_pe(w, prompt, i)
                for g in range(2):
                    w("t_new", lt(L, g))
                    w("xt_new", lv(L - 1, g))
                    if L == 1:
                        w("v_in", u0 + g + 1)
                    for p in range(4):
                        t = 4 * g + p
                        if L < n - 1:
                            mm(bank(g, 1)[:, P * p:P * p + P], xtd[:, t, :], td[:, t, :], start=True, stop=True)
                        last = mm(bank(g, 2)[:, P * p:P * p + P], td[:, t, :], xtd[:, t, :], start=True, stop=True)
                    last.then_inc(S["x_ready"], 1)
            for g in range(2):
                w("xt_new", lv(n - 1, g))
                w("rhs_in", u0 + g + 1)
                for p in range(4):
                    last = mm(bank(g, 3)[:, P * p:P * p + P], xtd[:, 4 * g + p, :], rhsd[:, 4 * g + p, :], start=True, stop=True)
                last.then_inc(S["u_psum"], 1)
            for g in range(2):
                w("u_in", u0 + g + 1)
                if prompt:
                    for p in range(4):
                        t = 4 * g + p
                        out = bank(g, 2)[:, P * p:P * p + P]
                        mm(out, btd[:, t, :], ud[:, t, :], start=True, stop=False)
                        last = mm(out, ktd[:, t, :], vtd[:, t, :], start=False, stop=True)
                else:
                    w("um_ready", 2 * i + g + 1)
                    for p in range(4):
                        t = 4 * g + p
                        out = bank(g, 3 - p // 2)[:, 256 * (p % 2):256 * (p % 2) + 256]
                        mm(out, btd[:, t, :], um[:, t, :, :], start=True, stop=False)
                        last = mm(out, ktd[:, t, :], vm[:, t, :, :], start=False, stop=True)
                last.then_inc(S["s_ready"], 1)
            for g in range(2):
                for p in range(4):
                    t = 4 * g + p
                    out = bank(g, 1)[:, 64 * p:64 * p + 64]
                    if prompt:
                        mm(out, sd[:, t, :], ar[:, t, 1, col], start=True, stop=False)
                    mm(out, ud[:, t, :], scb[:, t, 64:128], start=not prompt, stop=False)
                    last = mm(out, vtd[:, t, :], sck[:, t, 64:128], start=False, stop=True)
                last.then_inc(S["y_ready"], 1)

        def rec_pool(pool, prompt, i):
            u0, col = places(prompt, i)[:2]
            for g in range(2):
                await_(pool, S["vd_ready"], u0 + g + 1)
                for dst, src in ((bd, bt), (kd, kt), (vd, vt)):
                    for h in (EVEN, ODD):
                        last = nc.gpsimd.tensor_copy(dst[h, gs[g], h], src[h, gs[g], col])
                last.then_inc(S["staged"], 1)
            if prompt:
                for g in range(2):
                    await_(pool, S["rhs_ready"], u0 + g + 1)
                    for h in (EVEN, ODD):
                        last = nc.gpsimd.tensor_copy(ad[h, gs[g], h], ar[h, gs[g], 0, col])
                    last.then_inc(S["ad_staged"], 1)

        def rec_act(act, prompt, i):
            u0, col, n, lv, lt, lx = places(prompt, i)

            def w(name, v):
                act.wait_ge(S[name], v)

            def copy(out, in_):
                return nc.scalar.activation(out, in_, ACT.Copy)

            for g in range(2):
                w("scm", u0 + g + 1)
                copy(atd[EVEN, gs[g], EVEN], scb[EVEN, gs[g], 0:64]).then_inc(S["ad_e"], 1)
            for g in range(2):
                w("tb_ready", u0 + g + 1)
                copy(btd[:, gs[g], :], four(bank(g, 2)[:, :]))
                copy(ktd[:, gs[g], :], four(bank(g, 3)[:, :])).then_inc(S["bkt_in"], 1)
            for g in range(2):
                w("sck_in", u0 + g + 1)
                copy(akd[EVEN, gs[g], EVEN], sck[EVEN, gs[g], 0:64])
                w("vd_ready", u0 + g + 3)
                copy(vtd[:, gs[g], :], four(bank(g, 2)[:, :])).then_inc(S["v_in"], 1)
            for g in range(2):
                if not prompt:
                    w("pst_ready", 2 * i + g + 1)
                    v = bank(g, 3)[:, :].rearrange("p (t a c) -> p t a c", t=4, a=2)
                    copy(ad[EVEN, gs[g], EVEN], v[EVEN, :, 0, :]).then_inc(S["pd_e"], 1)
                    w("pd_o", 2 * i + g + 1)
                    copy(sd[:, gs[g], 0:64], v[:, :, 1, :]).then_inc(S["ys_in"], 1)
            for g in range(2):
                w("rhs_ready", u0 + g + 3)
                copy(rhsd[:, gs[g], :], four(bank(g, 3)[:, :])).then_inc(S["rhs_in"], 1)
            for g in range(2):
                w("u_psum", u0 + g + 1)
                copy(ud[:, gs[g], :], four(bank(g, 3)[:, :])).then_inc(S["u_in"], 1)
            if prompt:
                for g in range(2):
                    w("y_ready", u0 + g + 1)
                    copy(ar[:, gs[g], 1, col], four(bank(g, 1)[:, 0:256])).then_inc(S["y_in"], 1)

        def rec_dve(dve, prompt, i):
            u0, col, n, lv, lt, lx = places(prompt, i)

            def w(name, v):
                dve.wait_ge(S[name], v)

            tt = nc.vector.tensor_tensor

            def b4(a, n=64, parts=slice(0, P)):
                return a[parts].rearrange("p (a c) -> p a c", a=1).to_broadcast([len(range(*parts.indices(P))), 4, n])

            m0 = 0 if prompt else 128
            step = lambda L: b4(wmask[:, 256 + P * L:256 + P * L + P], P)
            one = b4(const("ident"), P)
            for g in range(2):
                w("sc_ready", 2 * u0 + (2 * g + 1))
                tt(scb[:, gs[g], :], four(bank(g, 0)[:, :]), b4(wmask[:, m0:m0 + 128], 128), ALU.mult).then_inc(S["scm"], 1)
                tt(atd[ODD, gs[g], ODD], four(bank(g, 0)[:, :])[ODD, :, 0:64], b4(wmask[:, m0:m0 + 64], 64, ODD), ALU.mult)\
                    .then_inc(S["ad_o"], 1)
            for g in range(2):
                w("ad_e", u0 + g + 1)
                w("ad_o", u0 + g + 1)
                tt(xtd[:, gs[g], :], atd[:, gs[g], :], step(LEVELS), ALU.mult).then_inc(S["xt_part"], 1)
            for g in range(2):
                w("xt_part", u0 + g + 1)
                tt(xtd[:, gs[g], :], xtd[:, gs[g], :], one, ALU.add).then_inc(S["xt_new"], 1)
            for g in range(2):
                w("t_ready", lv(0, g))
                tt(xd[:, gs[g], :], four(bank(g, 0)[:, :]), step(0), ALU.mult).then_inc(S["x_part"], 1)
            for g in range(2):
                w("x_part", u0 + g + 1)
                tt(xd[:, gs[g], :], xd[:, gs[g], :], one, ALU.add).then_inc(S["x_new"], 1)
            for g in range(2):
                w("sc_ready", 2 * u0 + (2 * g + 2))
                tt(sck[:, gs[g], :], four(bank(g, 1)[:, :]), b4(wmask[:, m0:m0 + 128], 128), ALU.mult).then_inc(S["sck_in"], 1)
                tt(akd[ODD, gs[g], ODD], four(bank(g, 1)[:, :])[ODD, :, 0:64], b4(wmask[:, m0:m0 + 64], 64, ODD), ALU.mult)\
                    .then_inc(S["ak_o"], 1)
            for L in range(1, n):
                for g in range(2):
                    w("t_ready", lv(L, g))
                    tt(td[:, gs[g], :], four(bank(g, 0)[:, :]), step(L), ALU.mult).then_inc(S["t_new"], 1)
                if L == RHS_LEVEL and not prompt:
                    for g in range(2):
                        w("pst_ready", 2 * i + g + 1)
                        v = bank(g, 3)[:, :].rearrange("p (t a c) -> p t a c", t=4, a=2)
                        w("pd_e", 2 * i + g + 1)
                        nc.vector.tensor_copy(ad[ODD, gs[g], ODD], v[ODD, :, 0, :]).then_inc(S["pd_o"], 1)
                for g in range(2):
                    w("x_ready", lt(L, g))
                    if L < n - 1:
                        w("x_new", lx(L - 1, g))
                        tt(xd[:, gs[g], :], four(bank(g, 1)[:, :]), xd[:, gs[g], :], ALU.add).then_inc(S["x_new"], 1)
                    w("xt_new", lv(L - 1, g))
                    tt(xtd[:, gs[g], :], four(bank(g, 2)[:, :]), xtd[:, gs[g], :], ALU.add).then_inc(S["xt_new"], 1)
            if prompt:
                for g in range(2):
                    w("s_ready", u0 + g + 1)
                    w("y_ready", u0 + g + 1)
                    w("s_new", u0 + g + 1)
                    tt(sd[:, gs[g], :], four(bank(g, 2)[:, :]), sd[:, gs[g], :], ALU.add).then_inc(S["s_sum"], 1)
                for g in range(2):
                    w("s_sum", u0 + g + 1)
                    tt(sd[:, gs[g], :], sd[:, gs[g], :], wcum[:, gs[g], bass.ds(i, 1)].to_broadcast([P, 4, P]), ALU.mult)\
                        .then_inc(S["s_new"], 1)
            else:
                for g in range(2):
                    w("u_in", u0 + g + 1)
                    for b in range(4):
                        sb_ = cst[:, CCOL["stream"] + b:CCOL["stream"] + b + 1]
                        for h in (EVEN, ODD):
                            nc.vector.tensor_scalar(um[h, gs[g], b, :], ud[h, gs[g], h], sb_[h], None, ALU.mult)
                            last = nc.vector.tensor_scalar(vm[h, gs[g], b, :], vtd[h, gs[g], h], sb_[h], None, ALU.mult)
                    last.then_inc(S["um_ready"], 1)
                for g in range(2):
                    w("s_ready", u0 + g + 1)
                    w("ns_out", 16 * i + 16)
                    for hp in range(2):
                        pp = slice(4 * g + 2 * hp, 4 * g + 2 * hp + 2)
                        for h in (slice(0, 64), slice(64, 128)):
                            tt(ns[h, pp, :, :], bank(g, 3 - hp)[h, :].rearrange("p (t b c) -> p t b c", t=2, b=4),
                               ssd[h, pp, :, h], ALU.add).then_inc(S["ns_sum"], 1)
                for g in range(2):
                    w("ns_sum", 8 * i + 4 * g + 4)
                    wb = wcum[:, gs[g], bass.ds(4 * i + NCH, 4)].rearrange("p t (b c) -> p t b c", c=1).to_broadcast([P, 4, 4, 64])
                    tt(ns[:, gs[g], :, :], ns[:, gs[g], :, :], wb, ALU.mult).then_inc(S["s_new"], 1)
                for g in range(2):
                    w("y_ready", u0 + g + 1)
                    w("ys_in", 2 * i + g + 1)
                    tt(ar[:, gs[g], 1, col], four(bank(g, 1)[:, 0:256]), sd[:, gs[g], 0:64], ALU.add)\
                        .then_inc(S["y_in"], 1)

        n_bufs = (sq, std, rstd, xnf)

        @block.sync
        def _(sp):
            sp.dma_start(xin[:], io["x"]).then_inc(S["x_in"], 16)
            sp.dma_start(cst[:], io["consts"]).then_inc(S["consts_in"], 16)
            sp.dma_start(vec[:], io["vecs"]).then_inc(S["consts_in"], 16)
            load_slots(sp, 0, 2)
            sp.dma_start(shin[:], io["shift_in"]).then_inc(S["consts_in"], 16)
            sp.dma_start(wmask[:], io["wmask"]).then_inc(S["consts_in"], 16)
            load_slots(sp, 2, 4)
            sp.wait_ge(S["xn_ready"], DT)
            for j in range(CT):
                sp.dma_start(streams(up[:, j, :], BUF + SEQ, BUF + TS, 0, BUF), io["conv_in"][:, j, :, :])\
                    .then_inc(S["history_in"], 16)
            load_slots(sp, 4, SLOTS["conv"][0])
            sp.wait_ge(S["u_ready"], CT + 1)
            for s in range(2):
                sp.wait_ge(psum_free[s], CT + 1)
            sp.wait_ge(S["history_in"], 16 * CT)
            for j in range(CT):
                sp.dma_start(io["conv_p"][:, j, :], up[:, j, SEQ:SEQ + BUF]).then_inc(S["stored"], 16)
                sp.dma_start(io["conv_s"][:, j, :, :], streams(up[:, j, :], BUF + SEQ, BUF + TS, TS, BUF)).then_inc(S["stored"], 16)
            for s in range(2):
                sp.wait_ge(psum_free[s], SLOTS["gate"][0] // 2 + 1)
            sp.dma_start(io["shift_out"], shout[:]).then_inc(S["stored"], 16)
            load_slots(sp, SLOTS["conv"][0], SLOTS["orwkv"][0] + 2)
            sp.wait_ge(S["conv_done"], 1)
            sp.wait_ge(S["stored"], 16 * (2 * CT + 1))
            sp.dma_start(lw[:], io["lw"]).then_inc(S["lw_in"], 16)
            sp.dma_start(erow[:], io["erow"]).then_inc(S["lw_in"], 16)
            sp.dma_start(smask[:], io["smask"]).then_inc(S["lw_in"], 16)
            sp.wait_ge(S["staged"], 2 * NCH)
            for j in range(2):
                if j:
                    sp.wait_ge(S["pst_ready"], 2)
                    sp.wait_ge(S["s_new"], 2 + 2 * NCH + 2)
                sp.dma_start(ssd, io["ssd"][j]).then_inc(S["ss_in"], 16)
                if j == 0:
                    sp.wait_ge(S["s_new"], 2 + 2 * NCH)
                    for h in (EVEN, ODD):
                        sp.dma_start(io["wkv_p"][h], sd[h, :, h]).then_inc(S["stored"], 16)
                sp.wait_ge(S["s_new"], 2 + 2 * NCH + 2 * j + 2)
                sp.dma_start(io["wkv_s"][j], ns).then_inc(S["ns_out"], 16)
            sp.wait_ge(S["ns_out"], 48)
            sp.wait_ge(S["y_in"], 2 + 2 * NCH + 4)
            sp.wait_ge(S["stored"], 16 * (2 * CT + 3))
            sp.dma_start(erow2[:], io["erow"]).then_inc(S["gup_in"], 16)
            sp.dma_start(gup[:], io["gup"]).then_inc(S["gup_in"], 16)
            sp.dma_start(m1t[:], io["m1"].rearrange("t p n -> p t n")).then_inc(S["mt_in"], 16)
            sp.dma_start(t2t[:], io["g2"].rearrange("t p n -> p t n")).then_inc(S["mt_in"], 16)
            load_slots(sp, SLOTS["orwkv"][0] + 2, SLOTS["orwkv"][0] + 8)
            sp.wait_ge(S["post_dve"], 5 * DT)
            sp.dma_start(ht[:], io["x"]).then_inc(S["res_in"], 16)
            load_slots(sp, SLOTS["out"][0], SLOTS["out"][0] + 2)
            sp.wait_ge(S["mg_ready"], DT)
            sp.dma_start(memt[:], io["mem"]).then_inc(S["mem_in"], 16)
            load_slots(sp, SLOTS["out"][0] + 2, SLOTS["q"][0] + 2)
            sp.wait_ge(S["mk_in"], DT)
            sp.dma_start(io["mk"], mkt[:]).then_inc(S["all_stored"], 16)
            sp.wait_ge(S["mvt_in"], DT)
            sp.dma_start(io["mv"], mvt[:]).then_inc(S["all_stored"], 16)
            load_slots(sp, SLOTS["q"][0] + 2, SLOTS["ox"][0] + 2)
            sp.wait_ge(S["q_in"], DT)
            sp.dma_start(xmask[:], io["xmask"]).then_inc(S["xm_in"], 16)
            for p in range(4):
                if p:
                    sp.wait_ge(S["kc_used"], p)
                sp.dma_start(kc[:], io["kc"][p]).then_inc(S["kc_in"], 16)
                if p:
                    sp.wait_ge(S["vc_used"], p)
                sp.dma_start(vc[:], io["vc"][p]).then_inc(S["vc_in"], 16)
            load_slots(sp, SLOTS["ox"][0] + 2, NSLOT)
            for k in range(DT):
                sp.wait_ge(S["y_done"], k + 1)
                sp.dma_start(io["y"][:, k, :], ht[:, k, :]).then_inc(S["all_stored"], 16)
            sp.wait_ge(S["all_stored"], 16 * (2 + DT))

        @block.scalar
        def _(act):
            act.wait_ge(S["consts_in"], 64)
            act.wait_ge(S["x_in"], 16)
            hi_part(act, 0, 0, first=True)
            norm_act(act, 0, lambda k: xin[:, k, :], xnh, n_bufs)
            n0, cnt = SLOTS["glu"]
            with act.Fori(0, cnt // 2) as i:
                hi_part(act, i, n0 + 1)
                hi_part(act, i, n0 + 2)
                act.wait_ge(S["mm_done"], 2 * i + (n0 + 4))
                nc.scalar.activation(tmp[0][:, 0:NT], span(ps[1]), ACT.Tanh, scale=0.5).then_inc(S["glu_gate"], 1)
            n0 = SLOTS["rkv"][0]
            with act.Fori(0, SHT // 2) as i:
                for s in range(2):
                    hi_part(act, i, n0 + s + 1)
                    act.wait_ge(S["mm_done"], 2 * i + (n0 + s + 3))
                    act.wait_ge(S["pr_free"], 2 * i + (s + 1))
                    nc.scalar.activation(pr[s][:, 1:1 + SEQ], ps[s][:, CUT:CUT + SEQ], ACT.Copy).then_inc(S["pr_ready"], 1)
                    nc.scalar.activation(streams(pr[s], 1 + SEQ, 1 + TS, 1, TS), by_stream(ps[s][:, CUT + SEQ:CUT + NT]),
                                         ACT.Copy).then_inc(S["pr_ready"], 1)
            n0 = SLOTS["gate"][0]
            act.wait_ge(S["pr_free"], 2 + SHT)
            with act.Fori(0, 4) as i:
                for s in range(2):
                    hi_part(act, i, n0 + s + 1)
                    act.wait_ge(S["mm_done"], 2 * i + (n0 + s + 3))
                    nc.scalar.activation(row(ar[:, bass.ds(2 * i + s, 1), 0, :]), span(ps[s]),
                                         ACT.Tanh, scale=0.5).then_inc(psum_free[s], 1)

            def rwkv_gate(i, first):
                for s in range(2):
                    hi_part(act, i, n0 + 8 + s + 1)
                    act.wait_ge(S["mm_done"], 2 * i + (n0 + 8 + s + 3))
                    if not first:
                        act.wait_ge(g2_out[s], 16 * i)
                    nc.scalar.activation(tmp[s][:, 0:NT], span(ps[s]), ACT.Tanh, scale=0.5).then_inc(psum_free[s], 1)

            rwkv_gate(0, True)
            with act.Fori(1, 4) as i:
                rwkv_gate(i, False)
            nc.scalar.activation(lora[0:64, :], lora[0:64, :], ACT.Tanh).then_inc(S["lora_tanh"], 1)
            nc.scalar.activation(sgd[:], sgd[:], ACT.Tanh, scale=0.5).then_inc(S["lora_tanh"], 1)
            act.wait_ge(g2_out[0], 64)
            act.wait_ge(g2_out[1], 64)
            for j in range(CT):
                act.wait_ge(S["centred"], j + 1)
                if j >= 2:
                    act.wait_ge(S["square_summed"], j - 1)
                nc.scalar.activation(tmp[j % 2][:, 0:NT], acc[:, j, :], ACT.Square).then_inc(S["square_ready"], 1)
            act.wait_ge(S["var_ready"], 1)
            nc.scalar.activation(pr[0][:, 0:NT], span(ps[2]), ACT.Sqrt, bias=eps(1)).then_inc(S["dev_ready"], 1)
            for j in range(CT):
                act.wait_ge(S["cn_ready"], 2 * j + 2)
                if j >= 2:
                    act.wait_ge(S["cs_ready"], j - 1)
                nc.scalar.activation(tmp[j % 2][:, 0:NT], acc[:, j, :], ACT.Tanh).then_inc(S["ct_ready"], 1)
            for j in range(CT):
                act.wait_ge(S["cs_ready"], j + 1)
                nc.scalar.activation(ch[:, j, :], acc[:, j, :], ACT.Copy).then_inc(S["ch_ready"], 1)
            n0 = SLOTS["conv"][0]
            with act.Fori(0, 4) as i:
                for s in range(2):
                    hi_part(act, i, n0 + s + 1)
            act.wait_ge(m1_out[0], 64)
            act.wait_ge(m1_out[1], 64)
            act.wait_ge(S["lw_in"], 48)
            for j in range(DT):
                s = j % 2
                if j >= 2:
                    act.wait_ge(S["square_summed"], j - 1 + 3)
                nc.scalar.activation(p_kk[s][:], kt[:, j, :], ACT.Square, scale=v1("k_k", j)).then_inc(S["square_ready"], 1)
            act.wait_ge(S["var_ready"], 2)
            nc.scalar.activation(rn[:], span(ps[3])[0:16, :], ACT.Sqrt).then_inc(S["dev_ready"], 1)

            def low_rank(j):
                s = j % 2
                act.wait_ge(S["z_ready"], j + 1)
                if j >= 2:
                    act.wait_ge(S["prep_dve"], 10 * (j - 2) + 7)
                nc.scalar.activation(p_l[s][:], span(ps[0]), ACT.Tanh, scale=0.5, bias=par[:, j:j + 1]).then_inc(S["tz_ready"], 1)
                nc.scalar.activation(p_ta[s][:], span(ps[1]), ACT.Tanh, scale=0.5, bias=par[:, 8 + j:9 + j]).then_inc(S["tz_ready"], 1)

            act.wait_ge(S["params"], 4)
            low_rank(0)
            for j in range(DT):
                s = j % 2
                if j + 1 < DT:
                    low_rank(j + 1)
                act.wait_ge(S["prep_dve"], 10 * j + 3)
                if j >= 2:
                    act.wait_ge(S["prep_pool"], 4 * (j - 2) + 4)
                nc.scalar.activation(p_e1[s][:], p_L[s][:], ACT.Exp, scale=-DECAY / 2).then_inc(S["e_ready"], 1)
                nc.scalar.activation(p_L[s][:], p_L[s][:], ACT.Exp, scale=DECAY / 2).then_inc(S["e_ready"], 1)
                nc.scalar.activation(p_m[s][:], p_m[s][:], ACT.Exp, scale=-DECAY / 2).then_inc(S["e_ready"], 1)
            act.wait_ge(S["bonus_ready"], 1)
            nc.scalar.activation(bon[:], span(ps[3])[0:16, :], ACT.Copy).then_inc(S["bonus_in"], 1)
            act.wait_ge(S["prep_dve"], 10 * DT)
            act.wait_ge(S["prep_pool"], 4 * DT)
            act.wait_ge(S["zeroed"], 2)
            act.sem_inc(S["y_in"], 2)
            with act.Fori(0, NCH) as i:
                rec_act(act, True, i)
            act.wait_ge(S["stored"], 16 * (2 * CT + 3))
            with act.Fori(0, 2) as i:
                rec_act(act, False, i)
            act.wait_ge(S["ysum_ready"], 1)
            nc.scalar.activation(mean16[:], span(ps[3])[0:16, :], ACT.Copy, scale=1 / 64).then_inc(S["mean_in"], 1)
            for j in range(DT):
                act.wait_ge(S["centred"], j + 5)
                if j >= 2:
                    act.wait_ge(S["square_summed"], j - 1 + 10)
                nc.scalar.activation(psq[j % 2][:], ar[:, j, 1, :], ACT.Square).then_inc(S["square_ready"], 1)
            act.wait_ge(S["var_ready"], 3)
            nc.scalar.activation(mean16[:], span(ps[3])[0:16, :], ACT.Sqrt, scale=1 / 64, bias=eps(2)[0:16, :]).then_inc(S["dev_ready"], 1)
            for j in range(DT):
                act.wait_ge(S["po_ready"], j + 1)
                nc.scalar.activation(yoh[:, j, :], po[j % 2][:], ACT.Copy).then_inc(S["yh_ready"], 1)
            n0 = SLOTS["orwkv"][0]
            with act.Fori(0, 4) as i:
                for s in range(2):
                    hi_part(act, i, n0 + s + 1)
                    act.wait_ge(S["mg_ready"], 2 * i + (s + 1))
                    nc.scalar.activation(tile_of(mgh, 2 * i + s), po[s][:], ACT.Copy).then_inc(S["mgh_ready"], 1)
            act.wait_ge(S["mem_in"], 16)
            norm_act(act, 1, lambda k: memt[:, k, :], memh, n2_bufs, NMEM)
            n0 = SLOTS["out"][0]
            with act.Fori(0, 4) as i:
                for s in range(2):
                    hi_part(act, i, n0 + s + 1)
            act.wait_ge(S["h_added"], DT)
            norm_act(act, 2, lambda k: ht[:, k, :], hnh, n2_bufs)
            for stage, dst, done in (("mk", mkt, S["mk_in"]), ("mv", mvt, S["mvt_in"])):
                n0 = SLOTS[stage][0]
                with act.Fori(0, 4) as i:
                    for s in range(2):
                        hi_part(act, i, n0 + s + 1)
                        act.wait_ge(S["mm_done"], 2 * i + (n0 + s + 3))
                        nc.scalar.activation(tile_of(dst, 2 * i + s), ps[s][:, 0:NMEM], ACT.Copy).then_inc(done, 1)
                        act.wait_ge(done, 2 * i + (s + 1))
                        act.sem_inc(psum_free[s], 1)
            n0 = SLOTS["q"][0]
            with act.Fori(0, 4) as i:
                for s in range(2):
                    hi_part(act, i, n0 + s + 1)
                    act.wait_ge(S["mm_done"], 2 * i + (n0 + s + 3))
                    nc.scalar.activation(tile_of(qt, 2 * i + s), span(ps[s]), ACT.Copy, scale=1 / 16).then_inc(S["q_in"], 1)
                    act.wait_ge(S["q_in"], 2 * i + (s + 1))
                    act.sem_inc(psum_free[s], 1)
            for m in range(2):
                act.wait_ge(S["mvx_ready"], m + 1)
                nc.scalar.activation(mv[:, m, :], ps[m][:, :], ACT.Copy).then_inc(S["mv_in"], 1)

            def softmax_in(i):
                s = i % 2
                act.wait_ge(S["mx_ready"], 2 * i + 2)
                if i >= 2:
                    act.wait_ge(S["ptp_ready"], i - 1)
                for h in range(XH):
                    nc.scalar.activation(pex[s][:, NMEM * h:NMEM * h + NMEM], ps[2 + s][:, NMEM * h:NMEM * h + NMEM], ACT.Exp,
                                         bias=nmx[:, s, h:h + 1], accum_out=sm[:, s, h:h + 1]).then_inc(S["ex_ready"], 1)

            softmax_in(0)
            for i in range(4):
                if i < 3:
                    softmax_in(i + 1)
                act.wait_ge(S["ptp_ready"], i + 1)
                nc.scalar.activation(pt[:, :, :, P * i:P * i + P].rearrange("p m h t -> p (m h) t"),
                                     ps[i % 2][:, :].rearrange("p (a t) -> p a t", a=8), ACT.Copy).then_inc(S["pt_in"], 1)
            for c in range(DT):
                act.wait_ge(S["o_ready"], c + 1)
                nc.scalar.activation(oth[:, c, 0:SEQ], ps[c % 2][:, 0:SEQ], ACT.Copy).then_inc(S["oh_ready"], 1)
            for p in range(4):
                act.wait_ge(S["mx_ready"], 3 * p + 11)
                nc.scalar.activation(pex[0][:, 0:2 * NMEM], pex[1][:, 0:2 * NMEM], ACT.Exp, bias=nmx[:, 0, 0:1],
                                     accum_out=sm[:, 0, 0:1]).then_inc(S["ex_ready"], 1)
                act.wait_ge(S["ptp_ready"], p + 5)
                nc.scalar.activation(pt[:, 0, 0, :], ps[3][:, 0:SEQ], ACT.Copy).then_inc(S["pt_in"], 1)
                act.wait_ge(S["o_ready"], p + 9)
                nc.scalar.activation(oth[:, :, SEQ + 32 * p:SEQ + 32 * p + 32], ps[0][:, 0:256].rearrange("p (c t) -> p c t", c=8),
                                     ACT.Copy).then_inc(S["oh_ready"], 1)
            n0 = SLOTS["ox"][0]
            with act.Fori(0, 4) as i:
                for s in range(2):
                    hi_part(act, i, n0 + s + 1)
            act.wait_ge(S["h_added"], 2 * DT)
            norm_act(act, 3, lambda k: ht[:, k, :], fnh, n3_bufs)
            done = 0
            for c, n in enumerate(THIRDS):
                n0 = SLOTS[f"f{c}"][0]
                with act.Fori(0, n) as i:
                    hi_part(act, i, n0 + 1)
                    act.wait_ge(S["mm_done"], 2 * i + (n0 + 3))
                    nc.scalar.activation(fth[:], span(ps[0]), ACT.Tanh, scale=0.5).then_inc(S["ft_ready"], 1)
                    hi_part(act, i, n0 + 2)
                    act.wait_ge(S["fh_ready"], i + (done + 1))
                    nc.scalar.activation(tile_of(hdh, i), fhd[:], ACT.Copy).then_inc(S["fhh_ready"], 1)
                done += n
                n0 = SLOTS[f"d{c}"][0]
                last = c == len(THIRDS) - 1
                with act.Fori(0, 3 if last else 4) as i:
                    for s in range(2):
                        hi_part(act, i, n0 + s + 1)
                if last:
                    hi_part(act, 3, n0 + 1)
            act.wait_ge(S["h_added"], 5 * DT)
            norm_act(act, 4, lambda k: ht[:, k, :], None, n3_bufs)

        @block.vector
        def _(dve):
            dve.wait_ge(S["consts_in"], 64)
            a = VCOL["w0"]
            nc.vector.tensor_scalar(par[:, 0:16], vec[:, a:a + 16], 0.5, None, ALU.mult).then_inc(S["params"], 1)
            a = VCOL["k_a"]
            nc.vector.tensor_scalar(par[:, 16:24], vec[:, a:a + 8], 0.5, None, ALU.mult).then_inc(S["params"], 1)
            nc.vector.tensor_scalar(par[:, 24:32], vec[:, a:a + 8], -0.5, 1.0, ALU.mult, ALU.add).then_inc(S["params"], 1)
            a = VCOL["ln_conv_g"]
            nc.vector.tensor_scalar(par[:, 32:40], vec[:, a:a + 8], 0.5, None, ALU.mult).then_inc(S["params"], 1)
            norm_dve(dve, 0, lambda k: xin[:, k, :], "g_norm_mix", n_bufs)
            dve.sem_inc(S["u_ready"], 1)
            dve.wait_ge(S["xn_ready"], DT)
            nc.vector.memset(up[:, :, 0:BUF], 0.0).then_inc(S["up_zero"], 1)
            with dve.Fori(0, CT) as i:
                dve.wait_ge(S["glu_gate"], i + 1)
                dve.wait_ge(S["u_ready"], i + 1)
                nc.vector.tensor_scalar(tmp[1][:, 0:NT], tmp[0][:, 0:NT], 0.5, 0.5, ALU.mult, ALU.add).then_inc(psum_free[1], 1)
                dve.wait_ge(psum_free[1], i + 2)
                nc.vector.tensor_tensor(row(up[:, bass.ds(i, 1), BUF:BUF + SEQ]), tmp[1][:, 0:SEQ], ps[0][:, CUT:CUT + SEQ],
                                        ALU.mult).then_inc(S["u_ready"], 1)
                nc.vector.tensor_tensor(streams(row(up[:, bass.ds(i, 1), :]), BUF + SEQ, BUF + TS, BUF, TS),
                                        by_stream(tmp[1][:, SEQ:NT]), by_stream(ps[0][:, CUT + SEQ:CUT + NT]), ALU.mult)\
                    .then_inc(psum_free[0], 1)
            dve.sem_inc(S["pr_free"], 2)
            for t0, dest in ((0, lambda k: row(ar[:, bass.ds(k, 1), 1, :])), (8, lambda k: row(kt[:, bass.ds(k, 1), :])),
                             (16, lambda k: row(vt[:, bass.ds(k, 1), :])), (24, None)):
                with (dve.Fori(0, 4) if dest else nullcontext(0)) as i:
                    for s in range(2):
                        out = dest(2 * i + s) if dest else (lora, sgd)[s][:]
                        t = t0 + s
                        dve.wait_ge(S["pad_ready"], 2 * i + (t + 1))
                        dve.wait_ge(S["pr_ready"], 4 * i + (2 * t + 2))
                        nc.vector.tensor_tensor(tmp[s][:, 0:PW - 1], pr[s][:, 0:PW - 1], pr[s][:, 1:PW], ALU.subtract)\
                            .then_inc(S["diff_ready"], 1)
                        dve.wait_ge(S["diff_ready"], 2 * i + (t + 1))
                        mu = v1("mu_shift", 2 * i + t)
                        nc.vector.scalar_tensor_tensor(out=out[:, 0:SEQ], in0=tmp[s][:, 0:SEQ], scalar=mu, in1=pr[s][:, 1:1 + SEQ],
                                                       op0=ALU.mult, op1=ALU.add)
                        nc.vector.scalar_tensor_tensor(out=by_stream(out[:, SEQ:NT]), in0=streams(tmp[s], 1 + SEQ, 1 + TS, 0, TS), scalar=mu,
                                                       in1=streams(pr[s], 1 + SEQ, 1 + TS, 1, TS),
                                                       op0=ALU.mult, op1=ALU.add).then_inc(S["pr_free"], 1)
            dve.wait_ge(S["history_in"], 16 * CT)
            dve.wait_ge(psum_free[0], 1 + CT)
            dve.wait_ge(S["pr_free"], 2 + SHT)

            def windows(j, tap):
                u = up[:, j, :]
                if isinstance(tap, int):
                    return u[:, tap:tap + SEQ], streams(u, BUF + SEQ, BUF + TS, tap, TS)
                return u[:, bass.ds(tap, SEQ)], by_seg(u, tap)

            def by_seg(u, tap):
                return u[:, BUF + SEQ:UW].rearrange("p (b c) -> p b c", b=NS)[:, :, bass.ds(tap, TS)]

            for j in range(CT):
                for n, (src, dst) in enumerate(zip(windows(j, 0), (acc[:, j, 0:SEQ], by_stream(acc[:, j, SEQ:NT])))):
                    nc.vector.tensor_scalar(dst, src, v1("w_dw", TAPS * j), v1("b_dw", j), ALU.mult, ALU.add)\
                        .then_inc(S["conv_step"], 1)
            with dve.Fori(1, TAPS) as tap:
                for j in range(CT):
                    for n, (src, dst) in enumerate(zip(windows(j, tap), (acc[:, j, 0:SEQ], by_stream(acc[:, j, SEQ:NT])))):
                        dve.wait_ge(S["conv_step"], 8 * tap + (2 * j + n - 7))
                        nc.vector.scalar_tensor_tensor(out=dst, in0=src, scalar=v1("w_dw", tap + TAPS * j), in1=dst,
                                                       op0=ALU.mult, op1=ALU.add).then_inc(S["conv_step"], 1)
            dve.wait_ge(S["conv_step"], 8 * TAPS)
            dve.sem_inc(S["conv_done"], 1)
            dve.wait_ge(S["lora_tanh"], 2)
            nc.vector.tensor_scalar(sgd[:], sgd[:], 0.5, 0.5, ALU.mult, ALU.add).then_inc(S["sig_ready"], 1)
            dve.wait_ge(S["cmean_ready"], 1)
            for j in range(CT):
                nc.vector.tensor_tensor(acc[:, j, :], acc[:, j, :], span(ps[3]), ALU.subtract).then_inc(S["centred"], 1)
            dve.wait_ge(S["dev_ready"], 1)
            nc.vector.reciprocal(pr[1][:, 0:NT], pr[0][:, 0:NT]).then_inc(S["inv_ready"], 1)
            dve.wait_ge(S["inv_ready"], 1)
            for j in range(CT):
                nc.vector.tensor_tensor(acc[:, j, :], acc[:, j, :], pr[1][:, 0:NT], ALU.mult).then_inc(S["cn_ready"], 1)
                dve.wait_ge(S["cn_ready"], 2 * j + 1)
                nc.vector.tensor_scalar(acc[:, j, :], acc[:, j, :], par[:, 32 + j:33 + j], par[:, 36 + j:37 + j], ALU.mult, ALU.add)\
                    .then_inc(S["cn_ready"], 1)
            for j in range(CT):
                dve.wait_ge(S["ct_ready"], j + 1)
                nc.vector.scalar_tensor_tensor(out=acc[:, j, :], in0=tmp[j % 2][:, 0:NT], scalar=1.0, in1=acc[:, j, :],
                                               op0=ALU.add, op1=ALU.mult).then_inc(S["cs_ready"], 1)
            n0 = SLOTS["conv"][0]

            def gated_conv(i, first):
                for s in range(2):
                    dve.wait_ge(S["mm_done"], 2 * i + (n0 + s + 3))
                    if not first:
                        dve.wait_ge(m1_out[s], 16 * i)
                    nc.vector.scalar_tensor_tensor(out=pr[s][:, 0:NT], in0=tile_of(ar, 2 * i + s, 0), scalar=1.0,
                                                   in1=span(ps[s]), op0=ALU.add, op1=ALU.mult).then_inc(psum_free[s], 1)

            gated_conv(0, True)
            with dve.Fori(1, 4) as i:
                gated_conv(i, False)
            dve.wait_ge(S["dev_ready"], 2)
            nc.vector.tensor_scalar(rn[:], rn[:], 1e-12, None, ALU.max).then_inc(S["rn_ready"], 1)
            dve.wait_ge(S["rn_ready"], 1)
            nc.vector.reciprocal(rn[:], rn[:]).then_inc(S["rn_ready"], 1)
            for j in range(DT):
                s = j % 2

                def made(n):
                    dve.wait_ge(S["prep_dve"], 10 * j + n)

                def done(ins):
                    ins.then_inc(S["prep_dve"], 1)

                dve.wait_ge(S["tz_ready"], 2 * j + 2)
                done(nc.vector.tensor_scalar(p_l[s][:], p_l[s][:], 1.0, None, ALU.add))
                if j >= 2:
                    dve.wait_ge(S["prep_pool"], 4 * (j - 2) + 4)
                made(1)
                done(nc.vector.tensor_tensor_scan(p_L[s][:], smask[:], p_l[s][:], 0.0, ALU.mult, ALU.add))
                made(2)
                done(nc.vector.tensor_tensor(p_m[s][:], p_L[s][:], p_l[s][:], ALU.subtract))
                dve.wait_ge(S["rnb_ready"], j + 1)
                done(nc.vector.scalar_tensor_tensor(out=p_kk[s][:], in0=kt[:, j, :], scalar=v1("k_k", j), in1=span(ps[2]),
                                                    op0=ALU.mult, op1=ALU.mult))
                done(nc.vector.tensor_scalar(p_kf[s][:], p_ta[s][:], par[:, 16 + j:17 + j], par[:, 24 + j:25 + j],
                                             ALU.mult, ALU.add))
                made(5)
                done(nc.vector.tensor_tensor(p_kf[s][:], p_kf[s][:], kt[:, j, :], ALU.mult))
                done(nc.vector.scalar_tensor_tensor(out=p_b2[s][:], in0=p_ta[s][:], scalar=1.0, in1=p_kk[s][:],
                                                    op0=ALU.add, op1=ALU.mult))
                made(6)
                if j >= 2:
                    dve.wait_ge(S["bonus_used"], j - 1)
                done(nc.vector.scalar_tensor_tensor(out=p_rk[s][:], in0=ar[:, j, 1, :], scalar=v1("r_k", j), in1=p_kf[s][:],
                                                    op0=ALU.mult, op1=ALU.mult))
                dve.wait_ge(S["e_ready"], 3 * j + 3)
                made(7)
                done(nc.vector.scalar_tensor_tensor(out=bt[:, j, :], in0=p_b2[s][:], scalar=0.5, in1=p_L[s][:],
                                                    op0=ALU.mult, op1=ALU.mult))
                done(nc.vector.scalar_tensor_tensor(out=ar[:, j, 0, :], in0=p_kk[s][:], scalar=-1.0, in1=p_m[s][:],
                                                    op0=ALU.mult, op1=ALU.mult))
            dve.wait_ge(S["prep_pool"], 4 * DT)
            dve.wait_ge(S["prep_dve"], 10 * DT)
            dve.wait_ge(S["bonus_ready"], 1)
            for b in (atd, akd):
                last = nc.vector.memset(b[:], 0.0)
            last.then_inc(S["zeroed"], 1)
            dve.wait_ge(S["zeroed"], 2)
            dve.sem_inc(S["s_new"], 2)
            with dve.Fori(0, NCH) as i:
                rec_dve(dve, True, i)
            with dve.Fori(0, 2) as i:
                rec_dve(dve, False, i)
            for j in range(DT):
                dve.wait_ge(S["mb_ready"], j + 1)
                nc.vector.tensor_tensor(ar[:, j, 1, :], ar[:, j, 1, :], span(ps[j % 2]), ALU.subtract).then_inc(S["centred"], 1)
            dve.wait_ge(S["dev_ready"], 3)
            nc.vector.reciprocal(rstd16[:], mean16[:]).then_inc(S["inv_ready"], 1)
            dve.wait_ge(S["centred"], DT + 4)
            for j in range(DT):
                y = ar[:, j, 1, :]

                def made(n):
                    dve.wait_ge(S["post_dve"], 5 * j + n)

                dve.wait_ge(S["g3_ready"], j + 1)
                nc.vector.tensor_tensor(y, y, span(ps[0]), ALU.mult).then_inc(S["post_dve"], 1)
                if j:
                    made(0)
                nc.vector.tensor_tensor(bv[:], vt[:, j, :], span(ps[1]), ALU.mult).then_inc(S["post_dve"], 1)
                made(1)
                nc.vector.tensor_scalar(y, y, v1("ln_x_g", j), v1("ln_x_b", j), ALU.mult, ALU.add).then_inc(S["post_dve"], 1)
                made(3)
                nc.vector.tensor_tensor(y, y, bv[:], ALU.add).then_inc(S["post_dve"], 1)
                made(4)
                if j >= 2:
                    dve.wait_ge(S["yl_ready"], j - 1)
                nc.vector.tensor_tensor(po[j % 2][:], y, span(ps[2]), ALU.mult).then_inc(S["po_ready"], 1)
                dve.sem_inc(S["post_dve"], 1)
            dve.wait_ge(S["po_ready"], DT)
            dve.wait_ge(S["mt_in"], 32)
            dve.wait_ge(S["yl_ready"], DT)
            dve.sem_inc(S["mgl_ready"], 2)
            n0 = SLOTS["orwkv"][0]
            with dve.Fori(0, 4) as i:
                for s in range(2):
                    dve.wait_ge(S["mm_done"], 2 * i + (n0 + s + 3))
                    dve.wait_ge(S["mgl_ready"], 2 * i + (s + 1))
                    nc.vector.scalar_tensor_tensor(out=po[s][:], in0=tile_of(t2t, 2 * i + s), scalar=1.0, in1=span(ps[s]),
                                                   op0=ALU.add, op1=ALU.mult).then_inc(psum_free[s], 1)
                    dve.wait_ge(psum_free[s], i + (n0 // 2 + 2))
                    nc.vector.tensor_tensor(po[s][:], po[s][:], tile_of(m1t, 2 * i + s), ALU.add).then_inc(S["merge_dve"], 1)
                    dve.wait_ge(S["merge_dve"], 2 * i + (s + 1))
                    nc.vector.tensor_scalar(po[s][:], po[s][:], 0.5, None, ALU.mult).then_inc(S["mg_ready"], 1)
            norm_dve(dve, 1, lambda k: memt[:, k, :], "g_mem", n2_bufs, NMEM)

            def add_residual(stage):
                n0 = SLOTS[stage][0]
                with dve.Fori(0, 4) as i:
                    for s in range(2):
                        dve.wait_ge(S["mm_done"], 2 * i + (n0 + s + 3))
                        nc.vector.tensor_tensor(tile_of(ht, 2 * i + s), tile_of(ht, 2 * i + s), span(ps[s]), ALU.add)\
                            .then_inc(S["h_added"], 1)
                        dve.wait_ge(S["h_added"], 2 * i + (s + 1 + added[0]))
                        dve.sem_inc(psum_free[s], 1)
                added[0] += DT

            added = [0]
            dve.wait_ge(S["res_in"], 16)
            add_residual("out")
            norm_dve(dve, 2, lambda k: ht[:, k, :], "g_norm_x", n2_bufs)
            for i in range(4):
                s = i % 2
                dve.wait_ge(S["sp_ready"], i + 1)
                nc.vector.tensor_reduce(out=mx[:, s, :], in_=ps[2 + s][:, :].rearrange("p (h m) -> p h m", h=XH), op=ALU.max, axis=AX.X)\
                    .then_inc(S["mx_ready"], 1)
                dve.wait_ge(S["mx_ready"], 2 * i + 1)
                nc.vector.tensor_scalar(nmx[:, s, :], mx[:, s, :], -1.0, None, ALU.mult).then_inc(S["mx_ready"], 1)
                dve.wait_ge(S["ex_ready"], XH * i + XH)
                nc.vector.reciprocal(rs[:, s, :], sm[:, s, :]).then_inc(S["pn_ready"], 1)
                dve.wait_ge(S["pn_ready"], 2 * i + 1)
                v = pex[s][:, :].rearrange("p (h m) -> p h m", h=XH)
                nc.vector.tensor_tensor(v, v, rs[:, s, :].rearrange("p (h m) -> p h m", m=1).to_broadcast([P, XH, NMEM]), ALU.mult)\
                    .then_inc(S["pn_ready"], 1)
            for c in range(DT):
                dve.wait_ge(S["oh_ready"], c + 1)
                nc.vector.tensor_tensor(otl[:, c, 0:SEQ], ps[c % 2][:, 0:SEQ], oth[:, c, 0:SEQ].bitcast(F32), ALU.subtract)\
                    .then_inc(S["ol_ready"], 1)
            dve.wait_ge(S["xm_in"], 16)
            for p in range(4):
                dve.wait_ge(S["sp_ready"], p + 5)
                nc.vector.tensor_tensor(pex[1][:, 0:2 * NMEM], ps[2][:, 0:2 * NMEM], xmask[:], ALU.add).then_inc(S["mx_ready"], 1)
                dve.wait_ge(S["mx_ready"], 3 * p + 9)
                nc.vector.tensor_reduce(out=mx[:, 0, 0:1], in_=pex[1][:, 0:2 * NMEM], op=ALU.max, axis=AX.X).then_inc(S["mx_ready"], 1)
                dve.wait_ge(S["mx_ready"], 3 * p + 10)
                nc.vector.tensor_scalar(nmx[:, 0, 0:1], mx[:, 0, 0:1], -1.0, None, ALU.mult).then_inc(S["mx_ready"], 1)
                dve.wait_ge(S["ex_ready"], p + 17)
                nc.vector.reciprocal(rs[:, 0, 0:1], sm[:, 0, 0:1]).then_inc(S["pn_ready"], 1)
                dve.wait_ge(S["pn_ready"], 2 * p + 9)
                nc.vector.tensor_scalar(pex[0][:, 0:2 * NMEM], pex[0][:, 0:2 * NMEM], rs[:, 0, 0:1], None, ALU.mult)\
                    .then_inc(S["pn_ready"], 1)
                dve.wait_ge(S["oh_ready"], p + 9)
                w32 = slice(SEQ + 32 * p, SEQ + 32 * p + 32)
                nc.vector.tensor_tensor(otl[:, :, w32], ps[0][:, 0:256].rearrange("p (c t) -> p c t", c=8), oth[:, :, w32].bitcast(F32),
                                        ALU.subtract).then_inc(S["ol_ready"], 1)
            add_residual("ox")
            norm_dve(dve, 3, lambda k: ht[:, k, :], "g_norm_ffn", n3_bufs)
            done = 0
            for c, n in enumerate(THIRDS):
                n0 = SLOTS[f"f{c}"][0]
                with dve.Fori(0, n) as i:
                    dve.wait_ge(S["ft_ready"], i + (done + 1))
                    nc.vector.scalar_tensor_tensor(out=fsg[:], in0=fth[:], scalar=1.0, in1=span(ps[0]), op0=ALU.add, op1=ALU.mult)\
                        .then_inc(psum_free[0], 1)
                    dve.wait_ge(psum_free[0], i + (n0 // 2 + 2))
                    dve.wait_ge(S["mm_done"], 2 * i + (n0 + 4))
                    dve.wait_ge(S["fhl_ready"], i + (done + 1))
                    nc.vector.scalar_tensor_tensor(out=fhd[:], in0=fsg[:], scalar=0.5, in1=span(ps[1]), op0=ALU.mult, op1=ALU.mult)\
                        .then_inc(S["fh_ready"], 1)
                    dve.wait_ge(S["fh_ready"], i + (done + 1))
                    dve.sem_inc(psum_free[1], 1)
                done += n
                add_residual(f"d{c}")
            dve.wait_ge(S["std_ready"], 5)
            nc.vector.reciprocal(n3_bufs[2][:], n3_bufs[1][:]).then_inc(S["rstd_ready"], 1)
            dve.wait_ge(S["rstd_ready"], 5)
            for k in range(DT):
                nc.vector.scalar_tensor_tensor(out=ht[:, k, :], in0=ht[:, k, :], scalar=v1("g_norm_final", k), in1=n3_bufs[2][:],
                                               op0=ALU.mult, op1=ALU.mult).then_inc(S["y_done"], 1)

        @block.gpsimd
        def _(pool):
            for s in range(2):
                nc.gpsimd.memset(pr[s][:, 0:1], 0.0).then_inc(S["pr_zero"], 1)
            pool.sem_inc(S["ns_out"], 16)
            lo_part(pool, 0, 0)
            norm_pool(pool, 0, xnh, xnl, n_bufs)
            with pool.Fori(0, CT) as i:
                lo_part(pool, i, 1)
                lo_part(pool, i, 2)
            n0 = SLOTS["rkv"][0]
            with pool.Fori(0, SHT // 2) as i:
                for s in range(2):
                    await_(pool, S["pr_free"], 2 * i + (s + 1))
                    nc.gpsimd.tensor_copy(streams(pr[s], 1 + SEQ, 1 + TS, 0, 1),
                                          shin[:, bass.ds(2 * i + s, 1), :].rearrange("p a (b c) -> p (a b) c", c=1))\
                        .then_inc(S["pad_ready"], 1)
                    lo_part(pool, i, n0 + s + 1)
                    await_(pool, S["pr_ready"], 4 * i + (2 * s + 2))
                    nc.gpsimd.tensor_copy(row(shout[:, bass.ds(2 * i + s, 1), 0:1]), pr[s][:, SEQ:SEQ + 1]).then_inc(S["shift_half"], 1)
                    nc.gpsimd.tensor_copy(shout[:, bass.ds(2 * i + s, 1), 1:1 + NS].rearrange("p a (b c) -> p (a b) c", c=1),
                                          streams(pr[s], 1 + SEQ, 1 + TS, TS, 1)).then_inc(psum_free[s], 1)
            n0 = SLOTS["gate"][0]
            with pool.Fori(0, 4) as i:
                for s in range(2):
                    lo_part(pool, i, n0 + s + 1)
            with pool.Fori(0, 4) as i:
                for s in range(2):
                    lo_part(pool, i, n0 + 8 + s + 1)
                    await_(pool, psum_free[s], i + (n0 // 2 + 4 + 2))
                    pool.dma_start(io["g2"][bass.ds(2 * i + s, 1), :, :].rearrange("a p n -> (a p) n"), tmp[s][:, 0:NT])\
                        .then_inc(g2_out[s], 16)
            for j in range(CT):
                await_(pool, S["ch_ready"], j + 1)
                nc.gpsimd.tensor_tensor(cl[:, j, :], acc[:, j, :], ch[:, j, :].bitcast(F32), ALU.subtract).then_inc(S["cl_ready"], 1)
            n0 = SLOTS["conv"][0]
            with pool.Fori(0, 4) as i:
                for s in range(2):
                    lo_part(pool, i, n0 + s + 1)
                    await_(pool, psum_free[s], i + (n0 // 2 + 2))
                    pool.dma_start(io["m1"][bass.ds(2 * i + s, 1), :, :].rearrange("a p n -> (a p) n"), pr[s][:, 0:NT])\
                        .then_inc(m1_out[s], 16)
            for j in range(DT):
                s = j % 2
                await_(pool, S["prep_dve"], 10 * j + 8)
                await_(pool, S["e_ready"], 3 * j + 3)
                nc.gpsimd.tensor_tensor(kt[:, j, :], p_kf[s][:], p_L[s][:], ALU.mult).then_inc(S["prep_pool"], 1)
                nc.gpsimd.tensor_tensor(ar[:, j, 1, :], ar[:, j, 1, :], p_e1[s][:], ALU.mult).then_inc(S["prep_pool"], 1)
                nc.gpsimd.tensor_copy(wcum[:, j, 0:NCH], p_e1[s][:, C - 1:SEQ:C]).then_inc(S["prep_pool"], 1)
                await_(pool, S["prep_dve"], 10 * j + 9)
                nc.gpsimd.tensor_copy(wcum[:, j, NCH:NCH + NS], p_e1[s][:, SEQ + TS - 1:NT:TS]).then_inc(S["prep_pool"], 1)
            await_(pool, S["prep_dve"], 10 * DT)
            await_(pool, S["bonus_ready"], 1)
            await_(pool, S["prep_pool"], 4 * DT)
            for b in (bd, kd, ad, vd, sd):
                last = nc.gpsimd.memset(b[:], 0.0)
            last.then_inc(S["zeroed"], 1)
            await_(pool, S["zeroed"], 2)
            with pool.Fori(0, NCH) as i:
                rec_pool(pool, True, i)
            with pool.Fori(0, 2) as i:
                rec_pool(pool, False, i)
            for j in range(DT):
                await_(pool, S["yh_ready"], j + 1)
                nc.gpsimd.tensor_tensor(yol[:, j, :], po[j % 2][:], yoh[:, j, :].bitcast(F32), ALU.subtract).then_inc(S["yl_ready"], 1)
            n0 = SLOTS["orwkv"][0]
            with pool.Fori(0, 4) as i:
                for s in range(2):
                    lo_part(pool, i, n0 + s + 1)
                    await_(pool, S["mgh_ready"], 2 * i + (s + 1))
                    nc.gpsimd.tensor_tensor(tile_of(mgl, 2 * i + s), po[s][:], tile_of(mgh, 2 * i + s).bitcast(F32), ALU.subtract)\
                        .then_inc(S["mgl_ready"], 1)
            norm_pool(pool, 1, memh, meml, n2_bufs, NMEM)
            for stage in ("out", "mk", "mv", "q"):
                n0 = SLOTS[stage][0]
                if stage == "mk":
                    norm_pool(pool, 2, hnh, hnl, n2_bufs)
                with pool.Fori(0, 4) as i:
                    for s in range(2):
                        lo_part(pool, i, n0 + s + 1)
            n0 = SLOTS["ox"][0]
            with pool.Fori(0, 4) as i:
                for s in range(2):
                    lo_part(pool, i, n0 + s + 1)
            norm_pool(pool, 3, fnh, fnl, n3_bufs)
            pool.sem_inc(S["fhl_ready"], 1)
            done = 0
            for c, n in enumerate(THIRDS):
                n0 = SLOTS[f"f{c}"][0]
                with pool.Fori(0, n) as i:
                    lo_part(pool, i, n0 + 1)
                    lo_part(pool, i, n0 + 2)
                    await_(pool, S["fhh_ready"], i + (done + 1))
                    nc.gpsimd.tensor_tensor(tile_of(hdl, i), fhd[:], tile_of(hdh, i).bitcast(F32), ALU.subtract).then_inc(S["fhl_ready"], 1)
                done += n
                n0 = SLOTS[f"d{c}"][0]
                last = c == len(THIRDS) - 1
                with pool.Fori(0, 3 if last else 4) as i:
                    for s in range(2):
                        lo_part(pool, i, n0 + s + 1)
                if last:
                    lo_part(pool, 3, n0 + 1)

        @block.tensor
        def _(pe):
            pe.sem_inc(psum_free[0], 1)
            pe.sem_inc(psum_free[1], 1)
            pe.sem_inc(S["mm_done"], 2)
            pe.wait_ge(S["consts_in"], 64)
            norm_pe(pe, 0, n_bufs)
            pe.wait_ge(S["xl_ready"], DT)
            dense(pe, "glu", xnh, xnl)
            dense(pe, "rkv", xnh, xnl)
            dense(pe, "lora", xnh, xnl)
            dense(pe, "gate", xnh, xnl)
            pe.wait_ge(S["conv_done"], 1)
            for j in range(CT):
                for h in range(2):
                    last = nc.tensor.matmul(cut(ps[3], h), const("mean_c"), acc[:, j, h * HALF:(h + 1) * HALF],
                                            start=(j == 0), stop=(j == CT - 1))
            last.then_inc(S["cmean_ready"], 1)
            for j in range(CT):
                pe.wait_ge(S["square_ready"], j + 1)
                for h in range(2):
                    last = nc.tensor.matmul(cut(ps[2], h), const("mean_c"), tmp[j % 2][:, h * HALF:(h + 1) * HALF],
                                            start=(j == 0), stop=(j == CT - 1))
                last.then_inc(S["square_summed"] if j < CT - 1 else S["var_ready"], 1)
            pe.wait_ge(S["cl_ready"], CT)
            dense(pe, "conv", ch, cl, k_tiles=CT)
            def head_sum(j, src, done):
                for h in range(2):
                    last = nc.tensor.matmul(cut(ps[3], h)[0:16, :], const("head_sum")[:, 16 * j:16 * j + 16],
                                            src[:, h * HALF:(h + 1) * HALF], start=(j == 0), stop=(j == DT - 1))
                if done is not None:
                    last.then_inc(done, 1)

            for j in range(DT):
                pe.wait_ge(S["square_ready"], j + 5)
                head_sum(j, p_kk[j % 2], S["square_summed"] if j < DT - 1 else S["var_ready"])
            pe.wait_ge(S["rn_ready"], 2)
            pe.wait_ge(S["lora_tanh"], 2)
            pe.wait_ge(psum_free[0], SLOTS["orwkv"][0] // 2 + 1)
            pe.wait_ge(psum_free[1], SLOTS["orwkv"][0] // 2 + 1)
            pe.wait_ge(S["lw_in"], 48)
            for j in range(DT):
                if j:
                    pe.wait_ge(S["tz_ready"], 2 * j)
                cols = slice(P * j, P * j + P)
                for h in range(2):
                    nc.tensor.matmul(cut(ps[0], h), lw[0:64, cols], lora[0:64, h * HALF:(h + 1) * HALF], start=True, stop=True)
                for h in range(2):
                    last = nc.tensor.matmul(cut(ps[1], h), lw[64:128, cols], lora[64:128, h * HALF:(h + 1) * HALF], start=True, stop=True)
                last.then_inc(S["z_ready"], 1)
                if j:
                    pe.wait_ge(S["prep_dve"], 10 * (j - 1) + 4)
                for h in range(2):
                    last = nc.tensor.matmul(cut(ps[2], h), erow[:, cols], rn[:, h * HALF:(h + 1) * HALF], start=True, stop=True)
                last.then_inc(S["rnb_ready"], 1)
                if j:
                    pe.wait_ge(S["prep_dve"], 10 * (j - 1) + 8)
                    head_sum(j - 1, p_rk[(j - 1) % 2], S["bonus_used"])
            pe.wait_ge(S["prep_dve"], 10 * (DT - 1) + 8)
            head_sum(DT - 1, p_rk[(DT - 1) % 2], S["bonus_ready"])
            pe.wait_ge(S["bonus_in"], 1)
            pe.wait_ge(S["zeroed"], 2)
            pe.sem_inc(S["rhs_ready"], 2)
            pe.sem_inc(S["vd_ready"], 2)
            with pe.Fori(0, NCH) as i:
                rec_pe(pe, True, i)
            with pe.Fori(0, 2) as i:
                rec_pe(pe, False, i)
            pe.wait_ge(S["gup_in"], 32)
            pe.wait_ge(S["y_in"], 2 + 2 * NCH + 4)
            for j in range(DT):
                head_sum(j, ar[:, j, 1, :], S["ysum_ready"] if j == DT - 1 else None)
            pe.wait_ge(S["mean_in"], 1)
            for j in range(DT):
                if j >= 2:
                    pe.wait_ge(S["centred"], j - 1 + 4)
                for h in range(2):
                    last = nc.tensor.matmul(cut(ps[j % 2], h), erow2[:, P * j:P * j + P], mean16[:, h * HALF:(h + 1) * HALF], start=True, stop=True)
                last.then_inc(S["mb_ready"], 1)
            for j in range(DT):
                pe.wait_ge(S["square_ready"], j + 13)
                head_sum(j, psq[j % 2], S["square_summed"] if j < DT - 1 else S["var_ready"])
            pe.wait_ge(S["inv_ready"], 2)
            for j in range(DT):
                if j:
                    pe.wait_ge(S["po_ready"], j)
                cols = slice(P * j, P * j + P)
                for b, (w, src) in enumerate(((erow2[:, cols], rstd16), (erow2[:, cols], bon), (gup[:, cols], sgd))):
                    for h in range(2):
                        last = nc.tensor.matmul(cut(ps[b], h), w, src[:, h * HALF:(h + 1) * HALF], start=True, stop=True)
                last.then_inc(S["g3_ready"], 1)
            pe.wait_ge(S["po_ready"], DT)
            pe.wait_ge(S["yl_ready"], DT)
            dense(pe, "orwkv", yoh, yol)
            norm_pe(pe, 1, n2_bufs, NMEM)
            pe.wait_ge(S["mgl_ready"], 2 + DT)
            dense(pe, "out", mgh, mgl)
            norm_pe(pe, 2, n2_bufs)
            pe.wait_ge(S["xl_ready"], 2 * DT)
            dense(pe, "mk", memh, meml, n=NMEM)
            dense(pe, "mv", memh, meml, n=NMEM)
            pe.wait_ge(S["xl_ready"], 3 * DT)
            dense(pe, "q", hnh, hnl)
            for s in range(2):
                pe.wait_ge(psum_free[s], SLOTS["ox"][0] // 2 + 1)
            for m in range(2):
                for j in range(DT):
                    last = nc.tensor.transpose(ps[m][:, P * j:P * j + P], mvt[:, j, P * m:P * m + P], const("ident"))
                last.then_inc(S["mvx_ready"], 1)

            def scores(i):
                if i >= 2:
                    pe.wait_ge(S["ex_ready"], XH * (i - 1))
                for h in range(XH):
                    for k in range(2):
                        last = nc.tensor.matmul(ps[2 + i % 2][:, NMEM * h:NMEM * h + NMEM], qt[:, 2 * h + k, P * i:P * i + P],
                                                mkt[:, 2 * h + k, :], start=(k == 0), stop=(k == 1))
                last.then_inc(S["sp_ready"], 1)

            scores(0)
            scores(1)
            for i in range(4):
                pe.wait_ge(S["pn_ready"], 2 * i + 2)
                if i < 2:
                    pe.wait_ge(S["mv_in"], i + 1)
                else:
                    pe.wait_ge(S["pt_in"], i - 1)
                for m in range(2):
                    for h in range(XH):
                        a = XH * m + h
                        last = nc.tensor.transpose(ps[i % 2][:, P * a:P * a + P], pex[i % 2][:, NMEM * h + P * m:NMEM * h + P * m + P], const("ident"))
                last.then_inc(S["ptp_ready"], 1)
                if i + 2 < 4:
                    scores(i + 2)
            pe.wait_ge(S["pt_in"], 4)
            for c in range(DT):
                if c >= 2:
                    pe.wait_ge(S["ol_ready"], c - 1)
                for m in range(2):
                    last = nc.tensor.matmul(ps[c % 2][:, 0:SEQ], mv[:, m, P * c:P * c + P], pt[:, m, c // 2, :], start=(m == 0), stop=(m == 1))
                last.then_inc(S["o_ready"], 1)
            pe.wait_ge(S["ol_ready"], DT)
            for p in range(4):
                pe.wait_ge(S["kc_in"], 16 * p + 16)
                for h in range(XH):
                    for k in range(2):
                        last = nc.tensor.matmul(ps[2][32 * h:32 * h + 32, 0:2 * NMEM], qt[:, 2 * h + k, SEQ + 32 * p:SEQ + 32 * p + 32],
                                                kc[:, 2 * h + k, :], start=(k == 0), stop=(k == 1), tile_position=(0, 32 * h))
                last.then_inc(S["sp_ready"], 1)
                pe.wait_ge(S["sp_ready"], p + 5)
                pe.sem_inc(S["kc_used"], 1)
                pe.wait_ge(S["pn_ready"], 2 * p + 10)
                for m in range(4):
                    last = nc.tensor.transpose(ps[3][:, P * m:P * m + P], pex[0][:, P * m:P * m + P], const("ident"))
                last.then_inc(S["ptp_ready"], 1)
                pe.wait_ge(S["pt_in"], p + 5)
                pe.wait_ge(S["vc_in"], 16 * p + 16)
                if p:
                    pe.wait_ge(S["ol_ready"], p + 8)
                for c in range(DT):
                    for m in range(4):
                        last = nc.tensor.matmul(ps[0][:, 32 * c:32 * c + 32], vc[:, m, P * c:P * c + P],
                                                pt[:, 0, 0, P * m + 32 * (c // 2):P * m + 32 * (c // 2) + 32], start=(m == 0), stop=(m == 3))
                last.then_inc(S["o_ready"], 1)
                pe.wait_ge(S["o_ready"], p + 9)
                pe.sem_inc(S["vc_used"], 1)
            pe.wait_ge(S["ol_ready"], 12)
            dense(pe, "ox", oth, otl)
            norm_pe(pe, 3, n3_bufs)
            pe.wait_ge(S["xl_ready"], 4 * DT)
            done = 0
            for c, n in enumerate(THIRDS):
                dense(pe, f"f{c}", fnh, fnl)
                done += n
                pe.wait_ge(S["fhl_ready"], 1 + done)
                dense(pe, f"d{c}", hdh, hdl, k_tiles=n)
            norm_pe(pe, 4, n3_bufs)


def kernel(**inputs):
    import numpy as _np
    import concourse.bacc as _bacc
    from concourse import mybir as _mybir
    from concourse.bass_utils import run_bass_kernel_spmd as _run

    A = {k: _np.asarray(v) for k, v in inputs.items()}

    def tiles(a):
        return _np.ascontiguousarray(a.reshape(a.shape[0], -1, P).transpose(2, 1, 0))

    x = _np.concatenate([A["x_prompt"].reshape(SEQ, D), A["x_sample"].reshape(NS * TS, D)])

    def slots(w, order=None):
        k, n = w.shape
        s = _np.zeros((n // P, P, 8, P), w.dtype)
        s[:, :, :k // P, :] = w.reshape(k // P, P, n // P, P).transpose(2, 1, 0, 3)
        return s if order is None else s[order]

    w_in = A["w_in"][0]
    pairs = lambda n: [q for j in range(n) for q in (j, n + j)]
    parts = [slots(w_in[:, :2 * DC], pairs(CT)), slots(w_in[:, 2 * DC:2 * DC + SHT * P]), slots(w_in[:, 2 * DC + SHT * P:]),
             slots(A["w_o_conv"][0]), slots(A["w_o_rwkv"][0]), slots(A["w_out"][0]), slots(A["w_k_mem"][0]),
             slots(A["w_v_mem"][0]), slots(A["w_q_x"][0]), slots(A["w_o_x"][0])]
    a = 0
    for n in THIRDS:
        c = slice(a * P, (a + n) * P)
        parts.append(slots(_np.concatenate([A["w_ffn_gate"][0][:, c], A["w_ffn_up"][0][:, c]], 1), pairs(n)))
        parts.append(slots(A["w_ffn_down"][0][c, :]))
        a += n
    w_slots = _np.concatenate(parts).reshape(NSLOT, P, D)

    vecs = [tiles(A[n].reshape(1, -1))[:, :, 0] for n, _ in VECS[:-1]]
    vecs.append(tiles(A["w_dw"][0]).reshape(P, CT * TAPS))
    consts, wmask, smask, erow, xmask = tables(_np)
    ssd = _np.zeros((2, P, 8, 4, P), x.dtype)
    s0 = A["state_wkv"][0].reshape(2, 4, 8, 2, 64, 64).transpose(0, 3, 5, 2, 1, 4)
    ssd[:, 0:64, :, :, 0:64] = s0[:, 0]
    ssd[:, 64:128, :, :, 64:128] = s0[:, 1]
    kc = A["cache_mem_k"][0].reshape(4, 2 * NMEM, DT, P).transpose(0, 3, 2, 1)
    vc = A["cache_mem_v"][0].reshape(4, 4, P, D).transpose(0, 2, 1, 3)
    arrays = {
        "x": tiles(x), "mem": tiles(A["mem_prompt"][0]), "slots": w_slots, "vecs": _np.concatenate(vecs, 1), "consts": consts,
        "wmask": wmask, "smask": smask, "erow": erow, "xmask": xmask,
        "shift_in": tiles(A["state_shift"][0, :, 0]),
        "conv_in": A["state_conv"][0].reshape(NS, BUF, CT, P).transpose(3, 2, 0, 1),
        "lw": _np.concatenate([A["w_up"][0], A["a_up"][0]]), "gup": A["g_up"][0], "ssd": ssd, "kc": kc, "vc": vc,
    }
    arrays = {k: _np.ascontiguousarray(v) for k, v in arrays.items()}
    outs = {"y": (P, DT, NT), "mk": (P, DT, NMEM), "mv": (P, DT, NMEM), "conv_p": (P, CT, BUF), "conv_s": (P, CT, NS, BUF),
            "shift_out": (P, SHT, 1 + NS), "wkv_p": (P, 8, 64), "wkv_s": (2, P, 8, 4, 64)}
    nc = _bacc.Bacc("TRN2", target_bir_lowering=False, num_devices=1)
    f32 = _mybir.dt.float32
    io = {k: nc.dram_tensor("in_" + k, v.shape, f32, kind="ExternalInput").ap() for k, v in arrays.items()}
    io |= {k: nc.dram_tensor("out_" + k, v, f32, kind="ExternalOutput").ap() for k, v in outs.items()}
    io |= {k: nc.dram_tensor("tmp_" + k, (DT, P, NT), f32, kind="Internal").ap() for k in ("g2", "m1")}
    program(nc, io)
    r = _run(nc, [{"in_" + k: v for k, v in arrays.items()}], core_ids=[0]).results[0]
    o = {k: r["out_" + k] for k in outs}

    def rows(t):
        return t.transpose(2, 1, 0).reshape(t.shape[2], -1)

    y, sh = rows(o["y"]), rows(o["shift_out"])
    wp = o["wkv_p"].reshape(2, 64, 8, 64).transpose(2, 0, 3, 1).reshape(1, 1, HEADS, 64, 64)
    ws = o["wkv_s"].reshape(2, 2, 64, 8, 4, 64).transpose(0, 4, 3, 1, 5, 2).reshape(1, NS, HEADS, 64, 64)
    return (y[:SEQ].reshape(1, SEQ, D), y[SEQ:].reshape(NS, TS, D),
            rows(o["mk"]).reshape(1, 1, NMEM, XH, D // XH), rows(o["mv"]).reshape(1, 1, NMEM, XH, D // XH),
            rows(o["conv_p"]).reshape(1, 1, BUF, DC), sh[0].reshape(1, 1, 1, -1), wp,
            o["conv_s"].transpose(2, 3, 1, 0).reshape(1, NS, BUF, DC), sh[1:].reshape(1, NS, 1, -1), ws)


def tables(np_):
    f = np_.float32
    eye = np_.eye(P, dtype=f)
    t = np_.arange(64)
    consts = np_.zeros((P, NCONST), f)

    def put(name, a):
        consts[:, CCOL[name]:CCOL[name] + a.shape[1]] = a

    put("ident", eye)
    put("mean_d", np_.full((P, P), 1 / D, f))
    put("mean_c", np_.full((P, P), 1 / DC, f))
    head = (np_.arange(HEADS)[None, None, :] == 2 * np_.arange(8)[None, :, None] + (np_.arange(P) // 64)[:, None, None]).astype(f)
    put("head_sum", head.reshape(P, P))
    put("stream", np_.tile((t[:, None] // TS == np_.arange(4)).astype(f), (2, 1)))
    put("eps", np_.tile(np_.array([[EPS_RMS, EPS_LN, EPS_GN]], f), (P, 1)))
    i, j = t[:, None], t[None, :]
    same = i // TS == j // TS
    cols = [(i < j), (i <= j), (i < j) & same, (i <= j) & same]
    cols += [((i // 2 ** L) % 2 == 1) & (j // 2 ** L == i // 2 ** L - 1) for L in range(LEVELS)]
    cols.append(cols[4].T)
    cols = [np_.tile(c, (2, 1)) for c in cols[:4]] + [np_.kron(np_.eye(2), c) for c in cols[4:]]
    wmask = np_.concatenate(cols, 1).astype(f)
    start = np_.arange(NT)
    start = np_.where(start < SEQ, start % C, (start - SEQ) % TS) == 0
    smask = np_.tile((~start).astype(f)[None], (P, 1))
    erow = head.transpose(2, 1, 0).reshape(HEADS, D)
    q, m = np_.arange(P)[:, None], np_.arange(2 * NMEM)[None, :]
    xmask = np_.where((q % 32) // TS == m // NMEM, 0.0, -1e30).astype(f)
    return consts, wmask, smask, np_.ascontiguousarray(erow), xmask
```

```python
from contextlib import ExitStack, nullcontext

import concourse.bass as bass
import numpy as np
from concourse import mybir

F32 = mybir.dt.float32
F32R = mybir.dt.float32r
ALU = mybir.AluOpType
ACT = mybir.ActivationFunctionType
AX = mybir.AxisListType

P = 128
D = 1024
DT = D // P
SEQ = 512
NS = 8
TS = 16
NT = SEQ + NS * TS
HALF = NT // 2
DC = 512
CT = DC // P
TAPS = 31
BUF = TAPS - 1
NMEM = 256
XH = 4
HEADS = 16
SHT = 26
RT = 24
C = 64
NCH = SEQ // C
LEVELS = 6
DECAY = float(np.exp(-0.5))
EPS_RMS, EPS_LN, EPS_GN = 1e-6, 1e-5, 64e-5
UW = (BUF + SEQ) + NS * (BUF + TS)
PW = (1 + SEQ) + NS * (1 + TS)

VECS = [("g_norm_mix", 8), ("mu_shift", 26), ("b_dw", 4), ("ln_conv_g", 4), ("ln_conv_b", 4), ("w0", 8), ("a0", 8),
        ("k_k", 8), ("k_a", 8), ("r_k", 8), ("ln_x_g", 8), ("ln_x_b", 8), ("g_norm_x", 8), ("g_mem", 8),
        ("g_norm_ffn", 8), ("g_norm_final", 8), ("w_dw", CT * TAPS)]
VCOL, _n = {}, 0
for _name, _w in VECS:
    VCOL[_name] = _n
    _n += _w
NVEC = _n

CONSTS = [("ident", 128), ("mean_d", 128), ("mean_c", 128), ("head_sum", 128),
          ("stream", 4), ("eps", 4)]
CCOL, _n = {}, 0
for _name, _w in CONSTS:
    CCOL[_name] = _n
    _n += _w
NCONST = _n
STREAM_LEVELS = 4
NWMASK = 2 * 128 + (LEVELS + 1) * 128

THIRDS = (8, 8, 6)
SLOTS, _n = {}, 0
for _name, _w in [("glu", 8), ("rkv", 24), ("lora", 2), ("gate", 16), ("conv", 8), ("orwkv", 8), ("out", 8),
                  ("mk", 8), ("mv", 8), ("q", 8), ("ox", 8), ("f0", 16), ("d0", 8), ("f1", 16), ("d1", 8),
                  ("f2", 12), ("d2", 8)]:
    SLOTS[_name] = (_n, _w)
    _n += _w
NSLOT = _n


def program(nc, io):
    ctx = ExitStack()
    with ctx:
        base = -(-nc.sbuf_base // 32) * 32

        def at(name, offset, shape, dt=F32):
            return nc.alloc_sbuf_tensor_at(name, shape, dt, offset=base + offset)

        def sem(name):
            return ctx.enter_context(nc.semaphore(name))

        KB = 1024
        raw = [at(f"raw{s}", s * 4 * KB, [P, D]) for s in range(2)]
        whi = [at(f"whi{s}", (2 + s) * 4 * KB, [P, 8, P], F32R) for s in range(2)]
        wlo = [at(f"wlo{s}", (4 + s) * 4 * KB, [P, 8, P], F32R) for s in range(2)]
        o = 24 * KB
        cst = at("cst", o, [P, NCONST]); o += -(-4 * NCONST // 32) * 32
        wmask = at("wmask", o, [P, NWMASK]); o += 4 * NWMASK
        vec = at("vec", o, [P, NVEC]); o += -(-4 * NVEC // 32) * 32
        par = at("par", o, [P, 40]); o += 160
        o = -(-o // 64) * 64
        T20 = 4 * DT * NT
        A_O, K_O, V_O, B_O, M_O = o, o + 2 * T20, o + 3 * T20, o + 4 * T20, o + 5 * T20
        W_O = M_O + 3 * 2560 + 512
        ar = at("ar", A_O, [P, DT, 2, NT])
        kt = at("kt", K_O, [P, DT, NT])
        vt = at("vt", V_O, [P, DT, NT])
        bt = at("bt", B_O, [P, DT, NT])
        lora = at("lora", M_O, [P, NT])
        sgd = at("sgd", M_O + 2560, [P, NT])
        bon = at("bon", M_O + 5120, [16, NT])
        wcum = at("wcum", M_O + 7680, [P, DT, 16])
        xnh = at("xnh", B_O, [P, DT, NT], F32R)
        xnl = at("xnl", W_O, [P, DT, NT], F32R)
        up = at("up", W_O + T20, [P, CT, UW])
        acc = at("acc", W_O + T20 + 4 * CT * UW, [P, CT, NT])
        o = W_O + T20 + 4 * CT * UW + 4 * CT * NT
        pr = [at(f"pr{s}", o + s * 2624, [P, PW]) for s in range(2)]
        tmp = [at(f"tmp{s}", o + (2 + s) * 2624, [P, PW]) for s in range(2)]
        o += 4 * 2624
        shin = at("shin", o, [P, SHT, NS]); o += 4 * SHT * NS
        shout = at("shout", o, [P, SHT, 1 + NS]); o += 4 * SHT * (1 + NS)
        assert o <= 212800, o
        xin = at("xin", W_O + T20, [P, DT, NT])
        sq = [at(f"sq{s}", V_O + s * 2560, [P, NT]) for s in range(2)]
        std = at("std", V_O + 5120, [P, NT])
        rstd = at("rstd", V_O + 7680, [P, NT])
        xnf = [at(f"xnf{s}", V_O + 10240 + s * 2560, [P, NT]) for s in range(2)]
        ch = at("ch", W_O, [P, CT, NT], F32R)
        cl = at("cl", W_O + T20 // 2, [P, CT, NT], F32R)
        lw = at("lw", W_O + T20, [P, D])
        erow = at("erow", W_O + T20 + 4096, [16, D])
        smask = at("smask", W_O + T20 + 8192, [P, NT])
        slot_o = [W_O + q * 2560 for q in range(8)] + [W_O + T20 + 4 * CT * UW + q * 2560 for q in range(13)]

        def pair(name):
            return [at(f"{name}{s}", slot_o.pop(0), [P, NT]) for s in range(2)]

        p_l, p_L, p_m, p_e1, p_ta, p_kf, p_kk, p_b2, p_rk = [
            pair(n) for n in ("p_l", "p_L", "p_m", "p_e1", "p_ta", "p_kf", "p_kk", "p_b2", "p_rk")]
        rn = at("rn", slot_o.pop(0), [16, NT])
        o = W_O

        def blk(name):
            nonlocal o
            o += 4096
            return at(name, o - 4096, [P, 8, P])

        def stk(name, w=64):
            nonlocal o
            o += 8 * w * 4
            return at(name, o - 8 * w * 4, [P, 8, w])

        bd, kd, ad, vd = blk("bd"), blk("kd"), blk("ad"), blk("vd")
        atd, akd, xtd, td = blk("atd"), blk("akd"), blk("xtd"), blk("td")
        btd, ktd, vtd, sd = blk("btd"), blk("ktd"), blk("vtd"), blk("sd")
        ud, xd, rhsd = blk("ud"), blk("xd"), blk("rhsd")
        scb, sck = stk("scb", 128), stk("sck", 128)
        assert o <= 212800, o
        ssd = bt[:, :, 0:SEQ].rearrange("p t (b c) -> p t b c", b=4)
        um = kt[:, :, 0:256].rearrange("p t (b c) -> p t b c", b=4)
        vm = kt[:, :, 256:512].rearrange("p t (b c) -> p t b c", b=4)
        ns = ar[:, :, 0, 0:256].rearrange("p t (b c) -> p t b c", b=4)
        gup = at("gup", W_O + 4096, [P, D])
        erow2 = at("erow2", W_O, [16, D])
        dev16 = at("dev16", W_O + 8192, [16, NT])
        rstd16 = at("rstd16", W_O + 8192 + 2560, [16, NT])
        psq = [at(f"psq{s}", W_O + 8192 + (2 + s) * 2560, [P, NT]) for s in range(2)]
        hmean = at("hmean", W_O + 8192 + 4 * 2560, [P, P])
        bv = at("bv", M_O, [P, NT])
        po = [at(f"po{s}", W_O + T20 + 2 * T20 + s * 2560, [P, NT]) for s in range(2)]
        yoh = at("yoh", K_O, [P, DT, NT], F32R)
        yol = at("yol", B_O, [P, DT, NT], F32R)
        m1t = at("m1t", W_O + T20, [P, DT, NT])
        t2t = at("t2t", W_O + 2 * T20, [P, DT, NT])
        mgh = at("mgh", A_O, [P, DT, NT], F32R)
        mgl = at("mgl", A_O + T20, [P, DT, NT], F32R)

        ht = at("ht", V_O, [P, DT, NT])
        q_o = W_O
        n2_bufs = ([at(f"sqb{s}", q_o + s * 2560, [P, NT]) for s in range(2)], at("stdb", q_o + 5120, [P, NT]),
                   at("rstdb", q_o + 7680, [P, NT]), [at(f"xnb{s}", q_o + 10240 + s * 2560, [P, NT]) for s in range(2)])
        hnh = at("hnh", B_O, [P, DT, NT], F32R)
        hnl = at("hnl", W_O + T20, [P, DT, NT], F32R)
        T8 = 4 * DT * NMEM
        memt = at("memt", W_O + 2 * T20, [P, DT, NMEM])
        memh = at("memh", W_O + 2 * T20 + T8, [P, DT, NMEM], F32R)
        meml = at("meml", W_O + 2 * T20 + 2 * T8, [P, DT, NMEM], F32R)
        mkt = at("mkt", A_O, [P, DT, NMEM])
        mvt = at("mvt", A_O + T8, [P, DT, NMEM])
        mv = at("mv", A_O + 2 * T8, [P, 2, D])
        qt = at("qt", A_O + 3 * T8, [P, DT, NT])
        pt = at("pt", A_O + 3 * T8 + T20, [P, 2, XH, SEQ])
        kcs = [at(f"kc{s}", (B_O, A_O)[s], [P, DT, 2 * NMEM]) for s in range(2)]
        vcs = [[at(f"vc{s}_{m}", o, [P, 2, D]) for m, o in enumerate(os)]
               for s, os in enumerate(((W_O + T20, W_O + T20 + T8), (W_O + 3 * T20, A_O + 3 * T8 + T20 + T8)))]
        pex = [at(f"pex{s}", B_O + 2 * T8 + s * 4096, [P, 1024]) for s in range(2)]
        xmask = at("xmask", B_O + 2 * T8 + 8192, [P, 2 * NMEM])
        o = B_O + 2 * T8 + 10240
        mx = at("mx", o, [P, 2, XH])
        nmx = at("nmx", o + 32, [P, 2, XH])
        sm = at("sm", o + 64, [P, 2, XH])
        rs = at("rs", o + 96, [P, 2, XH])
        ost = at("ost", o + 128, [P, NMEM])
        assert o + 128 + 1024 <= W_O
        oth = at("oth", W_O + 2 * T20, [P, DT, NT], F32R)
        otl = at("otl", W_O, [P, DT, NT], F32R)
        n3_bufs = ([at(f"sqc{s}", B_O + s * 2560, [P, NT]) for s in range(2)], at("stdc", B_O + 5120, [P, NT]),
                   at("rstdc", B_O + 7680, [P, NT]), [at(f"xnc{s}", B_O + 10240 + s * 2560, [P, NT]) for s in range(2)])
        fnh = at("fnh", A_O, [P, DT, NT], F32R)
        fnl = at("fnl", A_O + T20, [P, DT, NT], F32R)
        hdh = at("hdh", W_O, [P, DT, NT], F32R)
        hdl = at("hdl", W_O + T20, [P, DT, NT], F32R)
        fth = at("fth", W_O + 2 * T20, [P, NT])
        fsg = at("fsg", W_O + 2 * T20 + 2560, [P, NT])
        fhd = at("fhd", W_O + 2 * T20 + 5120, [P, NT])

        ps = [ctx.enter_context(nc.psum_tensor(f"ps{i}", [P, 1024], F32)) for i in range(4)]
        CUT = 512 - HALF

        def span(t, n=NT):
            return t[:, CUT:CUT + NT] if n == NT else t[:, 0:n]

        def cut(t, h, n=NT):
            return t[:, CUT + h * HALF:CUT + (h + 1) * HALF] if n == NT else t[:, 0:n]

        def bank(g, b):
            return ps[2 * g + b // 2][:, 512 * (b % 2):512 * (b % 2) + 512]

        def const(name):
            c = CCOL[name]
            return cst[:, c:c + dict(CONSTS)[name]]

        def v1(name, k):
            if isinstance(k, int):
                return vec[:, VCOL[name] + k:VCOL[name] + k + 1]
            return vec[:, bass.ds(k + VCOL[name], 1)]

        def eps(i):
            return cst[:, CCOL["eps"] + i:CCOL["eps"] + i + 1]

        def row(a):
            return a.rearrange("p a n -> p (a n)")

        def tile_of(a, k, part=None):
            ks = slice(k, k + 1) if isinstance(k, int) else bass.ds(k, 1)
            return row(a[:, ks, :] if part is None else a[:, ks, part, :])

        def streams(a, start, width, off, n):
            return a[:, start:start + NS * width].rearrange("p (b c) -> p b c", b=NS)[:, :, off:off + n]

        def by_stream(a):
            return a.rearrange("p (b c) -> p b c", b=NS)

        names = """consts_in w_hi w_lo mm_done params sq_ready sq_part sq_summed ms_ready std_ready rstd_ready xn_ready
            xh_ready xl_ready glu_gate u_ready history_in pad_ready pr_ready pr_free diff_ready
            lora_tanh conv_step conv_done cmean_ready centred square_ready square_summed var_ready dev_ready inv_ready
            cn_ready ct_ready cs_ready ch_ready cl_ready stored lw_in
            rn_ready z_ready tz_ready kf_ready rnb_ready e_ready prep_dve prep_pool bonus_ready bonus_in
            pool_waits zeroed staged ad_staged sck_in sc_ready tb_ready vd_ready scm ad_e ad_o ak_o bkt_in v_in t_ready t_new x_ready
            x_new x_part xt_new xt_part rhs_ready rhs_in u_psum u_in s_ready s_sum s_new y_ready y_in sig_ready
            ss_in pst_ready pd_e pd_o ys_in um_ready ns_out up_zero pr_zero shift_half bonus_used ns_sum mb_ready g3_ready             post_dve po_ready yh_ready yl_ready mt_in merge_dve mg_ready mgh_ready mgl_ready res_in mem_in h_added mk_in mvt_in q_in mvx_ready mv_in             sp_ready mx_ready ex_ready pn_ready ptp_ready pt_in o_ready oh_ready ol_ready ost_in xm_in             kc_used vc_used ft_ready fh_ready fhh_ready             fhl_ready y_done all_stored gup_in""".split()
        S = {n: sem(n) for n in names}
        raw_in = [sem(f"raw_in{s}") for s in range(2)]
        psum_free = [sem(f"psum_free{s}") for s in range(2)]
        g2_out = [sem(f"g2_out{s}") for s in range(2)]
        m1_out = [sem(f"m1_out{s}") for s in range(2)]
        x_in = [sem(f"x_in{s}") for s in range(DT // 2)]
        kc_in = [sem(f"kc_in{s}") for s in range(2)]
        vc_in = [sem(f"vc_in{s}") for s in range(2)]

        block = ctx.enter_context(nc.Block())

        def load_slots(sp, lo, hi):
            with sp.Fori(0, (hi - lo) // 2) as i:
                for s in range(2):
                    if lo > 0:
                        sp.wait_ge(S["w_lo"], 2 * i + (lo + s - 1))
                    sp.dma_start(raw[s][:], io["slots"][bass.ds(2 * i + (lo + s), 1), :, :].rearrange("a p n -> (a p) n"))\
                        .then_inc(raw_in[s], 16)

        def hi_part(act, i, m, first=False):
            s = m % 2
            act.wait_ge(raw_in[s], 16 * i + 16 * (m // 2) + 16)
            if not first:
                act.wait_ge(S["mm_done"], 2 * i + (m + 1))
            nc.scalar.activation(whi[s][:].rearrange("p a b -> p (a b)"), raw[s][:], ACT.Copy).then_inc(S["w_hi"], 1)

        def await_(pool, s, value):
            pool.wait_ge(s, value)
            pool.sem_inc(S["pool_waits"], 1)

        def lo_part(pool, i, m):
            s = m % 2
            pool.wait_ge(S["w_hi"], 2 * i + (m + 1))
            nc.gpsimd.tensor_tensor(wlo[s][:].rearrange("p a b -> p (a b)"), raw[s][:],
                                    whi[s][:].rearrange("p a b -> p (a b)").bitcast(F32), ALU.subtract).then_inc(S["w_lo"], 1)

        def dense(pe, stage, hi, lo, k_tiles=DT, n=NT, part=None, split=None):
            n0, cnt = SLOTS[stage]
            if part:
                n0, cnt = n0 + part[0], part[1]
            nh = 2 if n == NT else 1
            w = n // nh
            with pe.Fori(0, cnt // 2) as i:
                for s in range(2):
                    pe.wait_ge(S["w_lo"], 2 * i + (n0 + s + 1))
                    pe.wait_ge(psum_free[s], i + (n0 // 2 + 1))
                    for k in range(k_tiles):
                        if split and s == 0:
                            pe.wait_ge(S[split[0]], split[1] + k + 1)
                        for q, (a, b) in enumerate(((whi[s], lo), (whi[s], hi), (wlo[s], hi))):
                            for h in range(nh):
                                last = nc.tensor.matmul(cut(ps[s], h, n), a[:, k, :], b[:, k, h * w:(h + 1) * w],
                                                        start=(k == 0 and q == 0), stop=(k == k_tiles - 1 and q == 2))
                    last.then_inc(S["mm_done"], 1)

        def stats_act(act, q, src, bufs, n=NT, loaded=None):
            sqb, stdb, _, _ = bufs
            for k in range(DT if q < 2 else 0):
                if loaded:
                    act.wait_ge(loaded[k // 2], 16)
                if 8 * q + k >= 2:
                    act.wait_ge(S["sq_summed"], 8 * q + k - 1)
                nc.scalar.activation(sqb[k % 2][:, 0:n], src(k), ACT.Square).then_inc(S["sq_ready"], 1)
            act.wait_ge(S["ms_ready"], q + 1)
            nc.scalar.activation(stdb[:, 0:n], span(ps[2], n), ACT.Sqrt, bias=eps(0)).then_inc(S["std_ready"], 1)

        def high_tile(act, q, k, s, xh, bufs, n=NT):
            act.wait_ge(S["xn_ready"], k + (8 * q + 1))
            nc.scalar.activation(tile_of(xh, k), bufs[3][s][:, 0:n], ACT.Copy).then_inc(S["xh_ready"], 1)

        def norm_act(act, q, src, xh, bufs, n=NT, loaded=None):
            stats_act(act, q, src, bufs, n, loaded)
            if q == 0:
                hi_part(act, 0, 0, first=True)
            for k in range(DT):
                high_tile(act, q, k, k % 2, xh, bufs, n)

        def norm_pe(pe, q, bufs, n=NT):
            nh = 2 if n == NT else 1
            w = n // nh
            if q >= 2:
                pe.wait_ge(S["sq_part"], (2 * DT + 1) * (q - 1))
                for h in range(nh):
                    last = nc.tensor.matmul(cut(ps[2], h, n), const("mean_d"), bufs[0][1][:, h * w:(h + 1) * w], start=True, stop=True)
                last.then_inc(S["ms_ready"], 1)
                return
            for k in range(DT):
                pe.wait_ge(S["sq_ready"], 8 * q + k + 1)
                for h in range(nh):
                    last = nc.tensor.matmul(cut(ps[2], h, n), const("mean_d"), bufs[0][k % 2][:, h * w:(h + 1) * w],
                                            start=(k == 0), stop=(k == DT - 1))
                last.then_inc(S["sq_summed"] if k < DT - 1 else S["ms_ready"], 1)
            pe.wait_ge(S["ms_ready"], q + 1)
            pe.sem_inc(S["sq_summed"], 1)

        def stats_dve(dve, q, bufs, n=NT):
            dve.wait_ge(S["std_ready"], q + 1)
            nc.vector.reciprocal(bufs[2][:, 0:n], bufs[1][:, 0:n]).then_inc(S["rstd_ready"], 1)
            dve.wait_ge(S["rstd_ready"], q + 1)

        def normed_tile(dve, q, k, s, src, gname, bufs, n=NT):
            if q > 0 or k >= 2:
                dve.wait_ge(S["xl_ready"], k + (8 * q - 1))
            nc.vector.scalar_tensor_tensor(out=bufs[3][s][:, 0:n], in0=src(k), scalar=v1(gname, k), in1=bufs[2][:, 0:n],
                                           op0=ALU.mult, op1=ALU.mult).then_inc(S["xn_ready"], 1)

        def norm_dve(dve, q, src, gname, bufs, n=NT):
            stats_dve(dve, q, bufs, n)
            for k in range(DT):
                normed_tile(dve, q, k, k % 2, src, gname, bufs, n)

        def low_tile(pool, q, k, s, xh, xl, bufs, n=NT):
            await_(pool, S["xh_ready"], k + (8 * q + 1))
            nc.gpsimd.tensor_tensor(tile_of(xl, k), bufs[3][s][:, 0:n], tile_of(xh, k).bitcast(F32),
                                    ALU.subtract).then_inc(S["xl_ready"], 1)

        def norm_pool(pool, q, xh, xl, bufs, n=NT):
            for k in range(DT):
                low_tile(pool, q, k, k % 2, xh, xl, bufs, n)


        gs = [slice(0, 4), slice(4, 8)]
        EVEN, ODD = slice(0, 64), slice(64, 128)
        RHS_LEVEL = 3

        def places(prompt, i):
            n = LEVELS if prompt else STREAM_LEVELS
            u0 = 2 * i + (0 if prompt else 2 * NCH)
            lv = lambda L, g: 2 * n * i + (0 if prompt else 2 * LEVELS * NCH) + 2 * L + g + 1
            lt = lambda L, g: 2 * (n - 1) * i + (0 if prompt else 2 * (LEVELS - 1) * NCH) + 2 * (L - 1) + g + 1
            return u0, bass.ds(C * i + (0 if prompt else SEQ), C), n, lv, lt, (lambda L, g: lt(L + 1, g))

        def four(a):
            return a.rearrange("p (t c) -> p t c", t=4)

        def rec_rhs_pe(w, prompt, i):
            mm = nc.tensor.matmul
            u0 = places(prompt, i)[0]
            if not prompt:
                w("ss_in", 16 * i + 16)
                for g in range(2):
                    w("v_in", u0 + g + 1)
                    for p in range(4):
                        t = 4 * g + p
                        v = bank(g, 3)[:, P * p:P * p + P].rearrange("p (a b c) -> p a b c", a=2, b=4)
                        for b in range(4):
                            last = mm(v[:, :, b, :], ssd[:, t, b, :], ar[:, t, :, bass.ds(C * i + (SEQ + TS * b), TS)],
                                      start=True, stop=True)
                    last.then_inc(S["pst_ready"], 1)
            for g in range(2):
                w("v_in", u0 + g + 1)
                w("ak_o", u0 + g + 1)
                if prompt:
                    w("s_new", u0 + g + 1)
                    w("ad_staged", u0 + g + 1)
                else:
                    w("pd_e", 2 * i + g + 1)
                    w("pd_o", 2 * i + g + 1)
                    w("ys_in", 2 * i + g + 1)
                for p in range(4):
                    t = 4 * g + p
                    out = bank(g, 3)[:, P * p:P * p + P]
                    mm(out, ad[:, t, :], sd[:, t, :] if prompt else const("ident"), start=True, stop=False)
                    last = mm(out, akd[:, t, :], vtd[:, t, :], start=False, stop=True)
                last.then_inc(S["rhs_ready"], 1)

        def rec_pe(pe, prompt, i):
            u0, col, n, lv, lt, lx = places(prompt, i)

            def w(name, v):
                pe.wait_ge(S[name], v)

            mm = nc.tensor.matmul
            for g in range(2):
                w("staged", u0 + g + 1)
                w("y_in", u0 + g + 1)
                for d, b in ((bd, 0), (kd, 1)):
                    for p in range(4):
                        last = mm(bank(g, b)[:, P * p:P * p + P].rearrange("p (a c) -> p a c", a=2), d[:, 4 * g + p, :],
                                  ar[:, 4 * g + p, :, col], start=True, stop=True)
                    last.then_inc(S["sc_ready"], 1)
            for g in range(2):
                w("s_new", u0 + g + 1)
                for d, b in ((bd, 2), (kd, 3)):
                    for p in range(4):
                        last = nc.tensor.transpose(bank(g, b)[:, P * p:P * p + P], d[:, 4 * g + p, :], const("ident"))
                last.then_inc(S["tb_ready"], 1)
            for L in range(n):
                for g in range(2):
                    if L == 0:
                        w("ad_e", u0 + g + 1)
                        w("ad_o", u0 + g + 1)
                    else:
                        w("x_new", lx(L - 1, g))
                    for p in range(4):
                        last = mm(bank(g, 0)[:, P * p:P * p + P], atd[:, 4 * g + p, :],
                                  const("ident") if L == 0 else xd[:, 4 * g + p, :], start=True, stop=True)
                    last.then_inc(S["t_ready"], 1)
                if L == 0:
                    for g in range(2):
                        w("bkt_in", u0 + g + 1)
                        for p in range(4):
                            last = nc.tensor.transpose(bank(g, 2)[:, P * p:P * p + P], vd[:, 4 * g + p, :], const("ident"))
                        last.then_inc(S["vd_ready"], 1)
                    continue
                if L == RHS_LEVEL:
                    rec_rhs_pe(w, prompt, i)
                for g in range(2):
                    w("t_new", lt(L, g))
                    w("xt_new", lv(L - 1, g))
                    if L == 1:
                        w("v_in", u0 + g + 1)
                    for p in range(4):
                        t = 4 * g + p
                        if L < n - 1:
                            mm(bank(g, 1)[:, P * p:P * p + P], xtd[:, t, :], td[:, t, :], start=True, stop=True)
                        last = mm(bank(g, 2)[:, P * p:P * p + P], td[:, t, :], xtd[:, t, :], start=True, stop=True)
                    last.then_inc(S["x_ready"], 1)
            for g in range(2):
                w("xt_new", lv(n - 1, g))
                w("rhs_in", u0 + g + 1)
                for p in range(4):
                    last = mm(bank(g, 3)[:, P * p:P * p + P], xtd[:, 4 * g + p, :], rhsd[:, 4 * g + p, :], start=True, stop=True)
                last.then_inc(S["u_psum"], 1)
            for g in range(2):
                w("u_in", u0 + g + 1)
                if prompt:
                    for p in range(4):
                        t = 4 * g + p
                        out = bank(g, 2)[:, P * p:P * p + P]
                        mm(out, btd[:, t, :], ud[:, t, :], start=True, stop=False)
                        last = mm(out, ktd[:, t, :], vtd[:, t, :], start=False, stop=True)
                else:
                    w("um_ready", 2 * i + g + 1)
                    for p in range(4):
                        t = 4 * g + p
                        out = bank(g, 3 - p // 2)[:, 256 * (p % 2):256 * (p % 2) + 256]
                        mm(out, btd[:, t, :], um[:, t, :, :], start=True, stop=False)
                        last = mm(out, ktd[:, t, :], vm[:, t, :, :], start=False, stop=True)
                last.then_inc(S["s_ready"], 1)
            for g in range(2):
                for p in range(4):
                    t = 4 * g + p
                    out = bank(g, 1)[:, 64 * p:64 * p + 64]
                    if prompt:
                        mm(out, sd[:, t, :], ar[:, t, 1, col], start=True, stop=False)
                    mm(out, ud[:, t, :], scb[:, t, 64:128], start=not prompt, stop=False)
                    last = mm(out, vtd[:, t, :], sck[:, t, 64:128], start=False, stop=True)
                last.then_inc(S["y_ready"], 1)

        def rec_pool(pool, prompt, i):
            u0, col = places(prompt, i)[:2]
            for g in range(2):
                await_(pool, S["vd_ready"], u0 + g + 1)
                for dst, src in ((bd, bt), (kd, kt), (vd, vt)):
                    for h in (EVEN, ODD):
                        last = nc.gpsimd.tensor_copy(dst[h, gs[g], h], src[h, gs[g], col])
                last.then_inc(S["staged"], 1)
            if prompt:
                for g in range(2):
                    await_(pool, S["rhs_ready"], u0 + g + 1)
                    for h in (EVEN, ODD):
                        last = nc.gpsimd.tensor_copy(ad[h, gs[g], h], ar[h, gs[g], 0, col])
                    last.then_inc(S["ad_staged"], 1)

        def rec_act(act, prompt, i):
            u0, col, n, lv, lt, lx = places(prompt, i)

            def w(name, v):
                act.wait_ge(S[name], v)

            def copy(out, in_):
                return nc.scalar.activation(out, in_, ACT.Copy)

            for g in range(2):
                w("scm", u0 + g + 1)
                copy(atd[EVEN, gs[g], EVEN], scb[EVEN, gs[g], 0:64]).then_inc(S["ad_e"], 1)
            for g in range(2):
                w("tb_ready", u0 + g + 1)
                copy(btd[:, gs[g], :], four(bank(g, 2)[:, :]))
                copy(ktd[:, gs[g], :], four(bank(g, 3)[:, :])).then_inc(S["bkt_in"], 1)
            for g in range(2):
                w("sck_in", u0 + g + 1)
                copy(akd[EVEN, gs[g], EVEN], sck[EVEN, gs[g], 0:64])
                w("vd_ready", u0 + g + 3)
                copy(vtd[:, gs[g], :], four(bank(g, 2)[:, :])).then_inc(S["v_in"], 1)
            for g in range(2):
                if not prompt:
                    w("pst_ready", 2 * i + g + 1)
                    v = bank(g, 3)[:, :].rearrange("p (t a c) -> p t a c", t=4, a=2)
                    copy(ad[EVEN, gs[g], EVEN], v[EVEN, :, 0, :]).then_inc(S["pd_e"], 1)
                    w("pd_o", 2 * i + g + 1)
                    copy(sd[:, gs[g], 0:64], v[:, :, 1, :]).then_inc(S["ys_in"], 1)
            for g in range(2):
                w("rhs_ready", u0 + g + 3)
                copy(rhsd[:, gs[g], :], four(bank(g, 3)[:, :])).then_inc(S["rhs_in"], 1)
            for g in range(2):
                w("u_psum", u0 + g + 1)
                copy(ud[:, gs[g], :], four(bank(g, 3)[:, :])).then_inc(S["u_in"], 1)
            if prompt:
                for g in range(2):
                    w("y_ready", u0 + g + 1)
                    copy(ar[:, gs[g], 1, col], four(bank(g, 1)[:, 0:256])).then_inc(S["y_in"], 1)

        def rec_dve(dve, prompt, i):
            u0, col, n, lv, lt, lx = places(prompt, i)

            def w(name, v):
                dve.wait_ge(S[name], v)

            tt = nc.vector.tensor_tensor

            def b4(a, n=64, parts=slice(0, P)):
                return a[parts].rearrange("p (a c) -> p a c", a=1).to_broadcast([len(range(*parts.indices(P))), 4, n])

            m0 = 0 if prompt else 128

            def by_stream_rows(dst, src, g):
                for b in range(4):
                    for h in (EVEN, ODD):
                        last = nc.vector.tensor_scalar(dst[h, gs[g], b, :], src[h, gs[g], h],
                                                       cst[h, CCOL["stream"] + b:CCOL["stream"] + b + 1], None, ALU.mult)
                return last

            step = lambda L: b4(wmask[:, 256 + P * L:256 + P * L + P], P)
            one = b4(const("ident"), P)
            for g in range(2):
                w("sc_ready", 2 * u0 + (2 * g + 1))
                tt(scb[:, gs[g], :], four(bank(g, 0)[:, :]), b4(wmask[:, m0:m0 + 128], 128), ALU.mult).then_inc(S["scm"], 1)
                tt(atd[ODD, gs[g], ODD], four(bank(g, 0)[:, :])[ODD, :, 0:64], b4(wmask[:, m0:m0 + 64], 64, ODD), ALU.mult)\
                    .then_inc(S["ad_o"], 1)
            for g in range(2):
                w("ad_e", u0 + g + 1)
                w("ad_o", u0 + g + 1)
                tt(xtd[:, gs[g], :], atd[:, gs[g], :], step(LEVELS), ALU.mult).then_inc(S["xt_part"], 1)
            for g in range(2):
                w("xt_part", u0 + g + 1)
                tt(xtd[:, gs[g], :], xtd[:, gs[g], :], one, ALU.add).then_inc(S["xt_new"], 1)
            for g in range(2):
                w("t_ready", lv(0, g))
                tt(xd[:, gs[g], :], four(bank(g, 0)[:, :]), step(0), ALU.mult).then_inc(S["x_part"], 1)
            for g in range(2):
                w("x_part", u0 + g + 1)
                tt(xd[:, gs[g], :], xd[:, gs[g], :], one, ALU.add).then_inc(S["x_new"], 1)
            for g in range(2):
                w("sc_ready", 2 * u0 + (2 * g + 2))
                tt(sck[:, gs[g], :], four(bank(g, 1)[:, :]), b4(wmask[:, m0:m0 + 128], 128), ALU.mult).then_inc(S["sck_in"], 1)
                tt(akd[ODD, gs[g], ODD], four(bank(g, 1)[:, :])[ODD, :, 0:64], b4(wmask[:, m0:m0 + 64], 64, ODD), ALU.mult)\
                    .then_inc(S["ak_o"], 1)
            for L in range(1, n):
                for g in range(2):
                    w("t_ready", lv(L, g))
                    tt(td[:, gs[g], :], four(bank(g, 0)[:, :]), step(L), ALU.mult).then_inc(S["t_new"], 1)
                if L == RHS_LEVEL and not prompt:
                    for g in range(2):
                        w("pst_ready", 2 * i + g + 1)
                        v = bank(g, 3)[:, :].rearrange("p (t a c) -> p t a c", t=4, a=2)
                        w("pd_e", 2 * i + g + 1)
                        nc.vector.tensor_copy(ad[ODD, gs[g], ODD], v[ODD, :, 0, :]).then_inc(S["pd_o"], 1)
                if L == n - 1 and not prompt:
                    for g in range(2):
                        w("v_in", u0 + g + 1)
                        by_stream_rows(vm, vtd, g)
                for g in range(2):
                    w("x_ready", lt(L, g))
                    if L < n - 1:
                        w("x_new", lx(L - 1, g))
                        tt(xd[:, gs[g], :], four(bank(g, 1)[:, :]), xd[:, gs[g], :], ALU.add).then_inc(S["x_new"], 1)
                    w("xt_new", lv(L - 1, g))
                    tt(xtd[:, gs[g], :], four(bank(g, 2)[:, :]), xtd[:, gs[g], :], ALU.add).then_inc(S["xt_new"], 1)
            if prompt:
                for g in range(2):
                    w("s_ready", u0 + g + 1)
                    w("y_ready", u0 + g + 1)
                    w("s_new", u0 + g + 1)
                    tt(sd[:, gs[g], :], four(bank(g, 2)[:, :]), sd[:, gs[g], :], ALU.add).then_inc(S["s_sum"], 1)
                for g in range(2):
                    w("s_sum", u0 + g + 1)
                    tt(sd[:, gs[g], :], sd[:, gs[g], :], wcum[:, gs[g], bass.ds(i, 1)].to_broadcast([P, 4, P]), ALU.mult)\
                        .then_inc(S["s_new"], 1)
            else:
                for g in range(2):
                    w("u_in", u0 + g + 1)
                    last = by_stream_rows(um, ud, g)
                    last.then_inc(S["um_ready"], 1)
                for g in range(2):
                    w("s_ready", u0 + g + 1)
                    w("ns_out", 16 * i + 16)
                    for hp in range(2):
                        pp = slice(4 * g + 2 * hp, 4 * g + 2 * hp + 2)
                        for h in (slice(0, 64), slice(64, 128)):
                            tt(ns[h, pp, :, :], bank(g, 3 - hp)[h, :].rearrange("p (t b c) -> p t b c", t=2, b=4),
                               ssd[h, pp, :, h], ALU.add).then_inc(S["ns_sum"], 1)
                for g in range(2):
                    w("y_ready", u0 + g + 1)
                    w("ys_in", 2 * i + g + 1)
                    tt(ar[:, gs[g], 1, col], four(bank(g, 1)[:, 0:256]), sd[:, gs[g], 0:64], ALU.add)\
                        .then_inc(S["y_in"], 1)
                for g in range(2):
                    w("ns_sum", 8 * i + 4 * g + 4)
                    wb = wcum[:, gs[g], bass.ds(4 * i + NCH, 4)].rearrange("p t (b c) -> p t b c", c=1).to_broadcast([P, 4, 4, 64])
                    tt(ns[:, gs[g], :, :], ns[:, gs[g], :, :], wb, ALU.mult).then_inc(S["s_new"], 1)

        n_bufs = (sq, std, rstd, xnf)

        @block.sync
        def _(sp):
            for k in range(DT // 2):
                sp.dma_start(xin[:, 2 * k:2 * k + 2, :], io["x"][:, 2 * k:2 * k + 2, :]).then_inc(x_in[k], 16)
            sp.dma_start(cst[:], io["consts"]).then_inc(S["consts_in"], 16)
            sp.dma_start(vec[:], io["vecs"]).then_inc(S["consts_in"], 16)
            load_slots(sp, 0, 2)
            sp.dma_start(shin[:], io["shift_in"]).then_inc(S["consts_in"], 16)
            sp.dma_start(wmask[:], io["wmask"]).then_inc(S["consts_in"], 16)
            load_slots(sp, 2, 4)
            sp.wait_ge(S["xn_ready"], DT)
            for j in range(CT):
                sp.dma_start(streams(up[:, j, :], BUF + SEQ, BUF + TS, 0, BUF), io["conv_in"][:, j, :, :])\
                    .then_inc(S["history_in"], 16)
            load_slots(sp, 4, SLOTS["gate"][0])
            sp.wait_ge(S["u_ready"], CT + 1)
            for s in range(2):
                sp.wait_ge(psum_free[s], CT + 1)
            sp.wait_ge(S["history_in"], 16 * CT)
            for j in range(CT):
                sp.dma_start(io["conv_p"][:, j, :], up[:, j, SEQ:SEQ + BUF]).then_inc(S["stored"], 16)
                sp.dma_start(io["conv_s"][:, j, :, :], streams(up[:, j, :], BUF + SEQ, BUF + TS, TS, BUF)).then_inc(S["stored"], 16)
            load_slots(sp, SLOTS["gate"][0], SLOTS["conv"][0])
            for s in range(2):
                sp.wait_ge(psum_free[s], SLOTS["gate"][0] // 2 + 1)
            sp.dma_start(io["shift_out"], shout[:]).then_inc(S["stored"], 16)
            load_slots(sp, SLOTS["conv"][0], SLOTS["orwkv"][0] + 2)
            sp.wait_ge(S["cs_ready"], CT)
            sp.wait_ge(S["stored"], 16 * (2 * CT + 1))
            sp.dma_start(lw[:], io["lw"]).then_inc(S["lw_in"], 16)
            sp.dma_start(erow[:], io["erow"]).then_inc(S["lw_in"], 16)
            sp.dma_start(smask[:], io["smask"]).then_inc(S["lw_in"], 16)
            sp.wait_ge(S["staged"], 2 * NCH)
            for j in range(2):
                if j:
                    sp.wait_ge(S["pst_ready"], 2)
                    sp.wait_ge(S["s_new"], 2 + 2 * NCH + 2)
                sp.dma_start(ssd, io["ssd"][j]).then_inc(S["ss_in"], 16)
                if j == 0:
                    sp.wait_ge(S["s_new"], 2 + 2 * NCH)
                    for h in (EVEN, ODD):
                        sp.dma_start(io["wkv_p"][h], sd[h, :, h]).then_inc(S["stored"], 16)
                else:
                    sp.wait_ge(S["u_psum"], 2 * NCH + 4)
                    sp.dma_start(erow2[:], io["erow"]).then_inc(S["gup_in"], 16)
                    sp.dma_start(gup[:], io["gup"]).then_inc(S["gup_in"], 16)
                    sp.dma_start(hmean[:], io["hmean"]).then_inc(S["gup_in"], 16)
                sp.wait_ge(S["s_new"], 2 + 2 * NCH + 2 * j + 2)
                sp.dma_start(io["wkv_s"][j], ns).then_inc(S["ns_out"], 16)
            sp.wait_ge(S["y_in"], 2 + 2 * NCH + 4)
            sp.dma_start(m1t[:], io["m1"].rearrange("t p n -> p t n")).then_inc(S["mt_in"], 16)
            sp.dma_start(t2t[:], io["g2"].rearrange("t p n -> p t n")).then_inc(S["mt_in"], 16)
            load_slots(sp, SLOTS["orwkv"][0] + 2, SLOTS["orwkv"][0] + 8)
            sp.wait_ge(S["post_dve"], 5 * DT)
            sp.dma_start(ht[:], io["x"]).then_inc(S["res_in"], 16)
            load_slots(sp, SLOTS["out"][0], SLOTS["out"][0] + 2)
            sp.wait_ge(S["mg_ready"], DT)
            sp.dma_start(memt[:], io["mem"]).then_inc(S["mem_in"], 16)
            load_slots(sp, SLOTS["out"][0] + 2, SLOTS["q"][0] + 2)
            sp.wait_ge(S["mk_in"], DT)
            sp.dma_start(io["mk"], mkt[:]).then_inc(S["all_stored"], 16)
            sp.wait_ge(S["mvt_in"], DT)
            sp.dma_start(io["mv"], mvt[:]).then_inc(S["all_stored"], 16)
            load_slots(sp, SLOTS["q"][0] + 2, SLOTS["ox"][0] + 2)
            sp.wait_ge(S["q_in"], DT)
            sp.dma_start(xmask[:], io["xmask"]).then_inc(S["xm_in"], 16)
            for p in range(4):
                if p == 1:
                    sp.wait_ge(S["all_stored"], 32)
                    sp.wait_ge(S["mvx_ready"], 2)
                    sp.wait_ge(S["sp_ready"], 4)
                if p >= 2:
                    sp.wait_ge(S["kc_used"], p - 1)
                sp.dma_start(kcs[p % 2][:], io["kc"][p]).then_inc(kc_in[p % 2], 16)
                if p >= 2:
                    sp.wait_ge(S["vc_used"], p - 1)
                if p == 1:
                    sp.wait_ge(S["o_ready"], DT)
                for m in range(2):
                    sp.dma_start(vcs[p % 2][m][:], io["vc"][p][:, 2 * m:2 * m + 2, :]).then_inc(vc_in[p % 2], 16)
            load_slots(sp, SLOTS["ox"][0] + 2, NSLOT)
            for k in range(DT):
                sp.wait_ge(S["y_done"], k + 1)
                sp.dma_start(io["y"][:, k, :], ht[:, k, :]).then_inc(S["all_stored"], 16)
            sp.wait_ge(S["all_stored"], 16 * (2 + DT))
            sp.wait_ge(S["stored"], 16 * (2 * CT + 3))
            sp.wait_ge(S["ns_out"], 48)

        @block.scalar
        def _(act):
            act.wait_ge(S["consts_in"], 64)
            norm_act(act, 0, lambda k: xin[:, k, :], xnh, n_bufs, loaded=x_in)
            n0, cnt = SLOTS["glu"]
            with act.Fori(0, cnt // 2) as i:
                hi_part(act, i, n0 + 1)
                hi_part(act, i, n0 + 2)
                act.wait_ge(S["mm_done"], 2 * i + (n0 + 4))
                nc.scalar.activation(tmp[0][:, 0:NT], span(ps[1]), ACT.Tanh, scale=0.5).then_inc(S["glu_gate"], 1)
            n0 = SLOTS["rkv"][0]
            with act.Fori(0, SHT // 2) as i:
                for s in range(2):
                    hi_part(act, i, n0 + s + 1)
                    act.wait_ge(S["mm_done"], 2 * i + (n0 + s + 3))
                    act.wait_ge(S["pr_free"], 2 * i + (s + 1))
                    nc.scalar.activation(pr[s][:, 1:1 + SEQ], ps[s][:, CUT:CUT + SEQ], ACT.Copy).then_inc(S["pr_ready"], 1)
                    nc.scalar.activation(streams(pr[s], 1 + SEQ, 1 + TS, 1, TS), by_stream(ps[s][:, CUT + SEQ:CUT + NT]),
                                         ACT.Copy).then_inc(S["pr_ready"], 1)
            act.wait_ge(S["pr_free"], 2 + SHT)
            nc.scalar.activation(lora[0:64, :], lora[0:64, :], ACT.Tanh).then_inc(S["lora_tanh"], 1)
            nc.scalar.activation(sgd[:], sgd[:], ACT.Tanh, scale=0.5).then_inc(S["lora_tanh"], 1)
            n0 = SLOTS["gate"][0]
            with act.Fori(0, 4) as i:
                for s in range(2):
                    hi_part(act, i, n0 + s + 1)
                    act.wait_ge(S["mm_done"], 2 * i + (n0 + s + 3))
                    nc.scalar.activation(row(ar[:, bass.ds(2 * i + s, 1), 0, :]), span(ps[s]),
                                         ACT.Tanh, scale=0.5).then_inc(psum_free[s], 1)

            def rwkv_gate(i, first):
                for s in range(2):
                    hi_part(act, i, n0 + 8 + s + 1)
                    act.wait_ge(S["mm_done"], 2 * i + (n0 + 8 + s + 3))
                    if not first:
                        act.wait_ge(g2_out[s], 16 * i)
                    nc.scalar.activation(tmp[s][:, 0:NT], span(ps[s]), ACT.Tanh, scale=0.5).then_inc(psum_free[s], 1)

            act.wait_ge(S["stored"], 16 * 2 * CT)
            for j in range(CT):
                act.wait_ge(S["centred"], j + 1)
                nc.scalar.activation(up[:, j, 0:NT], acc[:, j, :], ACT.Square).then_inc(S["square_ready"], 1)
            rwkv_gate(0, True)
            rwkv_gate(1, False)
            act.wait_ge(S["var_ready"], 1)
            nc.scalar.activation(pr[0][:, 0:NT], span(ps[2]), ACT.Sqrt, bias=eps(1)).then_inc(S["dev_ready"], 1)
            rwkv_gate(2, False)
            for j in range(CT):
                act.wait_ge(S["cn_ready"], 2 * j + 2)
                nc.scalar.activation(up[:, j, 0:NT], acc[:, j, :], ACT.Tanh).then_inc(S["ct_ready"], 1)
            rwkv_gate(3, False)
            for j in range(CT):
                act.wait_ge(S["cs_ready"], j + 1)
                nc.scalar.activation(ch[:, j, :], acc[:, j, :], ACT.Copy).then_inc(S["ch_ready"], 1)
            for s in range(2):
                act.wait_ge(g2_out[s], 64)
            n0 = SLOTS["conv"][0]
            with act.Fori(0, 4) as i:
                for s in range(2):
                    hi_part(act, i, n0 + s + 1)
                    act.wait_ge(S["square_summed"], 2 * i + (s + 2))
                    nc.scalar.activation(tmp[s][:, 0:NT], tile_of(kt, 2 * i + s), ACT.Square, scale=v1("k_k", 2 * i + s))\
                        .then_inc(S["square_ready"], 1)
            act.wait_ge(S["var_ready"], 2)
            nc.scalar.activation(rn[:], span(ps[3])[0:16, :], ACT.Sqrt).then_inc(S["dev_ready"], 1)
            act.wait_ge(m1_out[0], 64)
            act.wait_ge(m1_out[1], 64)
            act.wait_ge(S["lw_in"], 48)

            def low_rank(j):
                s = j % 2
                act.wait_ge(S["z_ready"], j + 1)
                if j >= 2:
                    act.wait_ge(S["prep_dve"], 8 * (j - 2) + 5)
                nc.scalar.activation(p_l[s][:], span(ps[0]), ACT.Tanh, scale=0.5, bias=par[:, j:j + 1]).then_inc(S["tz_ready"], 1)
                nc.scalar.activation(p_ta[s][:], span(ps[1]), ACT.Tanh, scale=0.5, bias=par[:, 8 + j:9 + j]).then_inc(S["tz_ready"], 1)
                act.wait_ge(S["tz_ready"], 3 * j + 1)
                nc.scalar.activation(p_l[s][:], p_l[s][:], ACT.Identity, bias=eps(3)).then_inc(S["tz_ready"], 1)

            def rate_factor(j):
                act.wait_ge(S["tz_ready"], 3 * j + 2)
                if j >= 2:
                    act.wait_ge(S["prep_dve"], 8 * (j - 2) + 6)
                    act.wait_ge(S["prep_pool"], 4 * (j - 2) + 4)
                nc.scalar.activation(p_kf[j % 2][:], p_ta[j % 2][:], ACT.Identity, scale=par[:, 16 + j:17 + j], bias=par[:, 24 + j:25 + j])\
                    .then_inc(S["kf_ready"], 1)

            act.wait_ge(S["params"], 4)
            low_rank(0)
            rate_factor(0)
            for j in range(DT):
                s = j % 2
                if j + 1 < DT:
                    low_rank(j + 1)
                act.wait_ge(S["prep_dve"], 8 * j + 2)
                if j >= 2:
                    act.wait_ge(S["prep_pool"], 4 * (j - 2) + 4)
                nc.scalar.activation(p_e1[s][:], p_L[s][:], ACT.Exp, scale=-DECAY / 2).then_inc(S["e_ready"], 1)
                nc.scalar.activation(p_L[s][:], p_L[s][:], ACT.Exp, scale=DECAY / 2).then_inc(S["e_ready"], 1)
                nc.scalar.activation(p_m[s][:], p_m[s][:], ACT.Exp, scale=-DECAY / 2).then_inc(S["e_ready"], 1)
                if j + 1 < DT:
                    rate_factor(j + 1)
            act.wait_ge(S["bonus_ready"], 1)
            nc.scalar.activation(bon[:], span(ps[3])[0:16, :], ACT.Copy).then_inc(S["bonus_in"], 1)
            act.wait_ge(S["prep_dve"], 8 * DT)
            act.wait_ge(S["prep_pool"], 4 * DT)
            act.wait_ge(S["zeroed"], 2)
            act.sem_inc(S["y_in"], 2)
            with act.Fori(0, NCH) as i:
                rec_act(act, True, i)
            act.wait_ge(S["stored"], 16 * (2 * CT + 3))
            with act.Fori(0, 2) as i:
                rec_act(act, False, i)
            for j in range(DT):
                act.wait_ge(S["centred"], j + 5)
                if j >= 2:
                    act.wait_ge(S["square_summed"], j - 1 + 10)
                nc.scalar.activation(psq[j % 2][:], ar[:, j, 1, :], ACT.Square).then_inc(S["square_ready"], 1)
            act.wait_ge(S["var_ready"], 3)
            nc.scalar.activation(dev16[:], span(ps[3])[0:16, :], ACT.Sqrt, scale=1 / 64, bias=eps(2)[0:16, :]).then_inc(S["dev_ready"], 1)
            for j in range(DT):
                act.wait_ge(S["po_ready"], j + 1)
                nc.scalar.activation(yoh[:, j, :], po[j % 2][:], ACT.Copy).then_inc(S["yh_ready"], 1)
            act.wait_ge(S["ns_out"], 48)
            n0 = SLOTS["orwkv"][0]
            with act.Fori(0, 4) as i:
                for s in range(2):
                    hi_part(act, i, n0 + s + 1)
                    act.wait_ge(S["mg_ready"], 2 * i + (s + 1))
                    nc.scalar.activation(tile_of(mgh, 2 * i + s), po[s][:], ACT.Copy).then_inc(S["mgh_ready"], 1)
            act.wait_ge(S["mem_in"], 16)
            stats_act(act, 1, lambda k: memt[:, k, :], n2_bufs, NMEM)
            n0 = SLOTS["out"][0]
            with act.Fori(0, 4) as i:
                for s in range(2):
                    hi_part(act, i, n0 + s + 1)
                    high_tile(act, 1, 2 * i + s, s, memh, n2_bufs, NMEM)
            act.wait_ge(S["h_added"], DT)
            stats_act(act, 2, lambda k: ht[:, k, :], n2_bufs)
            for stage, dst, done in (("mk", mkt, S["mk_in"]), ("mv", mvt, S["mvt_in"])):
                n0 = SLOTS[stage][0]
                with act.Fori(0, 4) as i:
                    for s in range(2):
                        hi_part(act, i, n0 + s + 1)
                        act.wait_ge(S["mm_done"], 2 * i + (n0 + s + 3))
                        nc.scalar.activation(tile_of(dst, 2 * i + s), ps[s][:, 0:NMEM], ACT.Copy).then_inc(done, 1)
                        act.wait_ge(done, 2 * i + (s + 1))
                        act.sem_inc(psum_free[s], 1)
                        if stage == "mk":
                            high_tile(act, 2, 2 * i + s, s, hnh, n2_bufs)
            n0 = SLOTS["q"][0]
            with act.Fori(0, 4) as i:
                for s in range(2):
                    hi_part(act, i, n0 + s + 1)
                    act.wait_ge(S["mm_done"], 2 * i + (n0 + s + 3))
                    nc.scalar.activation(tile_of(qt, 2 * i + s), span(ps[s]), ACT.Copy, scale=1 / 16).then_inc(S["q_in"], 1)
                    act.wait_ge(S["q_in"], 2 * i + (s + 1))
                    act.sem_inc(psum_free[s], 1)
            for m in range(2):
                act.wait_ge(S["mvx_ready"], m + 1)
                nc.scalar.activation(mv[:, m, :], ps[m][:, :], ACT.Copy).then_inc(S["mv_in"], 1)

            def softmax_in(i):
                s = i % 2
                act.wait_ge(S["mx_ready"], 2 * i + 2)
                if i >= 2:
                    act.wait_ge(S["ptp_ready"], i - 1)
                for h in range(XH):
                    nc.scalar.activation(pex[s][:, NMEM * h:NMEM * h + NMEM], ps[2 + s][:, NMEM * h:NMEM * h + NMEM], ACT.Exp,
                                         bias=nmx[:, s, h:h + 1], accum_out=sm[:, s, h:h + 1]).then_inc(S["ex_ready"], 1)

            softmax_in(0)
            for i in range(4):
                if i < 3:
                    softmax_in(i + 1)
                act.wait_ge(S["ptp_ready"], i + 1)
                nc.scalar.activation(pt[:, :, :, P * i:P * i + P].rearrange("p m h t -> p (m h) t"),
                                     ps[i % 2][:, :].rearrange("p (a t) -> p a t", a=8), ACT.Copy).then_inc(S["pt_in"], 1)
            for c in range(DT):
                act.wait_ge(S["o_ready"], c + 1)
                nc.scalar.activation(oth[:, c, 0:SEQ], ps[c % 2][:, 0:SEQ], ACT.Copy).then_inc(S["oh_ready"], 1)
            for p in range(-1, 4):
                if p >= 0:
                    act.wait_ge(S["ptp_ready"], p + 5)
                    nc.scalar.activation(pt[:, 0, 0, :], ps[3][:, 0:SEQ], ACT.Copy).then_inc(S["pt_in"], 1)
                if p < 3:
                    act.wait_ge(S["mx_ready"], 3 * (p + 1) + 11)
                    nc.scalar.activation(pex[0][:, 0:2 * NMEM], pex[1][:, 0:2 * NMEM], ACT.Exp, bias=nmx[:, 0, 0:1],
                                         accum_out=sm[:, 0, 0:1]).then_inc(S["ex_ready"], 1)
                if p >= 0:
                    act.wait_ge(S["o_ready"], 2 * p + 9)
                    nc.scalar.activation(ost[:], ps[0][:, 0:NMEM], ACT.Copy).then_inc(S["ost_in"], 1)
                    act.wait_ge(S["o_ready"], 2 * p + 10)
                    nc.scalar.activation(oth[:, :, SEQ + 32 * p:SEQ + 32 * p + 32].rearrange("p (h k) t -> p h k t", k=2),
                                         ps[1][:, 0:256].rearrange("p (k h t) -> p h k t", k=2, h=XH), ACT.Copy).then_inc(S["oh_ready"], 1)
            n0 = SLOTS["ox"][0]
            with act.Fori(0, 4) as i:
                for s in range(2):
                    hi_part(act, i, n0 + s + 1)
            act.wait_ge(S["h_added"], 2 * DT)
            norm_act(act, 3, lambda k: ht[:, k, :], fnh, n3_bufs)
            done = 0
            for c, n in enumerate(THIRDS):
                n0 = SLOTS[f"f{c}"][0]
                with act.Fori(0, n) as i:
                    hi_part(act, i, n0 + 1)
                    act.wait_ge(S["mm_done"], 2 * i + (n0 + 3))
                    nc.scalar.activation(fth[:], span(ps[0]), ACT.Tanh, scale=0.5).then_inc(S["ft_ready"], 1)
                    hi_part(act, i, n0 + 2)
                    act.wait_ge(S["fh_ready"], i + (done + 1))
                    nc.scalar.activation(tile_of(hdh, i), fhd[:], ACT.Copy).then_inc(S["fhh_ready"], 1)
                done += n
                n0 = SLOTS[f"d{c}"][0]
                last = c == len(THIRDS) - 1
                with act.Fori(0, 3 if last else 4) as i:
                    for s in range(2):
                        hi_part(act, i, n0 + s + 1)
                if last:
                    hi_part(act, 3, n0 + 1)
            act.wait_ge(S["h_added"], 5 * DT)
            stats_act(act, 4, lambda k: ht[:, k, :], n3_bufs)

        @block.vector
        def _(dve):
            dve.wait_ge(S["consts_in"], 64)
            a = VCOL["w0"]
            nc.vector.tensor_scalar(par[:, 0:16], vec[:, a:a + 16], 0.5, None, ALU.mult).then_inc(S["params"], 1)
            a = VCOL["k_a"]
            nc.vector.tensor_scalar(par[:, 16:24], vec[:, a:a + 8], 0.5, None, ALU.mult).then_inc(S["params"], 1)
            nc.vector.tensor_scalar(par[:, 24:32], vec[:, a:a + 8], -0.5, 1.0, ALU.mult, ALU.add).then_inc(S["params"], 1)
            a = VCOL["ln_conv_g"]
            nc.vector.tensor_scalar(par[:, 32:40], vec[:, a:a + 8], 0.5, None, ALU.mult).then_inc(S["params"], 1)
            norm_dve(dve, 0, lambda k: xin[:, k, :], "g_norm_mix", n_bufs)
            dve.sem_inc(S["u_ready"], 1)
            dve.wait_ge(S["xn_ready"], DT)
            nc.vector.memset(up[:, :, 0:BUF], 0.0).then_inc(S["up_zero"], 1)
            with dve.Fori(0, CT) as i:
                dve.wait_ge(S["glu_gate"], i + 1)
                dve.wait_ge(S["u_ready"], i + 1)
                nc.vector.tensor_scalar(tmp[1][:, 0:NT], tmp[0][:, 0:NT], 0.5, 0.5, ALU.mult, ALU.add).then_inc(psum_free[1], 1)
                dve.wait_ge(psum_free[1], i + 2)
                nc.vector.tensor_tensor(row(up[:, bass.ds(i, 1), BUF:BUF + SEQ]), tmp[1][:, 0:SEQ], ps[0][:, CUT:CUT + SEQ],
                                        ALU.mult).then_inc(S["u_ready"], 1)
                nc.vector.tensor_tensor(streams(row(up[:, bass.ds(i, 1), :]), BUF + SEQ, BUF + TS, BUF, TS),
                                        by_stream(tmp[1][:, SEQ:NT]), by_stream(ps[0][:, CUT + SEQ:CUT + NT]), ALU.mult)\
                    .then_inc(psum_free[0], 1)
            dve.sem_inc(S["pr_free"], 2)
            dve.wait_ge(S["history_in"], 16 * CT)
            dve.wait_ge(psum_free[0], 1 + CT)

            def windows(j, tap):
                u = up[:, j, :]
                own = u[:, BUF + SEQ:UW].rearrange("p (b c) -> p b c", b=NS)
                if isinstance(tap, int):
                    return u[:, tap:tap + SEQ], own[:, :, tap:tap + TS]
                return u[:, bass.ds(tap, SEQ)], own[:, :, bass.ds(tap, TS)]

            def parts(j):
                return acc[:, j, 0:SEQ], by_stream(acc[:, j, SEQ:NT])

            for j in range(CT):
                for src, dst in zip(windows(j, 0), parts(j)):
                    nc.vector.tensor_scalar(dst, src, v1("w_dw", TAPS * j), v1("b_dw", j), ALU.mult, ALU.add)\
                        .then_inc(S["conv_step"], 1)

            def conv_tap(tap):
                for j in range(CT):
                    for n, (src, dst) in enumerate(zip(windows(j, tap), parts(j))):
                        dve.wait_ge(S["conv_step"], 8 * tap + (2 * j + n - 7))
                        nc.vector.scalar_tensor_tensor(out=dst, in0=src, scalar=v1("w_dw", tap + TAPS * j), in1=dst,
                                                       op0=ALU.mult, op1=ALU.add).then_inc(S["conv_step"], 1)

            for t0, dest in ((0, lambda k: row(ar[:, bass.ds(k, 1), 1, :])), (8, lambda k: row(kt[:, bass.ds(k, 1), :])),
                             (16, lambda k: row(vt[:, bass.ds(k, 1), :])), (24, None)):
                with (dve.Fori(0, 4) if dest else nullcontext(0)) as i:
                    for s in range(2):
                        out = dest(2 * i + s) if dest else (lora, sgd)[s][:]
                        t = t0 + s
                        dve.wait_ge(S["pad_ready"], 2 * i + (t + 1))
                        dve.wait_ge(S["pr_ready"], 4 * i + (2 * t + 2))
                        nc.vector.tensor_tensor(tmp[s][:, 0:PW - 1], pr[s][:, 0:PW - 1], pr[s][:, 1:PW], ALU.subtract)\
                            .then_inc(S["diff_ready"], 1)
                        dve.wait_ge(S["diff_ready"], 2 * i + (t + 1))
                        mu = v1("mu_shift", 2 * i + t)
                        nc.vector.scalar_tensor_tensor(out=out[:, 0:SEQ], in0=tmp[s][:, 0:SEQ], scalar=mu, in1=pr[s][:, 1:1 + SEQ],
                                                       op0=ALU.mult, op1=ALU.add)
                        nc.vector.scalar_tensor_tensor(out=by_stream(out[:, SEQ:NT]), in0=streams(tmp[s], 1 + SEQ, 1 + TS, 0, TS),
                                                       scalar=mu, in1=streams(pr[s], 1 + SEQ, 1 + TS, 1, TS),
                                                       op0=ALU.mult, op1=ALU.add).then_inc(S["pr_free"], 1)
                        if dest:
                            conv_tap(2 * i + (t + 1))
            with dve.Fori(RT + 1, TAPS) as tap:
                conv_tap(tap)
            dve.wait_ge(S["conv_step"], 8 * TAPS)
            dve.sem_inc(S["conv_done"], 1)
            dve.wait_ge(S["lora_tanh"], 2)
            nc.vector.tensor_scalar(sgd[:], sgd[:], 0.5, 0.5, ALU.mult, ALU.add).then_inc(S["sig_ready"], 1)
            dve.wait_ge(S["cmean_ready"], 1)
            for j in range(CT):
                nc.vector.tensor_tensor(acc[:, j, :], acc[:, j, :], span(ps[3]), ALU.subtract).then_inc(S["centred"], 1)
            dve.wait_ge(S["dev_ready"], 1)
            nc.vector.reciprocal(pr[1][:, 0:NT], pr[0][:, 0:NT]).then_inc(S["inv_ready"], 1)
            dve.wait_ge(S["inv_ready"], 1)
            for j in range(CT):
                nc.vector.tensor_tensor(acc[:, j, :], acc[:, j, :], pr[1][:, 0:NT], ALU.mult).then_inc(S["cn_ready"], 1)
                dve.wait_ge(S["cn_ready"], 2 * j + 1)
                nc.vector.tensor_scalar(acc[:, j, :], acc[:, j, :], par[:, 32 + j:33 + j], par[:, 36 + j:37 + j], ALU.mult, ALU.add)\
                    .then_inc(S["cn_ready"], 1)
            for j in range(CT):
                dve.wait_ge(S["ct_ready"], j + 1)
                nc.vector.scalar_tensor_tensor(out=acc[:, j, :], in0=up[:, j, 0:NT], scalar=1.0, in1=acc[:, j, :],
                                               op0=ALU.add, op1=ALU.mult).then_inc(S["cs_ready"], 1)
            n0 = SLOTS["conv"][0]

            def gated_conv(i, first):
                for s in range(2):
                    dve.wait_ge(S["mm_done"], 2 * i + (n0 + s + 3))
                    if not first:
                        dve.wait_ge(m1_out[s], 16 * i)
                    nc.vector.scalar_tensor_tensor(out=pr[s][:, 0:NT], in0=tile_of(ar, 2 * i + s, 0), scalar=1.0,
                                                   in1=span(ps[s]), op0=ALU.add, op1=ALU.mult).then_inc(psum_free[s], 1)

            gated_conv(0, True)
            with dve.Fori(1, 4) as i:
                gated_conv(i, False)
            dve.wait_ge(S["dev_ready"], 2)
            nc.vector.tensor_scalar(rn[:], rn[:], 1e-12, None, ALU.max).then_inc(S["rn_ready"], 1)
            dve.wait_ge(S["rn_ready"], 1)
            nc.vector.reciprocal(rn[:], rn[:]).then_inc(S["rn_ready"], 1)
            for j in range(DT):
                s = j % 2

                def made(n):
                    dve.wait_ge(S["prep_dve"], 8 * j + n)

                def done(ins):
                    ins.then_inc(S["prep_dve"], 1)

                dve.wait_ge(S["tz_ready"], 3 * j + 3)
                if j >= 2:
                    dve.wait_ge(S["prep_pool"], 4 * (j - 2) + 4)
                done(nc.vector.tensor_tensor_scan(p_L[s][:], smask[:], p_l[s][:], 0.0, ALU.mult, ALU.add))
                made(1)
                done(nc.vector.tensor_tensor(p_m[s][:], p_L[s][:], p_l[s][:], ALU.subtract))
                dve.wait_ge(S["rnb_ready"], j + 1)
                done(nc.vector.scalar_tensor_tensor(out=p_kk[s][:], in0=kt[:, j, :], scalar=v1("k_k", j), in1=span(ps[2]),
                                                    op0=ALU.mult, op1=ALU.mult))
                dve.wait_ge(S["kf_ready"], j + 1)
                done(nc.vector.tensor_tensor(p_kf[s][:], p_kf[s][:], kt[:, j, :], ALU.mult))
                made(3)
                done(nc.vector.scalar_tensor_tensor(out=p_b2[s][:], in0=p_ta[s][:], scalar=1.0, in1=p_kk[s][:],
                                                    op0=ALU.add, op1=ALU.mult))
                made(4)
                if j >= 2:
                    dve.wait_ge(S["bonus_used"], j - 1)
                done(nc.vector.scalar_tensor_tensor(out=p_rk[s][:], in0=ar[:, j, 1, :], scalar=v1("r_k", j), in1=p_kf[s][:],
                                                    op0=ALU.mult, op1=ALU.mult))
                dve.wait_ge(S["e_ready"], 3 * j + 3)
                made(5)
                done(nc.vector.scalar_tensor_tensor(out=bt[:, j, :], in0=p_b2[s][:], scalar=0.5, in1=p_L[s][:],
                                                    op0=ALU.mult, op1=ALU.mult))
                done(nc.vector.scalar_tensor_tensor(out=ar[:, j, 0, :], in0=p_kk[s][:], scalar=-1.0, in1=p_m[s][:],
                                                    op0=ALU.mult, op1=ALU.mult))
            dve.wait_ge(S["prep_pool"], 4 * DT)
            dve.wait_ge(S["prep_dve"], 8 * DT)
            dve.wait_ge(S["bonus_ready"], 1)
            for b in (atd, akd, ad, sd):
                last = nc.vector.memset(b[:], 0.0)
            last.then_inc(S["zeroed"], 1)
            dve.wait_ge(S["zeroed"], 2)
            dve.sem_inc(S["s_new"], 2)
            with dve.Fori(0, NCH) as i:
                rec_dve(dve, True, i)
            with dve.Fori(0, 2) as i:
                rec_dve(dve, False, i)
            for j in range(DT):
                dve.wait_ge(S["mb_ready"], j + 1)
                nc.vector.tensor_tensor(ar[:, j, 1, :], ar[:, j, 1, :], span(ps[j % 2]), ALU.subtract).then_inc(S["centred"], 1)
            dve.wait_ge(S["dev_ready"], 3)
            nc.vector.reciprocal(rstd16[:], dev16[:]).then_inc(S["inv_ready"], 1)
            dve.wait_ge(S["centred"], DT + 4)
            for j in range(DT):
                y = ar[:, j, 1, :]

                def made(n):
                    dve.wait_ge(S["post_dve"], 5 * j + n)

                dve.wait_ge(S["g3_ready"], j + 1)
                nc.vector.tensor_tensor(y, y, span(ps[0]), ALU.mult).then_inc(S["post_dve"], 1)
                if j:
                    made(0)
                nc.vector.tensor_tensor(bv[:], vt[:, j, :], span(ps[1]), ALU.mult).then_inc(S["post_dve"], 1)
                made(1)
                nc.vector.tensor_scalar(y, y, v1("ln_x_g", j), v1("ln_x_b", j), ALU.mult, ALU.add).then_inc(S["post_dve"], 1)
                made(3)
                nc.vector.tensor_tensor(y, y, bv[:], ALU.add).then_inc(S["post_dve"], 1)
                made(4)
                if j >= 2:
                    dve.wait_ge(S["yl_ready"], j - 1)
                nc.vector.tensor_tensor(po[j % 2][:], y, span(ps[2]), ALU.mult).then_inc(S["po_ready"], 1)
                dve.sem_inc(S["post_dve"], 1)
            dve.wait_ge(S["po_ready"], DT)
            dve.wait_ge(S["mt_in"], 32)
            dve.wait_ge(S["yl_ready"], DT)
            dve.sem_inc(S["mgl_ready"], 2)
            n0 = SLOTS["orwkv"][0]
            with dve.Fori(0, 4) as i:
                for s in range(2):
                    dve.wait_ge(S["mm_done"], 2 * i + (n0 + s + 3))
                    dve.wait_ge(S["mgl_ready"], 2 * i + (s + 1))
                    nc.vector.scalar_tensor_tensor(out=po[s][:], in0=tile_of(t2t, 2 * i + s), scalar=1.0, in1=span(ps[s]),
                                                   op0=ALU.add, op1=ALU.mult).then_inc(psum_free[s], 1)
                    dve.wait_ge(psum_free[s], i + (n0 // 2 + 2))
                    nc.vector.tensor_tensor(po[s][:], po[s][:], tile_of(m1t, 2 * i + s), ALU.add).then_inc(S["merge_dve"], 1)
                    dve.wait_ge(S["merge_dve"], 2 * i + (s + 1))
                    nc.vector.tensor_scalar(po[s][:], po[s][:], 0.5, None, ALU.mult).then_inc(S["mg_ready"], 1)
            stats_dve(dve, 1, n2_bufs, NMEM)

            def add_residual(stage, bufs=None):
                n0 = SLOTS[stage][0]
                part = (2 * DT + 1) * squared[0] + 1
                if bufs:
                    nc.vector.memset(bufs[0][1][:], 0.0).then_inc(S["sq_part"], 1)
                    squared[0] += 1
                with dve.Fori(0, 4) as i:
                    for s in range(2):
                        if stage == "out":
                            normed_tile(dve, 1, 2 * i + s, s, lambda k: tile_of(memt, k), "g_mem", n2_bufs, NMEM)
                        dve.wait_ge(S["mm_done"], 2 * i + (n0 + s + 3))
                        nc.vector.tensor_tensor(tile_of(ht, 2 * i + s), tile_of(ht, 2 * i + s), span(ps[s]), ALU.add)\
                            .then_inc(S["h_added"], 1)
                        dve.wait_ge(S["h_added"], 2 * i + (s + 1 + added[0]))
                        dve.sem_inc(psum_free[s], 1)
                        if bufs:
                            hk, (sq_, total) = tile_of(ht, 2 * i + s), bufs[0]
                            dve.wait_ge(S["sq_part"], 4 * i + (2 * s + part))
                            nc.vector.tensor_tensor(sq_[:], hk, hk, ALU.mult).then_inc(S["sq_part"], 1)
                            dve.wait_ge(S["sq_part"], 4 * i + (2 * s + 1 + part))
                            nc.vector.tensor_tensor(total[:], total[:], sq_[:], ALU.add).then_inc(S["sq_part"], 1)
                added[0] += DT

            added, squared = [0], [0]
            dve.wait_ge(S["res_in"], 16)
            add_residual("out", n2_bufs)
            norm_dve(dve, 2, lambda k: ht[:, k, :], "g_norm_x", n2_bufs)
            for i in range(4):
                s = i % 2
                dve.wait_ge(S["sp_ready"], i + 1)
                nc.vector.tensor_reduce(out=mx[:, s, :], in_=ps[2 + s][:, :].rearrange("p (h m) -> p h m", h=XH), op=ALU.max, axis=AX.X)\
                    .then_inc(S["mx_ready"], 1)
                dve.wait_ge(S["mx_ready"], 2 * i + 1)
                nc.vector.tensor_scalar(nmx[:, s, :], mx[:, s, :], -1.0, None, ALU.mult).then_inc(S["mx_ready"], 1)
                dve.wait_ge(S["ex_ready"], XH * i + XH)
                nc.vector.reciprocal(rs[:, s, :], sm[:, s, :]).then_inc(S["pn_ready"], 1)
                dve.wait_ge(S["pn_ready"], 2 * i + 1)
                v = pex[s][:, :].rearrange("p (h m) -> p h m", h=XH)
                nc.vector.tensor_tensor(v, v, rs[:, s, :].rearrange("p (h m) -> p h m", m=1).to_broadcast([P, XH, NMEM]), ALU.mult)\
                    .then_inc(S["pn_ready"], 1)
            for c in range(DT):
                dve.wait_ge(S["oh_ready"], c + 1)
                nc.vector.tensor_tensor(otl[:, c, 0:SEQ], ps[c % 2][:, 0:SEQ], oth[:, c, 0:SEQ].bitcast(F32), ALU.subtract)\
                    .then_inc(S["ol_ready"], 1)
            dve.wait_ge(S["xm_in"], 16)

            def stream_softmax(p):
                dve.wait_ge(S["sp_ready"], p + 5)
                if p:
                    dve.wait_ge(S["ex_ready"], p + 16)
                nc.vector.tensor_tensor(pex[1][:, 0:2 * NMEM], ps[2][:, 0:2 * NMEM], xmask[:], ALU.add).then_inc(S["mx_ready"], 1)
                dve.wait_ge(S["mx_ready"], 3 * p + 9)
                nc.vector.tensor_reduce(out=mx[:, 0, 0:1], in_=pex[1][:, 0:2 * NMEM], op=ALU.max, axis=AX.X).then_inc(S["mx_ready"], 1)
                dve.wait_ge(S["mx_ready"], 3 * p + 10)
                nc.vector.tensor_scalar(nmx[:, 0, 0:1], mx[:, 0, 0:1], -1.0, None, ALU.mult).then_inc(S["mx_ready"], 1)
                dve.wait_ge(S["ex_ready"], p + 17)
                nc.vector.reciprocal(rs[:, 0, 0:1], sm[:, 0, 0:1]).then_inc(S["pn_ready"], 1)
                dve.wait_ge(S["pn_ready"], 2 * p + 9)
                nc.vector.tensor_scalar(pex[0][:, 0:2 * NMEM], pex[0][:, 0:2 * NMEM], rs[:, 0, 0:1], None, ALU.mult)\
                    .then_inc(S["pn_ready"], 1)

            stream_softmax(0)
            for p in range(4):
                if p < 3:
                    stream_softmax(p + 1)
                dve.wait_ge(S["oh_ready"], p + 9)
                w32 = slice(SEQ + 32 * p, SEQ + 32 * p + 32)
                nc.vector.tensor_tensor(otl[:, :, w32].rearrange("p (h k) t -> p h k t", k=2),
                                        ps[1][:, 0:256].rearrange("p (k h t) -> p h k t", k=2, h=XH),
                                        oth[:, :, w32].rearrange("p (h k) t -> p h k t", k=2).bitcast(F32), ALU.subtract)\
                    .then_inc(S["ol_ready"], 1)
            add_residual("ox", n3_bufs)
            norm_dve(dve, 3, lambda k: ht[:, k, :], "g_norm_ffn", n3_bufs)
            done = 0
            for c, n in enumerate(THIRDS):
                n0 = SLOTS[f"f{c}"][0]
                with dve.Fori(0, n) as i:
                    dve.wait_ge(S["ft_ready"], i + (done + 1))
                    nc.vector.scalar_tensor_tensor(out=fsg[:], in0=fth[:], scalar=1.0, in1=span(ps[0]), op0=ALU.add, op1=ALU.mult)\
                        .then_inc(psum_free[0], 1)
                    dve.wait_ge(psum_free[0], i + (n0 // 2 + 2))
                    dve.wait_ge(S["mm_done"], 2 * i + (n0 + 4))
                    dve.wait_ge(S["fhl_ready"], i + (done + 1))
                    nc.vector.scalar_tensor_tensor(out=fhd[:], in0=fsg[:], scalar=0.5, in1=span(ps[1]), op0=ALU.mult, op1=ALU.mult)\
                        .then_inc(S["fh_ready"], 1)
                    dve.wait_ge(S["fh_ready"], i + (done + 1))
                    dve.sem_inc(psum_free[1], 1)
                done += n
                add_residual(f"d{c}", n3_bufs if c == len(THIRDS) - 1 else None)
            stats_dve(dve, 4, n3_bufs)
            for k in range(DT):
                nc.vector.scalar_tensor_tensor(out=ht[:, k, :], in0=ht[:, k, :], scalar=v1("g_norm_final", k), in1=n3_bufs[2][:],
                                               op0=ALU.mult, op1=ALU.mult).then_inc(S["y_done"], 1)

        @block.gpsimd
        def _(pool):
            for s in range(2):
                nc.gpsimd.memset(pr[s][:, 0:1], 0.0).then_inc(S["pr_zero"], 1)
            pool.sem_inc(S["ns_out"], 16)
            lo_part(pool, 0, 0)
            norm_pool(pool, 0, xnh, xnl, n_bufs)
            with pool.Fori(0, CT) as i:
                lo_part(pool, i, 1)
                lo_part(pool, i, 2)
            n0 = SLOTS["rkv"][0]
            with pool.Fori(0, SHT // 2) as i:
                for s in range(2):
                    await_(pool, S["pr_free"], 2 * i + (s + 1))
                    nc.gpsimd.tensor_copy(streams(pr[s], 1 + SEQ, 1 + TS, 0, 1),
                                          shin[:, bass.ds(2 * i + s, 1), :].rearrange("p a (b c) -> p (a b) c", c=1))\
                        .then_inc(S["pad_ready"], 1)
                    lo_part(pool, i, n0 + s + 1)
                    await_(pool, S["pr_ready"], 4 * i + (2 * s + 2))
                    nc.gpsimd.tensor_copy(row(shout[:, bass.ds(2 * i + s, 1), 0:1]), pr[s][:, SEQ:SEQ + 1]).then_inc(S["shift_half"], 1)
                    nc.gpsimd.tensor_copy(shout[:, bass.ds(2 * i + s, 1), 1:1 + NS].rearrange("p a (b c) -> p (a b) c", c=1),
                                          streams(pr[s], 1 + SEQ, 1 + TS, TS, 1)).then_inc(psum_free[s], 1)
            n0 = SLOTS["gate"][0]
            with pool.Fori(0, 4) as i:
                for s in range(2):
                    lo_part(pool, i, n0 + s + 1)
            with pool.Fori(0, 4) as i:
                for s in range(2):
                    lo_part(pool, i, n0 + 8 + s + 1)
                    await_(pool, psum_free[s], i + (n0 // 2 + 4 + 2))
                    pool.dma_start(io["g2"][bass.ds(2 * i + s, 1), :, :].rearrange("a p n -> (a p) n"), tmp[s][:, 0:NT])\
                        .then_inc(g2_out[s], 16)
            for j in range(CT):
                await_(pool, S["ch_ready"], j + 1)
                nc.gpsimd.tensor_tensor(cl[:, j, :], acc[:, j, :], ch[:, j, :].bitcast(F32), ALU.subtract).then_inc(S["cl_ready"], 1)
            n0 = SLOTS["conv"][0]
            with pool.Fori(0, 4) as i:
                for s in range(2):
                    lo_part(pool, i, n0 + s + 1)
                    await_(pool, psum_free[s], i + (n0 // 2 + 2))
                    pool.dma_start(io["m1"][bass.ds(2 * i + s, 1), :, :].rearrange("a p n -> (a p) n"), pr[s][:, 0:NT])\
                        .then_inc(m1_out[s], 16)
            for j in range(DT):
                s = j % 2
                await_(pool, S["prep_dve"], 8 * j + 6)
                await_(pool, S["e_ready"], 3 * j + 3)
                nc.gpsimd.tensor_tensor(kt[:, j, :], p_kf[s][:], p_L[s][:], ALU.mult).then_inc(S["prep_pool"], 1)
                nc.gpsimd.tensor_tensor(ar[:, j, 1, :], ar[:, j, 1, :], p_e1[s][:], ALU.mult).then_inc(S["prep_pool"], 1)
                nc.gpsimd.tensor_copy(wcum[:, j, 0:NCH], p_e1[s][:, C - 1:SEQ:C]).then_inc(S["prep_pool"], 1)
                await_(pool, S["prep_dve"], 8 * j + 7)
                nc.gpsimd.tensor_copy(wcum[:, j, NCH:NCH + NS], p_e1[s][:, SEQ + TS - 1:NT:TS]).then_inc(S["prep_pool"], 1)
            await_(pool, S["prep_dve"], 8 * DT)
            await_(pool, S["bonus_ready"], 1)
            await_(pool, S["prep_pool"], 4 * DT)
            for b in (bd, kd, vd):
                last = nc.gpsimd.memset(b[:], 0.0)
            last.then_inc(S["zeroed"], 1)
            await_(pool, S["zeroed"], 2)
            with pool.Fori(0, NCH) as i:
                rec_pool(pool, True, i)
            with pool.Fori(0, 2) as i:
                rec_pool(pool, False, i)
            for j in range(DT):
                await_(pool, S["yh_ready"], j + 1)
                nc.gpsimd.tensor_tensor(yol[:, j, :], po[j % 2][:], yoh[:, j, :].bitcast(F32), ALU.subtract).then_inc(S["yl_ready"], 1)
            n0 = SLOTS["orwkv"][0]
            with pool.Fori(0, 4) as i:
                for s in range(2):
                    lo_part(pool, i, n0 + s + 1)
                    await_(pool, S["mgh_ready"], 2 * i + (s + 1))
                    nc.gpsimd.tensor_tensor(tile_of(mgl, 2 * i + s), po[s][:], tile_of(mgh, 2 * i + s).bitcast(F32), ALU.subtract)\
                        .then_inc(S["mgl_ready"], 1)
            for stage in ("out", "mk", "mv", "q"):
                n0 = SLOTS[stage][0]
                with pool.Fori(0, 4) as i:
                    for s in range(2):
                        lo_part(pool, i, n0 + s + 1)
                        if stage == "out":
                            low_tile(pool, 1, 2 * i + s, s, memh, meml, n2_bufs, NMEM)
                        if stage == "mk":
                            low_tile(pool, 2, 2 * i + s, s, hnh, hnl, n2_bufs)
            n0 = SLOTS["ox"][0]
            with pool.Fori(0, 4) as i:
                for s in range(2):
                    lo_part(pool, i, n0 + s + 1)
            norm_pool(pool, 3, fnh, fnl, n3_bufs)
            pool.sem_inc(S["fhl_ready"], 1)
            done = 0
            for c, n in enumerate(THIRDS):
                n0 = SLOTS[f"f{c}"][0]
                with pool.Fori(0, n) as i:
                    lo_part(pool, i, n0 + 1)
                    lo_part(pool, i, n0 + 2)
                    await_(pool, S["fhh_ready"], i + (done + 1))
                    nc.gpsimd.tensor_tensor(tile_of(hdl, i), fhd[:], tile_of(hdh, i).bitcast(F32), ALU.subtract).then_inc(S["fhl_ready"], 1)
                done += n
                n0 = SLOTS[f"d{c}"][0]
                last = c == len(THIRDS) - 1
                with pool.Fori(0, 3 if last else 4) as i:
                    for s in range(2):
                        lo_part(pool, i, n0 + s + 1)
                if last:
                    lo_part(pool, 3, n0 + 1)

        @block.tensor
        def _(pe):
            pe.sem_inc(psum_free[0], 1)
            pe.sem_inc(psum_free[1], 1)
            pe.sem_inc(S["mm_done"], 2)
            pe.wait_ge(S["consts_in"], 64)
            norm_pe(pe, 0, n_bufs)
            dense(pe, "glu", xnh, xnl, split=("xl_ready", 0))
            dense(pe, "rkv", xnh, xnl)
            dense(pe, "lora", xnh, xnl)
            dense(pe, "gate", xnh, xnl, part=(0, 8))
            pe.wait_ge(S["conv_done"], 1)
            for j in range(CT):
                for h in range(2):
                    last = nc.tensor.matmul(cut(ps[3], h), const("mean_c"), acc[:, j, h * HALF:(h + 1) * HALF],
                                            start=(j == 0), stop=(j == CT - 1))
            last.then_inc(S["cmean_ready"], 1)
            dense(pe, "gate", xnh, xnl, part=(8, 4))
            for j in range(CT):
                pe.wait_ge(S["square_ready"], j + 1)
                for h in range(2):
                    last = nc.tensor.matmul(cut(ps[2], h), const("mean_c"), up[:, j, h * HALF:(h + 1) * HALF],
                                            start=(j == 0), stop=(j == CT - 1))
                last.then_inc(S["square_summed"] if j < CT - 1 else S["var_ready"], 1)
            dense(pe, "gate", xnh, xnl, part=(12, 4))
            def head_sum(j, src, done):
                for h in range(2):
                    last = nc.tensor.matmul(cut(ps[3], h)[0:16, :], const("head_sum")[:, 16 * j:16 * j + 16],
                                            src[:, h * HALF:(h + 1) * HALF], start=(j == 0), stop=(j == DT - 1))
                last.then_inc(done, 1)

            for i in range(4):
                dense(pe, "conv", ch, cl, k_tiles=CT, part=(2 * i, 2), split=("cl_ready", 0) if i == 0 else None)
                for j in (2 * i, 2 * i + 1):
                    pe.wait_ge(S["square_ready"], j + 5)
                    head_sum(j, tmp[j % 2], S["square_summed"] if j < DT - 1 else S["var_ready"])
            pe.wait_ge(S["rn_ready"], 2)
            pe.wait_ge(S["lora_tanh"], 2)
            pe.wait_ge(psum_free[0], SLOTS["orwkv"][0] // 2 + 1)
            pe.wait_ge(psum_free[1], SLOTS["orwkv"][0] // 2 + 1)
            pe.wait_ge(S["lw_in"], 48)
            for j in range(DT):
                if j:
                    pe.wait_ge(S["tz_ready"], 3 * j - 1)
                cols = slice(P * j, P * j + P)
                for h in range(2):
                    nc.tensor.matmul(cut(ps[0], h), lw[0:64, cols], lora[0:64, h * HALF:(h + 1) * HALF], start=True, stop=True)
                for h in range(2):
                    last = nc.tensor.matmul(cut(ps[1], h), lw[64:128, cols], lora[64:128, h * HALF:(h + 1) * HALF], start=True, stop=True)
                last.then_inc(S["z_ready"], 1)
                if j:
                    pe.wait_ge(S["prep_dve"], 8 * (j - 1) + 3)
                for h in range(2):
                    last = nc.tensor.matmul(cut(ps[2], h), erow[:, cols], rn[:, h * HALF:(h + 1) * HALF], start=True, stop=True)
                last.then_inc(S["rnb_ready"], 1)
                if j:
                    pe.wait_ge(S["prep_dve"], 8 * (j - 1) + 6)
                    head_sum(j - 1, p_rk[(j - 1) % 2], S["bonus_used"])
            pe.wait_ge(S["prep_dve"], 8 * (DT - 1) + 6)
            head_sum(DT - 1, p_rk[(DT - 1) % 2], S["bonus_ready"])
            pe.wait_ge(S["bonus_in"], 1)
            pe.wait_ge(S["zeroed"], 2)
            pe.sem_inc(S["rhs_ready"], 2)
            pe.sem_inc(S["vd_ready"], 2)
            with pe.Fori(0, NCH) as i:
                rec_pe(pe, True, i)
            with pe.Fori(0, 2) as i:
                rec_pe(pe, False, i)
            pe.wait_ge(S["gup_in"], 48)
            pe.wait_ge(S["y_in"], 2 + 2 * NCH + 4)
            for j in range(DT):
                if j >= 2:
                    pe.wait_ge(S["centred"], j - 1 + 4)
                for h in range(2):
                    last = nc.tensor.matmul(cut(ps[j % 2], h), hmean[:], ar[:, j, 1, h * HALF:(h + 1) * HALF], start=True, stop=True)
                last.then_inc(S["mb_ready"], 1)
            for j in range(DT):
                pe.wait_ge(S["square_ready"], j + 13)
                head_sum(j, psq[j % 2], S["square_summed"] if j < DT - 1 else S["var_ready"])
            pe.wait_ge(S["inv_ready"], 2)
            for j in range(DT):
                cols = slice(P * j, P * j + P)
                for b, (w, src) in enumerate(((erow2[:, cols], rstd16), (erow2[:, cols], bon), (gup[:, cols], sgd))):
                    if j:
                        pe.wait_ge(*((S["po_ready"], j) if b == 2 else (S["post_dve"], 5 * (j - 1) + 1 + b)))
                    for h in range(2):
                        last = nc.tensor.matmul(cut(ps[b], h), w, src[:, h * HALF:(h + 1) * HALF], start=True, stop=True)
                last.then_inc(S["g3_ready"], 1)
            pe.wait_ge(S["po_ready"], DT)
            dense(pe, "orwkv", yoh, yol, split=("yl_ready", 0))
            norm_pe(pe, 1, n2_bufs, NMEM)
            dense(pe, "out", mgh, mgl, split=("mgl_ready", 2))
            norm_pe(pe, 2, n2_bufs)
            pe.wait_ge(S["xl_ready"], 2 * DT)
            dense(pe, "mk", memh, meml, n=NMEM)
            dense(pe, "mv", memh, meml, n=NMEM)
            dense(pe, "q", hnh, hnl, split=("xl_ready", 2 * DT))
            for s in range(2):
                pe.wait_ge(psum_free[s], SLOTS["ox"][0] // 2 + 1)
            for m in range(2):
                for j in range(DT):
                    last = nc.tensor.transpose(ps[m][:, P * j:P * j + P], mvt[:, j, P * m:P * m + P], const("ident"))
                last.then_inc(S["mvx_ready"], 1)

            def scores(i):
                if i >= 2:
                    pe.wait_ge(S["ex_ready"], XH * (i - 1))
                for h in range(XH):
                    for k in range(2):
                        last = nc.tensor.matmul(ps[2 + i % 2][:, NMEM * h:NMEM * h + NMEM], qt[:, 2 * h + k, P * i:P * i + P],
                                                mkt[:, 2 * h + k, :], start=(k == 0), stop=(k == 1))
                last.then_inc(S["sp_ready"], 1)

            scores(0)
            scores(1)
            for i in range(4):
                pe.wait_ge(S["pn_ready"], 2 * i + 2)
                if i < 2:
                    pe.wait_ge(S["mv_in"], i + 1)
                else:
                    pe.wait_ge(S["pt_in"], i - 1)
                for m in range(2):
                    for h in range(XH):
                        a = XH * m + h
                        last = nc.tensor.transpose(ps[i % 2][:, P * a:P * a + P], pex[i % 2][:, NMEM * h + P * m:NMEM * h + P * m + P], const("ident"))
                last.then_inc(S["ptp_ready"], 1)
                if i + 2 < 4:
                    scores(i + 2)
            pe.wait_ge(S["pt_in"], 4)
            for c in range(DT):
                if c >= 2:
                    pe.wait_ge(S["ol_ready"], c - 1)
                for m in range(2):
                    last = nc.tensor.matmul(ps[c % 2][:, 0:SEQ], mv[:, m, P * c:P * c + P], pt[:, m, c // 2, :], start=(m == 0), stop=(m == 1))
                last.then_inc(S["o_ready"], 1)
            pe.wait_ge(S["ol_ready"], DT)

            def stream_scores(p):
                pe.wait_ge(kc_in[p % 2], 16 * (p // 2) + 16)
                for h in range(XH):
                    for k in range(2):
                        last = nc.tensor.matmul(ps[2][32 * h:32 * h + 32, 0:2 * NMEM], qt[:, 2 * h + k, SEQ + 32 * p:SEQ + 32 * p + 32],
                                                kcs[p % 2][:, 2 * h + k, :], start=(k == 0), stop=(k == 1), tile_position=(0, 32 * h))
                last.then_inc(S["sp_ready"], 1)
                pe.wait_ge(S["sp_ready"], p + 5)
                pe.sem_inc(S["kc_used"], 1)

            stream_scores(0)
            for p in range(4):
                pe.wait_ge(S["pn_ready"], 2 * p + 10)
                for m in range(4):
                    last = nc.tensor.transpose(ps[3][:, P * m:P * m + P], pex[0][:, P * m:P * m + P], const("ident"))
                last.then_inc(S["ptp_ready"], 1)
                if p < 3:
                    stream_scores(p + 1)
                pe.wait_ge(S["pt_in"], p + 5)
                pe.wait_ge(vc_in[p % 2], 32 * (p // 2) + 32)
                for h in range(XH):
                    for m in range(4):
                        last = nc.tensor.matmul(ps[0][32 * h:32 * h + 32, 0:NMEM], pt[:, 0, 0, P * m + 32 * h:P * m + 32 * h + 32],
                                                vcs[p % 2][m // 2][:, m % 2, NMEM * h:NMEM * h + NMEM], start=(m == 0), stop=(m == 3),
                                                tile_position=(0, 32 * h))
                last.then_inc(S["o_ready"], 1)
                pe.wait_ge(S["o_ready"], 2 * p + 9)
                pe.sem_inc(S["vc_used"], 1)
                pe.wait_ge(S["ost_in"], p + 1)
                if p:
                    pe.wait_ge(S["ol_ready"], p + 8)
                for k in range(2):
                    last = nc.tensor.transpose(ps[1][:, P * k:P * k + P], ost[:, P * k:P * k + P], const("ident"))
                last.then_inc(S["o_ready"], 1)
            pe.wait_ge(S["ol_ready"], 12)
            dense(pe, "ox", oth, otl)
            norm_pe(pe, 3, n3_bufs)
            done = 0
            for c, n in enumerate(THIRDS):
                dense(pe, f"f{c}", fnh, fnl, split=("xl_ready", 3 * DT) if c == 0 else None)
                dense(pe, f"d{c}", hdh, hdl, k_tiles=n, split=("fhl_ready", 1 + done))
                done += n
            norm_pe(pe, 4, n3_bufs)


def kernel(**inputs):
    import numpy as _np
    import concourse.bacc as _bacc
    from concourse import mybir as _mybir
    from concourse.bass_utils import run_bass_kernel_spmd as _run

    A = {k: _np.asarray(v) for k, v in inputs.items()}

    def tiles(a):
        return _np.ascontiguousarray(a.reshape(a.shape[0], -1, P).transpose(2, 1, 0))

    x = _np.concatenate([A["x_prompt"].reshape(SEQ, D), A["x_sample"].reshape(NS * TS, D)])

    def slots(w, order=None):
        k, n = w.shape
        s = _np.zeros((n // P, P, 8, P), w.dtype)
        s[:, :, :k // P, :] = w.reshape(k // P, P, n // P, P).transpose(2, 1, 0, 3)
        return s if order is None else s[order]

    w_in = A["w_in"][0]
    pairs = lambda n: [q for j in range(n) for q in (j, n + j)]
    parts = [slots(w_in[:, :2 * DC], pairs(CT)), slots(w_in[:, 2 * DC:2 * DC + SHT * P]), slots(w_in[:, 2 * DC + SHT * P:]),
             slots(A["w_o_conv"][0]), slots(A["w_o_rwkv"][0]), slots(A["w_out"][0]), slots(A["w_k_mem"][0]),
             slots(A["w_v_mem"][0]), slots(A["w_q_x"][0]), slots(A["w_o_x"][0])]
    a = 0
    for n in THIRDS:
        c = slice(a * P, (a + n) * P)
        parts.append(slots(_np.concatenate([A["w_ffn_gate"][0][:, c], A["w_ffn_up"][0][:, c]], 1), pairs(n)))
        parts.append(slots(A["w_ffn_down"][0][c, :]))
        a += n
    w_slots = _np.concatenate(parts).reshape(NSLOT, P, D)

    vecs = [tiles(A[n].reshape(1, -1))[:, :, 0] for n, _ in VECS[:-1]]
    vecs.append(tiles(A["w_dw"][0]).reshape(P, CT * TAPS))
    consts, wmask, smask, erow, xmask = tables(_np)
    ssd = _np.zeros((2, P, 8, 4, P), x.dtype)
    s0 = A["state_wkv"][0].reshape(2, 4, 8, 2, 64, 64).transpose(0, 3, 5, 2, 1, 4)
    ssd[:, 0:64, :, :, 0:64] = s0[:, 0]
    ssd[:, 64:128, :, :, 64:128] = s0[:, 1]
    kc = A["cache_mem_k"][0].reshape(4, 2 * NMEM, DT, P).transpose(0, 3, 2, 1)
    vc = A["cache_mem_v"][0].reshape(4, 4, P, D).transpose(0, 2, 1, 3)
    arrays = {
        "x": tiles(x), "mem": tiles(A["mem_prompt"][0]), "slots": w_slots, "vecs": _np.concatenate(vecs, 1), "consts": consts,
        "wmask": wmask, "smask": smask, "erow": erow, "xmask": xmask, "hmean": _np.kron(_np.eye(2), _np.full((64, 64), 1 / 64)).astype(x.dtype),
        "shift_in": tiles(A["state_shift"][0, :, 0]),
        "conv_in": A["state_conv"][0].reshape(NS, BUF, CT, P).transpose(3, 2, 0, 1),
        "lw": _np.concatenate([A["w_up"][0], A["a_up"][0]]), "gup": A["g_up"][0], "ssd": ssd, "kc": kc, "vc": vc,
    }
    arrays = {k: _np.ascontiguousarray(v) for k, v in arrays.items()}
    outs = {"y": (P, DT, NT), "mk": (P, DT, NMEM), "mv": (P, DT, NMEM), "conv_p": (P, CT, BUF), "conv_s": (P, CT, NS, BUF),
            "shift_out": (P, SHT, 1 + NS), "wkv_p": (P, 8, 64), "wkv_s": (2, P, 8, 4, 64)}
    nc = _bacc.Bacc("TRN2", target_bir_lowering=False, num_devices=1)
    f32 = _mybir.dt.float32
    io = {k: nc.dram_tensor("in_" + k, v.shape, f32, kind="ExternalInput").ap() for k, v in arrays.items()}
    io |= {k: nc.dram_tensor("out_" + k, v, f32, kind="ExternalOutput").ap() for k, v in outs.items()}
    io |= {k: nc.dram_tensor("tmp_" + k, (DT, P, NT), f32, kind="Internal").ap() for k in ("g2", "m1")}
    program(nc, io)
    r = _run(nc, [{"in_" + k: v for k, v in arrays.items()}], core_ids=[0]).results[0]
    o = {k: r["out_" + k] for k in outs}

    def rows(t):
        return t.transpose(2, 1, 0).reshape(t.shape[2], -1)

    y, sh = rows(o["y"]), rows(o["shift_out"])
    wp = o["wkv_p"].reshape(2, 64, 8, 64).transpose(2, 0, 3, 1).reshape(1, 1, HEADS, 64, 64)
    ws = o["wkv_s"].reshape(2, 2, 64, 8, 4, 64).transpose(0, 4, 3, 1, 5, 2).reshape(1, NS, HEADS, 64, 64)
    return (y[:SEQ].reshape(1, SEQ, D), y[SEQ:].reshape(NS, TS, D),
            rows(o["mk"]).reshape(1, 1, NMEM, XH, D // XH), rows(o["mv"]).reshape(1, 1, NMEM, XH, D // XH),
            rows(o["conv_p"]).reshape(1, 1, BUF, DC), sh[0].reshape(1, 1, 1, -1), wp,
            o["conv_s"].transpose(2, 3, 1, 0).reshape(1, NS, BUF, DC), sh[1:].reshape(1, NS, 1, -1), ws)


def tables(np_):
    f = np_.float32
    eye = np_.eye(P, dtype=f)
    t = np_.arange(64)
    consts = np_.zeros((P, NCONST), f)

    def put(name, a):
        consts[:, CCOL[name]:CCOL[name] + a.shape[1]] = a

    put("ident", eye)
    put("mean_d", np_.full((P, P), 1 / D, f))
    put("mean_c", np_.full((P, P), 1 / DC, f))
    head = (np_.arange(HEADS)[None, None, :] == 2 * np_.arange(8)[None, :, None] + (np_.arange(P) // 64)[:, None, None]).astype(f)
    put("head_sum", head.reshape(P, P))
    put("stream", np_.tile((t[:, None] // TS == np_.arange(4)).astype(f), (2, 1)))
    put("eps", np_.tile(np_.array([[EPS_RMS, EPS_LN, EPS_GN, 1.0]], f), (P, 1)))
    i, j = t[:, None], t[None, :]
    same = i // TS == j // TS
    cols = [(i < j), (i <= j), (i < j) & same, (i <= j) & same]
    cols += [((i // 2 ** L) % 2 == 1) & (j // 2 ** L == i // 2 ** L - 1) for L in range(LEVELS)]
    cols.append(cols[4].T)
    cols = [np_.tile(c, (2, 1)) for c in cols[:4]] + [np_.kron(np_.eye(2), c) for c in cols[4:]]
    wmask = np_.concatenate(cols, 1).astype(f)
    start = np_.arange(NT)
    start = np_.where(start < SEQ, start % C, (start - SEQ) % TS) == 0
    smask = np_.tile((~start).astype(f)[None], (P, 1))
    erow = head.transpose(2, 1, 0).reshape(HEADS, D)
    q, m = np_.arange(P)[:, None], np_.arange(2 * NMEM)[None, :]
    xmask = np_.where((q % 32) // TS == m // NMEM, 0.0, -1e30).astype(f)
    return consts, wmask, smask, np_.ascontiguousarray(erow), xmask
```
